# Optimizing a Trainium2 kernel written in Bass

```python
import jax, jax.numpy as jnp
from jax import lax
import numpy as np

D_MODEL = 1024
BATCH = 1
SEQ = 256
DEPTH = 1

RET_HEADS = 4
RET_V_DIM = D_MODEL // 2 // RET_HEADS
RET_QK_DIM = RET_V_DIM // 2
RET_CHUNK = 128
ATT_HEAD_DIM = 64
ATT_HEADS = D_MODEL // 2 // ATT_HEAD_DIM
DILATED_CONFIGS = ((128, 1), (512, 4), (2048, 16))
N_EXPERTS = 16
EC_CAPACITY_FACTOR = 2
D_FF_EXPERT = 2048

RET_QK_W = RET_HEADS * RET_QK_DIM
RET_V_W = RET_HEADS * RET_V_DIM
ATT_W = ATT_HEADS * ATT_HEAD_DIM
MIX_WIDTH = RET_V_W + ATT_W
IN_PROJ_WIDTH = 2 * RET_QK_W + 2 * RET_V_W + 3 * ATT_W
RMS_EPS = 1e-6
GN_EPS = 1e-5
MASK_VALUE = -1e30


def rmsnorm(x, g):
    xf = x.astype(jnp.float32)
    y = xf * lax.rsqrt(jnp.mean(xf * xf, axis=-1, keepdims=True) + RMS_EPS)
    return (y * g.astype(jnp.float32)).astype(x.dtype)

def alibi_slopes(n):
    return 2.0 ** (-8.0 * (jnp.arange(n, dtype=jnp.float32) + 1.0) / n)

def retention_scan(q, k, v, log_gamma, inclusive):
    B, H, S, dk = q.shape
    dv = v.shape[-1]
    C = RET_CHUNK
    n = S // C
    qc = q.reshape(B, H, n, C, dk)
    kc = k.reshape(B, H, n, C, dk)
    vc = v.reshape(B, H, n, C, dv)
    pos = jnp.arange(C, dtype=jnp.float32)
    rel = pos[:, None] - pos[None, :]
    mask = (rel >= 0) if inclusive else (rel > 0)
    lg = log_gamma[:, None, None]
    intra_decay = jnp.where(mask[None], jnp.exp(lg * jnp.where(mask, rel, 0.0)[None]), 0.0)
    scores = jnp.einsum('bhnid,bhnjd->bhnij', qc, kc) * intra_decay[None, :, None]
    o = jnp.einsum('bhnij,bhnjv->bhniv', scores, vc)
    k_tail = kc * jnp.exp(log_gamma[:, None] * (C - 1.0 - pos))[None, :, None, :, None]
    kv = jnp.einsum('bhnjd,bhnjv->nbhdv', k_tail, vc)
    chunk_decay = jnp.exp(log_gamma * C)[None, :, None, None]

    def step(state, kv_n):
        return chunk_decay * state + kv_n, state

    _, prev = lax.scan(step, jnp.zeros((B, H, dk, dv), jnp.float32), kv)
    q_head = qc * jnp.exp(log_gamma[:, None] * (pos + 1.0))[None, :, None, :, None]
    o = o + jnp.einsum('bhnid,nbhdv->bhniv', q_head, prev)
    return o.reshape(B, H, S, dv)

def bidirectional_retention(q, k, v, logit_fwd, logit_bwd):
    qf, kf, vf = q.astype(jnp.float32), k.astype(jnp.float32), v.astype(jnp.float32)
    lg_f = jax.nn.log_sigmoid(logit_fwd.astype(jnp.float32))
    lg_b = jax.nn.log_sigmoid(logit_bwd.astype(jnp.float32))
    y_f = retention_scan(qf, kf, vf, lg_f, True)
    y_b = jnp.flip(retention_scan(jnp.flip(qf, 2), jnp.flip(kf, 2), jnp.flip(vf, 2), lg_b, False), 2)
    y = y_f + y_b
    mu = jnp.mean(y, axis=-1, keepdims=True)
    var = jnp.mean(jnp.square(y - mu), axis=-1, keepdims=True)
    return (y - mu) * lax.rsqrt(var + GN_EPS)

def banded_attention(q, k, v, half, slopes):
    N, H, L, dh = q.shape
    W = half
    nb = -(-L // W)
    pad = nb * W - L
    qb = jnp.pad(q, ((0, 0), (0, 0), (0, pad), (0, 0))).reshape(N, H, nb, W, dh)

    def windows(t):
        tb = jnp.pad(t, ((0, 0), (0, 0), (W, pad + W), (0, 0))).reshape(N, H, nb + 2, W, dh)
        return jnp.concatenate([tb[:, :, :-2], tb[:, :, 1:-1], tb[:, :, 2:]], axis=3)

    kw, vw = windows(k), windows(v)
    qpos = jnp.arange(nb * W).reshape(nb, W)
    kpos = jnp.arange(nb)[:, None] * W - W + jnp.arange(3 * W)[None, :]
    dist = jnp.abs(kpos[:, None, :] - qpos[:, :, None])
    valid = (dist <= W) & (kpos[:, None, :] >= 0) & (kpos[:, None, :] < L)
    s = jnp.einsum('nhbqd,nhbkd->nhbqk', qb, kw).astype(jnp.float32) * (dh ** -0.5)
    s = s - slopes[None, :, None, None, None] * dist.astype(jnp.float32)[None, None]
    s = jnp.where(valid[None, None], s, MASK_VALUE)
    lse = jax.nn.logsumexp(s, axis=-1)
    p = jnp.exp(s - lse[..., None])
    o = jnp.einsum('nhbqk,nhbkd->nhbqd', p, vw.astype(jnp.float32))
    return o.reshape(N, H, nb * W, dh)[:, :, :L], lse.reshape(N, H, nb * W)[:, :, :L]

def dilated_attention(q, k, v, window, dilation, slopes):
    B, H, S, dh = q.shape
    L = S // dilation

    def to_sub(t):
        return t.reshape(B, H, L, dilation, dh).transpose(0, 3, 1, 2, 4).reshape(B * dilation, H, L, dh)

    o, lse = banded_attention(to_sub(q), to_sub(k), to_sub(v), window // (2 * dilation), slopes * dilation)
    o = o.reshape(B, dilation, H, L, dh).transpose(0, 2, 3, 1, 4).reshape(B, H, S, dh)
    lse = lse.reshape(B, dilation, H, L).transpose(0, 2, 3, 1).reshape(B, H, S)
    return o, lse

def expert_choice_moe(h, w_router, w_gate, w_up, w_down):
    B, S, D = h.shape
    E = w_router.shape[-1]
    cap = EC_CAPACITY_FACTOR * S // E
    affinity = jax.nn.softmax((h @ w_router).astype(jnp.float32), axis=-1)
    gates, idx = lax.top_k(jnp.swapaxes(affinity, 1, 2), cap)
    flat_idx = idx.reshape(B, E * cap)
    b_idx = jnp.arange(B)[:, None]
    xe = h[b_idx, flat_idx].reshape(B, E, cap, D)
    a = jnp.einsum('becd,edf->becf', xe, w_gate)
    u = jnp.einsum('becd,edf->becf', xe, w_up)
    ye = jnp.einsum('becf,efd->becd', jax.nn.silu(a) * u, w_down)
    ye = ye * gates[..., None].astype(ye.dtype)
    out = jnp.zeros_like(h).at[b_idx, flat_idx].add(ye.reshape(B, E * cap, D).astype(h.dtype))
    return out

def first_inputs(seed: int = 0) -> dict:
    key = jax.random.key(seed)
    ks = jax.random.split(key, 20)
    f32 = jnp.float32
    D, F, E = D_MODEL, D_FF_EXPERT, N_EXPERTS
    nrm = lambda k, shape, s: jax.random.normal(k, shape, f32) * s
    base_logit = jnp.log(2.0 ** (5.0 + jnp.arange(RET_HEADS, dtype=f32)) - 1.0)
    return {
        "x": nrm(ks[0], (BATCH, SEQ, D), 1.0),
        "c": nrm(ks[1], (BATCH, D), 1.0),
        "w_ada": nrm(ks[2], (DEPTH, D, 6 * D), 0.5 * D ** -0.5),
        "b_ada": nrm(ks[3], (DEPTH, 6 * D), 0.01),
        "g_pre_mix": 1.0 + nrm(ks[4], (DEPTH, D), 0.01),
        "g_post_mix": 1.0 + nrm(ks[5], (DEPTH, D), 0.01),
        "g_pre_ffn": 1.0 + nrm(ks[6], (DEPTH, D), 0.01),
        "g_post_ffn": 1.0 + nrm(ks[7], (DEPTH, D), 0.01),
        "w_in": nrm(ks[8], (DEPTH, D, IN_PROJ_WIDTH), D ** -0.5),
        "ret_decay_fwd": base_logit[None] + nrm(ks[9], (DEPTH, RET_HEADS), 0.1),
        "ret_decay_bwd": base_logit[None] + nrm(ks[10], (DEPTH, RET_HEADS), 0.1),
        "w_out": nrm(ks[11], (DEPTH, MIX_WIDTH, D), MIX_WIDTH ** -0.5),
        "w_router": nrm(ks[12], (DEPTH, D, E), D ** -0.5),
        "w_gate_e": nrm(ks[13], (DEPTH, E, D, F), D ** -0.5),
        "w_up_e": nrm(ks[14], (DEPTH, E, D, F), D ** -0.5),
        "w_down_e": nrm(ks[15], (DEPTH, E, F, D), F ** -0.5),
    }

def first_block(x, c, w_ada, b_ada, g_pre_mix, g_post_mix, g_pre_ffn, g_post_ffn, w_in,
              ret_decay_fwd, ret_decay_bwd, w_out, w_router, w_gate_e, w_up_e, w_down_e):
    B, S, D = x.shape
    slopes = alibi_slopes(ATT_HEADS)
    split_at = np.cumsum([RET_QK_W, RET_QK_W, RET_V_W, RET_V_W, ATT_W, ATT_W]).tolist()

    def heads(t, n_heads):
        return t.reshape(B, S, n_heads, -1).transpose(0, 2, 1, 3)

    for l in range(DEPTH):
        mod = jax.nn.silu(c) @ w_ada[l] + b_ada[l]
        shift_m, scale_m, gate_m, shift_f, scale_f, gate_f = [m[:, None, :] for m in jnp.split(mod, 6, axis=-1)]

        h = rmsnorm(x, g_pre_mix[l]) * (1.0 + scale_m) + shift_m
        proj = h @ w_in[l]
        rq, rk, rv, rg, aq, ak, av = jnp.split(proj, split_at, axis=-1)

        y_ret = bidirectional_retention(heads(rq, RET_HEADS), heads(rk, RET_HEADS) * (RET_QK_DIM ** -0.5),
                                        heads(rv, RET_HEADS), ret_decay_fwd[l], ret_decay_bwd[l])
        y_ret = y_ret.transpose(0, 2, 1, 3).reshape(B, S, RET_V_W).astype(x.dtype)
        y_ret = jax.nn.silu(rg) * y_ret

        qh, kh, vh = heads(aq, ATT_HEADS), heads(ak, ATT_HEADS), heads(av, ATT_HEADS)
        results = [dilated_attention(qh, kh, vh, w, d, slopes) for (w, d) in DILATED_CONFIGS]
        outs = jnp.stack([r[0] for r in results])
        lses = jnp.stack([r[1] for r in results])
        mix_w = jax.nn.softmax(lses, axis=0)
        y_att = jnp.sum(mix_w[..., None] * outs, axis=0)
        y_att = y_att.transpose(0, 2, 1, 3).reshape(B, S, ATT_W).astype(x.dtype)

        mixed = jnp.concatenate([y_ret, y_att], axis=-1) @ w_out[l]
        x = x + gate_m * rmsnorm(mixed, g_post_mix[l])

        h = rmsnorm(x, g_pre_ffn[l]) * (1.0 + scale_f) + shift_f
        moe = expert_choice_moe(h, w_router[l], w_gate_e[l], w_up_e[l], w_down_e[l])
        x = x + gate_f * rmsnorm(moe, g_post_ffn[l])
    return x


DEPTH_2 = 2

POOL_GROUPS = 4
POOL_GROUP_DIM = 128
POOL_WIDTH = POOL_GROUPS * POOL_GROUP_DIM
POOL_WINDOWS = (2, 4, 8, 16)
LRU_HEADS = 10
LRU_HEAD_DIM = 128
LRU_WIDTH = LRU_HEADS * LRU_HEAD_DIM
CONV_WIDTH = 4
LRU_C = 8.0
D_FF = 2816
EPS = 1e-6
IN_WIDTH = POOL_WIDTH + 2 * LRU_WIDTH + 2 * D_MODEL


def rmsnorm_2(x, g):
    xf = x.astype(jnp.float32)
    var = jnp.mean(xf * xf, axis=-1, keepdims=True)
    return (xf * lax.rsqrt(var + EPS) * g.astype(jnp.float32)).astype(x.dtype)

def swiglu_ffn(h, w_up, w_down):
    u = h @ w_up
    a, b = jnp.split(u, 2, axis=-1)
    return (jax.nn.silu(a) * b) @ w_down

def causal_pool_minus_self(u, window):
    b, s, c = u.shape
    uf = u.astype(jnp.float32)
    cs = jnp.cumsum(uf, axis=1)
    cs_pad = jnp.concatenate([jnp.zeros((b, 1, c), jnp.float32), cs], axis=1)
    prev = jnp.concatenate([jnp.zeros((b, window - 1, c), jnp.float32), cs_pad[:, : s - window + 1]], axis=1)
    count = jnp.minimum(jnp.arange(1, s + 1, dtype=jnp.float32), float(window))[None, :, None]
    return ((cs - prev) / count - uf).astype(u.dtype)

def pool_mixer(u, w_grp, b_grp, scale):
    b, s, _ = u.shape
    ug = u.reshape(b, s, POOL_GROUPS, POOL_GROUP_DIM)
    pooled = jnp.stack([causal_pool_minus_self(ug[:, :, g], POOL_WINDOWS[g]) for g in range(POOL_GROUPS)], axis=2)
    mixed = jnp.einsum('bsgc,gcd->bsgd', pooled, w_grp) + b_grp
    return mixed.reshape(b, s, POOL_WIDTH) * scale

def causal_depthwise_conv(u, w, bias):
    s = u.shape[1]
    up = jnp.pad(u, ((0, 0), (CONV_WIDTH - 1, 0), (0, 0)))
    y = sum(up[:, k:k + s] * w[k] for k in range(CONV_WIDTH))
    return y + bias

def _lru_combine(left, right):
    a_l, b_l = left
    a_r, b_r = right
    return a_l * a_r, a_r * b_l + b_r

def rg_lru(u, w_a, b_a, w_x, b_x, lam):
    b, s, _ = u.shape
    uh = u.reshape(b, s, LRU_HEADS, LRU_HEAD_DIM)
    r = jax.nn.sigmoid(jnp.einsum('bshd,hde->bshe', uh, w_a) + b_a).reshape(b, s, LRU_WIDTH)
    i = jax.nn.sigmoid(jnp.einsum('bshd,hde->bshe', uh, w_x) + b_x).reshape(b, s, LRU_WIDTH)
    log_a = -LRU_C * r.astype(jnp.float32) * jax.nn.softplus(-lam.astype(jnp.float32))
    a = jnp.exp(log_a)
    mult = jnp.sqrt(-jnp.expm1(2.0 * log_a))
    bx = mult * (i * u).astype(jnp.float32)
    _, h = lax.associative_scan(_lru_combine, (a, bx), axis=1)
    return h.astype(u.dtype)

def hybrid_mixer(h, w_in, pool_w, pool_b, pool_scale, w_pool_up, conv_w, conv_b,
                 lru_w_a, lru_b_a, lru_w_x, lru_b_x, lru_lambda, w_lru_up, w_out):
    proj = h @ w_in
    s1 = POOL_WIDTH
    s2 = s1 + LRU_WIDTH
    s3 = s2 + LRU_WIDTH
    u_pool, u_lru, u_gelu, g_logits = proj[..., :s1], proj[..., s1:s2], proj[..., s2:s3], proj[..., s3:]
    y_pool = pool_mixer(u_pool, pool_w, pool_b, pool_scale) @ w_pool_up
    v = causal_depthwise_conv(u_lru, conv_w, conv_b)
    y_lru = (rg_lru(v, lru_w_a, lru_b_a, lru_w_x, lru_b_x, lru_lambda) * jax.nn.gelu(u_gelu)) @ w_lru_up
    g = jax.nn.sigmoid(g_logits)
    g_pool, g_lru = g[..., :D_MODEL], g[..., D_MODEL:]
    return (g_pool * y_pool + g_lru * y_lru) @ w_out

def second_inputs(seed: int = 0) -> dict:
    key = jax.random.key(seed)
    ks = jax.random.split(key, 26)
    f32 = jnp.float32

    def nrm(k, shape, fan_in):
        return jax.random.normal(k, shape, f32) * (fan_in ** -0.5)

    def gain(k, shape):
        return 1.0 + 0.02 * jax.random.normal(k, shape, f32)

    def small(k, shape):
        return 0.01 * jax.random.normal(k, shape, f32)

    L = DEPTH_2
    a_c = jax.random.uniform(ks[17], (L, LRU_WIDTH), f32, 0.9, 0.999)
    sig = a_c ** (1.0 / LRU_C)
    lam = jnp.log(sig) - jnp.log1p(-sig)
    return {
        "x": jax.random.normal(ks[0], (BATCH, SEQ, D_MODEL), f32),
        "norm_ffn1": gain(ks[1], (L, D_MODEL)),
        "ffn1_w_up": nrm(ks[2], (L, D_MODEL, 2 * D_FF), D_MODEL),
        "ffn1_w_down": nrm(ks[3], (L, D_FF, D_MODEL), D_FF),
        "norm_mix": gain(ks[4], (L, D_MODEL)),
        "w_in": nrm(ks[5], (L, D_MODEL, IN_WIDTH), D_MODEL),
        "pool_w": nrm(ks[6], (L, POOL_GROUPS, POOL_GROUP_DIM, POOL_GROUP_DIM), POOL_GROUP_DIM),
        "pool_b": small(ks[7], (L, POOL_GROUPS, POOL_GROUP_DIM)),
        "pool_scale": 1.0 + 0.1 * jax.random.normal(ks[8], (L, POOL_WIDTH), f32),
        "w_pool_up": nrm(ks[9], (L, POOL_WIDTH, D_MODEL), POOL_WIDTH),
        "conv_w": nrm(ks[10], (L, CONV_WIDTH, LRU_WIDTH), CONV_WIDTH),
        "conv_b": small(ks[11], (L, LRU_WIDTH)),
        "lru_w_a": nrm(ks[12], (L, LRU_HEADS, LRU_HEAD_DIM, LRU_HEAD_DIM), LRU_HEAD_DIM),
        "lru_b_a": small(ks[13], (L, LRU_HEADS, LRU_HEAD_DIM)),
        "lru_w_x": nrm(ks[14], (L, LRU_HEADS, LRU_HEAD_DIM, LRU_HEAD_DIM), LRU_HEAD_DIM),
        "lru_b_x": small(ks[15], (L, LRU_HEADS, LRU_HEAD_DIM)),
        "lru_lambda": lam,
        "w_lru_up": nrm(ks[16], (L, LRU_WIDTH, D_MODEL), LRU_WIDTH),
        "w_out": nrm(ks[18], (L, D_MODEL, D_MODEL), D_MODEL),
        "norm_ffn2": gain(ks[19], (L, D_MODEL)),
        "ffn2_w_up": nrm(ks[20], (L, D_MODEL, 2 * D_FF), D_MODEL),
        "ffn2_w_down": nrm(ks[21], (L, D_FF, D_MODEL), D_FF),
        "final_norm": gain(ks[22], (D_MODEL,)),
    }

def second_block(x, norm_ffn1, ffn1_w_up, ffn1_w_down, norm_mix, w_in, pool_w, pool_b, pool_scale,
              w_pool_up, conv_w, conv_b, lru_w_a, lru_b_a, lru_w_x, lru_b_x, lru_lambda, w_lru_up,
              w_out, norm_ffn2, ffn2_w_up, ffn2_w_down, final_norm):
    for l in range(DEPTH_2):
        x = x + 0.5 * swiglu_ffn(rmsnorm_2(x, norm_ffn1[l]), ffn1_w_up[l], ffn1_w_down[l])
        x = x + hybrid_mixer(rmsnorm_2(x, norm_mix[l]), w_in[l], pool_w[l], pool_b[l], pool_scale[l],
                             w_pool_up[l], conv_w[l], conv_b[l], lru_w_a[l], lru_b_a[l],
                             lru_w_x[l], lru_b_x[l], lru_lambda[l], w_lru_up[l], w_out[l])
        x = x + 0.5 * swiglu_ffn(rmsnorm_2(x, norm_ffn2[l]), ffn2_w_up[l], ffn2_w_down[l])
    return rmsnorm_2(x, final_norm)


def setup_inputs(seed=0):
    out = dict(first_inputs(seed))
    for name, value in second_inputs(seed + 1).items():
        if name != "x":
            out[name + "_2"] = value
    return out


def reference(
    x, c, w_ada, b_ada, g_pre_mix, g_post_mix, g_pre_ffn, g_post_ffn, w_in, ret_decay_fwd,
    ret_decay_bwd, w_out, w_router, w_gate_e, w_up_e, w_down_e, norm_ffn1_2, ffn1_w_up_2,
    ffn1_w_down_2, norm_mix_2, w_in_2, pool_w_2, pool_b_2, pool_scale_2, w_pool_up_2, conv_w_2,
    conv_b_2, lru_w_a_2, lru_b_a_2, lru_w_x_2, lru_b_x_2, lru_lambda_2, w_lru_up_2, w_out_2,
    norm_ffn2_2, ffn2_w_up_2, ffn2_w_down_2, final_norm_2,
):
    x = first_block(
        x, c, w_ada, b_ada, g_pre_mix, g_post_mix, g_pre_ffn, g_post_ffn, w_in, ret_decay_fwd,
        ret_decay_bwd, w_out, w_router, w_gate_e, w_up_e, w_down_e,
    )
    return second_block(
        x, norm_ffn1_2, ffn1_w_up_2, ffn1_w_down_2, norm_mix_2, w_in_2, pool_w_2, pool_b_2,
        pool_scale_2, w_pool_up_2, conv_w_2, conv_b_2, lru_w_a_2, lru_b_a_2, lru_w_x_2,
        lru_b_x_2, lru_lambda_2, w_lru_up_2, w_out_2, norm_ffn2_2, ffn2_w_up_2, ffn2_w_down_2,
        final_norm_2,
    )


_drawn_inputs = setup_inputs


def setup_inputs(seed=0):
    import zlib

    import numpy as np

    out = dict(_drawn_inputs(seed))
    spreads = {}
    factors = {'g_pre_mix': 3.035,
     'g_post_ffn': 8.0,
     'norm_ffn1_2': 5.054,
     'norm_mix_2': 3.944,
     'pool_b_2': 51.052,
     'conv_b_2': 3.479,
     'lru_b_a_2': 49.927,
     'lru_b_x_2': 38.147,
     'norm_ffn2_2': 5.966,
     'final_norm_2': 8.734}
    for name, (base, spread) in spreads.items():
        noise = np.random.default_rng([zlib.crc32(name.encode()), seed]).standard_normal(out[name].shape)
        drawn = base * np.exp(spread * noise) if base else spread * noise
        out[name] = __import__('jax').numpy.asarray(drawn.astype(out[name].dtype))
    for name, factor in factors.items():
        out[name] = (out[name] * factor).astype(out[name].dtype)
    return out
```

```python
from contextlib import ExitStack

import numpy as np
import concourse.bass as bass
from concourse import mybir

F32 = mybir.dt.float32
BF16 = mybir.dt.bfloat16
I32 = mybir.dt.int32
U32 = mybir.dt.uint32
ALU = mybir.AluOpType
ACT = mybir.ActivationFunctionType
AX = mybir.AxisListType

P = 128
D = 1024
S = 256
KD = D // P
TT = S // P
EPS = 1e-6
GN_EPS = 1e-5

RET_HEADS, RET_QK = 4, 64
ATT_HEADS, ATT_DIM = 8, 64
QK_SCALE = 0.125
NEAR = 64
NEG = -1e30

E, CAP, FF = 16, 32, 2048
FB = FF // 512
LAYERS = 2
FFN = 2816
FK = FFN // P
HEADS = 10
POOLS = 4
POOL_WINDOWS = (2, 4, 8, 16)
TAPS = 4
LRU_C = 8.0

SLOTS = 6
SLOT = 4096
BANKS = 6


class Ring:

    def __init__(self, first, expert, layer):
        self.at = {}
        loads, uses = [0] * SLOTS, [0] * SLOTS
        self.per = {}
        for phase, tiles, turns in (("first", first, 1), ("expert", expert, E), ("layer", layer, LAYERS)):
            assert len(tiles) % SLOTS == 0
            own_loads, own_uses = [0] * SLOTS, [0] * SLOTS
            for i, tile in enumerate(tiles):
                if tile is None:
                    continue
                name, dmas = tile
                s = i % SLOTS
                own_loads[s] += dmas
                self.at[name] = (phase, s, loads[s] + own_loads[s], uses[s] + own_uses[s])
                own_uses[s] += 1
            self.per[phase] = (own_loads, own_uses)
            loads = [a + turns * b for a, b in zip(loads, own_loads)]
            uses = [a + turns * b for a, b in zip(uses, own_uses)]

    def slot(self, name):
        return self.at[name][1]

    def loaded(self, name, turn=0):
        phase, s, loads, _ = self.at[name]
        return turn * (16 * self.per[phase][0][s]) + 16 * loads

    def before(self, name, turn=0):
        phase, s, _, uses = self.at[name]
        return turn * self.per[phase][1][s] + uses

    def done(self, name, turn=0):
        phase, s, _, uses = self.at[name]
        return turn * self.per[phase][1][s] + uses + 1


def first_tiles():
    ada = [(("ada", i), 1) for i in range(12)]
    win = [(("win", i), 1) for i in range(6)]
    wout = [(("wout", i), 1) for i in range(2)]
    return ada[:4] + win + ada[4:] + wout + [None] * 4


def expert_tiles():
    pairs = [((kind, q), 1) for q in range(FB) for kind in ("gate", "up")]
    return pairs + [(("down", k), 1) for k in range(FB)]


def layer_tiles():
    def ffn(f):
        up = [((kind, f, j), 1) for j in range(5) for kind in ("upa", "upb")]
        return up + [(("upab", f), 2)] + [(("dn", f, c), 1) for c in range(KD)]

    mixer = [(("proj", i), 1) for i in (1, 2, 3, 0)] + [("small", 3)] + [(("proj", i), 1) for i in range(4, 10)]
    mixer += [("pup", 1)] + [(("lup", i), 1) for i in range(3)] + [(("lout", i), 1) for i in range(2)]
    tiles = ffn(0) + mixer + ffn(1)
    for at in (11, 23, 35, 47, 59):
        tiles.insert(at, None)
    return tiles


def layer_groups():
    def ffn(f):
        g = []
        for j in range(5):
            g += [(("a", f, 2 * j), "act"), (("a", f, 2 * j + 1), "act")]
            g += [(("b", f, 2 * j), "dve"), (("b", f, 2 * j + 1), "dve")]
        return g + [(("a", f, 10), "act"), (("b", f, 10), "dve")] + [(("dn", f, q), "dve") for q in range(4)]

    mixer = [(("lru", g), "act") for g in range(5)] + [(("gelu", 0), "act")]
    mixer += [(("pool", g), "act") for g in range(2)]
    mixer += [(("ra", g), "act") for g in range(5)] + [(("ix", g), "act") for g in range(5)]
    mixer += [(("pmix", g), "dve") for g in range(2)] + [(("gelu", g), "act") for g in range(1, 5)]
    mixer += [(("g", g), "act") for g in range(8)]
    mixer += [(("pup", g), "dve") for g in range(4)] + [(("lup", g), "dve") for g in range(4)]
    mixer += [(("out", g), "dve") for g in range(4)]
    return ffn(0) + mixer + ffn(1)


class Groups:

    def __init__(self, groups):
        self.n = {name: i for i, (name, _) in enumerate(groups)}
        self.engine = [e for _, e in groups]
        self.total = len(groups)
        assert self.total % BANKS == 0
        self.per = {e: self.engine.count(e) for e in ("act", "dve")}

    def bank(self, name):
        return self.n[name] % BANKS

    def done(self, name, layer):
        return layer * self.total + (self.total + self.n[name] + 1)

    def emptied(self, name, layer):
        n = self.n[name]
        e = self.engine[n]
        return e, layer * self.per[e] + (self.per[e] + self.engine[:n + 1].count(e))

    def bank_free(self, name, layer):
        n = self.n[name] - BANKS
        if n >= 0:
            e = self.engine[n]
            return e, layer * self.per[e] + (self.per[e] + self.engine[:n + 1].count(e))
        e = self.engine[n + self.total]
        return e, layer * self.per[e] + self.engine[:n + self.total + 1].count(e)


class Steps:

    def __init__(self, eng, sem, per=0, turn=0):
        self.eng, self.sem, self.per, self.turn, self.n = eng, sem, per, turn, 0

    def __call__(self, instruction):
        self.n += 1
        instruction.then_inc(self.sem, 1)
        if self.per:
            self.eng.wait_ge(self.sem, self.turn * self.per + self.n)
        else:
            self.eng.wait_ge(self.sem, self.n)


FIRST_ROWS = (("c", 8), ("b_ada", 48), ("g_pre_mix", 8), ("g_post_mix", 8), ("g_pre_ffn", 8),
              ("g_post_ffn", 8), ("final_norm", 8))
LAYER_ROWS = (("norm_ffn1", 8), ("norm_mix", 8), ("norm_ffn2", 8), ("conv_w", 40), ("conv_b", 10),
              ("lru_b_a", 10), ("lru_b_x", 10), ("lru_lambda", 10), ("pool_b", 4), ("pool_scale", 4))


def offsets(rows):
    at, out = 0, {}
    for name, n in rows:
        out[name] = at
        at += n
    return out, at


def block_kernel(nc, a, out):
    ring_plan = Ring(first_tiles(), expert_tiles(), layer_tiles())
    groups = Groups(layer_groups())
    fo, n_first = offsets(FIRST_ROWS)
    lo, n_layer = offsets(LAYER_ROWS)

    ctx = ExitStack()
    with ctx:
        def sb(name, shape, dt=F32):
            return ctx.enter_context(nc.sbuf_tensor(name, shape, dt))

        def sem(name):
            return ctx.enter_context(nc.semaphore(name))

        ring = sb("ring", [P, SLOTS, SLOT])
        x = sb("x", [P, KD, S])
        h = sb("h", [P, KD, S])
        std = sb("std", [P, S])
        rstd = sb("rstd", [P, S])
        ident = sb("ident", [P, P])
        mean_d = sb("mean_d", [P, P])
        mean_v = sb("mean_v", [P, P])
        first_cols = sb("first_cols", [P, n_first])
        layer_cols = sb("layer_cols", [P, LAYERS * n_layer])
        lc = sb("lc", [P, n_layer + 2 * HEADS])
        decay_in = sb("decay_in", [P, 8 + LAYERS * HEADS])
        soft = sb("soft", [P, 6, 8 + LAYERS * HEADS])
        nsp8 = sb("nsp8", [P, 2, LAYERS * HEADS])
        mod = sb("mod", [P, 48])
        gains = sb("gains", [P, 4, KD])
        inv_count = sb("inv_count", [P, POOLS, 16])
        pool_fix = sb("pool_fix", [P, POOLS, 16])
        upad = sb("upad", [P, HEADS, S + TAPS - 1])
        pool_u = sb("pool_u", [P, POOLS, 16 + S])
        WORK = 17664
        work = sb("work", [P, WORK])

        def carve(sizes):
            at, parts = 0, []
            for n in sizes:
                parts.append(work[:, at:at + n])
                at += n
            assert at <= WORK, at
            return parts

        (x_tok_, rqk_, rv_, rg_, aq_, ak_, av_, dret_, negdist_, mult_, pret_, s_, p_, patt_, gn_, gsq_,
         modrow_, sc_, wr_, small_) = carve(
            (2048, 1024, 1024, 1024, 1024, 1024, 1024, 2048, 512, 512, 1024, 1024, 1024, 512, 1024, 1024,
             256, 256, 128, 64))
        x_tok = x_tok_.rearrange("p (t d) -> p t d", t=TT)
        rows_in = gn_.rearrange("p (n r) -> p n r", r=P)
        rqk = rqk_.rearrange("p (c t) -> p c t", c=4)
        rv = rv_.rearrange("p (t v) -> p t v", t=TT)
        rg = rg_.rearrange("p (c t) -> p c t", c=4)
        aq = aq_.rearrange("p (c t) -> p c t", c=4)
        ak = ak_.rearrange("p (c t) -> p c t", c=4)
        av = av_.rearrange("p (t v) -> p t v", t=TT)
        dret = dret_.rearrange("p (h n) -> p h n", h=RET_HEADS)
        pret = pret_.rearrange("p (b s t) -> p b s t", b=2, s=TT)
        s_att = s_.rearrange("p (b t s) -> p b t s", b=2, t=TT)
        p_att = p_.rearrange("p (b t s) -> p b t s", b=2, t=TT)
        pT_att = patt_.rearrange("p (s t) -> p s t", s=TT)
        mixin = x_tok_.rearrange("p (c t) -> p c t", c=KD)
        gn = gn_.rearrange("p (c t) -> p c t", c=4)
        gsq = gsq_.rearrange("p (c t) -> p c t", c=4)
        modrow = modrow_.rearrange("p (b n) -> p b n", b=2)
        silu_c = sc_.rearrange("p (k m) -> p k m", k=KD)
        w_router = wr_.rearrange("p (k e) -> p k e", k=KD)
        att_max = small_[:, 0:4].rearrange("p (b t) -> p b t", b=2)
        att_sum = small_[:, 4:8].rearrange("p (b t) -> p b t", b=2)
        att_inv = small_[:, 8:12].rearrange("p (b t) -> p b t", b=2)
        mix = work[:, 2048:4096].rearrange("p (c t) -> p c t", c=KD)
        rel = p_[:, 0:512]
        dist = p_[:, 512:1024]
        keep = s_[:, 0:512]
        reli = s_[:, 512:1024]
        (xeT_, gT_, h_tok_, onehot_, weighted_, xe_, sg_, hg_, hT_, yp_, route_, zeros_) = carve(
            (KD * E * CAP, E * S, TT * D, TT * E * CAP, TT * E // 2 * P, KD * CAP, 256, 256, FB * P, D, 1024, 256))
        xeT = xeT_.rearrange("p (k n) -> p k n", k=KD)
        h_tok = h_tok_.rearrange("p (t d) -> p t d", t=TT)
        onehot = onehot_.rearrange("p (t n) -> p t n", t=TT)
        weighted = [part.rearrange("p (t e n) -> p t e n", t=TT, n=P) for part in (weighted_, h_tok_)]
        xe = xe_.rearrange("p (k n) -> p k n", k=KD)
        silu_gate = sg_.rearrange("p (b n) -> p b n", b=2)
        hidden = hg_.rearrange("p (b n) -> p b n", b=2)
        hiddenT = hT_.rearrange("p (q n) -> p q n", q=FB)
        y_part = yp_
        zeros = zeros_.bitcast(BF16)
        (u_, sa_) = carve((FK * S, 4 * 512))
        u = u_.rearrange("p (c t) -> p c t", c=FK)
        silu_a = sa_.rearrange("p (b n) -> p b n", b=4)
        (v_, i_, a_, r_, gel_, gs_) = carve((HEADS * S,) * 5 + (16 * S,))
        v = v_.rearrange("p (c t) -> p c t", c=HEADS)
        igate = i_.rearrange("p (c t) -> p c t", c=HEADS)
        decay = a_.rearrange("p (c t) -> p c t", c=HEADS)
        rgate = r_.rearrange("p (c t) -> p c t", c=HEADS)
        gel = gel_.rearrange("p (c t) -> p c t", c=HEADS)
        gs = gs_.rearrange("p (c t) -> p c t", c=16)
        pool_a = gs_[:, 0:1088].rearrange("p (g t) -> p g t", g=POOLS)
        pool_b = gs_[:, 1088:2176].rearrange("p (g t) -> p g t", g=POOLS)
        pooled = gs_[:, 2176:3200].rearrange("p (g t) -> p g t", g=POOLS)
        pool_mix = sb("pool_mix", [P, POOLS, S])
        routing = sb("routing", [P, 64 + 2 * E])
        t_col = routing[:, 0:2]
        lsum = routing[:, 2:4]
        lmax = routing[:, 4:6]
        linv = routing[:, 6:8]
        aff = routing[:, 64:64 + 2 * E].rearrange("p (t e) -> p t e", t=TT)
        affT = route_[0:E, 0:256]
        affW = route_[0:E, 256:512]
        top = route_[0:E, 512:544]
        topi = route_[0:E, 544:576].bitcast(U32)
        topf = route_[0:E, 576:608]
        spread = yp_[0:E, 0:512].rearrange("p (e c) -> p e c", e=E)
        ones_e = hT_[0:E, 0:P]
        out_tok = work[:, 0:2048].rearrange("p (t d) -> p t d", t=TT)

        psum = ctx.enter_context(nc.psum_tensor("psum", [P, 8 * 512], F32))
        bank = [psum[:, 512 * b:512 * (b + 1)] for b in range(8)]
        two_banks = [psum[:, 1024 * b:1024 * (b + 1)] for b in range(4)]
        moe_acc = psum[:, 2048:4096].rearrange("p (c t) -> p c t", c=KD)

        def mod_bank(i):
            return bank[6 + i % 2] if i < 4 else bank[7]

        loaded = [sem(f"loaded{s}") for s in range(SLOTS)]
        tile_done = [sem(f"tile_done{s}") for s in range(SLOTS)]
        slot_granted = sem("slot_granted")
        x_loaded, rows_loaded, misc_loaded = sem("x_loaded"), sem("rows_loaded"), sem("misc_loaded")
        ident_ready, consts_ready, rel_ready = sem("ident_ready"), sem("consts_ready"), sem("rel_ready")
        colsT_done, cols_ready = sem("colsT_done"), sem("cols_ready")
        xT_done, x_ready, sq_ready, ms_done = sem("xT_done"), sem("x_ready"), sem("sq_ready"), sem("ms_done")
        std_ready, scaled_ready, h_ready = sem("std_ready"), sem("scaled_ready"), sem("h_ready")
        silu_c_ready, modrow_ready, modT_done, mod_ready = (
            sem("silu_c_ready"), sem("modrow_ready"), sem("modT_done"), sem("mod_ready"))
        softexp_ready, soft_ready = sem("softexp_ready"), sem("soft_ready")
        dret_arg, dret_ready, masks_ready = sem("dret_arg"), sem("dret_ready"), sem("masks_ready")
        proj_ready = sem("proj_ready")
        ret_scored, pret_ready, ret_done, ret_copied = (
            sem("ret_scored"), sem("pret_ready"), sem("ret_done"), sem("ret_copied"))
        gmean_done, centred_ready, gsq_ready, gvar_done, gstd_ready, yret_ready = (
            sem("gmean_done"), sem("centred_ready"), sem("gsq_ready"), sem("gvar_done"), sem("gstd_ready"),
            sem("yret_ready"))
        att_scored, att_max_ready, att_exp, att_p_ready, att_pT_done, att_pT_ready, att_done, yatt_ready = (
            sem("att_scored"), sem("att_max_ready"), sem("att_exp"), sem("att_p_ready"), sem("att_pT_done"),
            sem("att_pT_ready"), sem("att_done"), sem("yatt_ready"))
        mix_ready = sem("mix_ready")
        htokT_done, htok_ready, logits_done, lmax_ready, lexp_ready, aff_ready = (
            sem("htokT_done"), sem("htok_ready"), sem("logits_done"), sem("lmax_ready"), sem("lexp_ready"),
            sem("aff_ready"))
        affT_done, spread_ready, index_done, onehot_ready, weighted_ready = (
            sem("affT_done"), sem("spread_ready"), sem("index_done"), sem("onehot_ready"), sem("weighted_ready"))
        xeT_done, xeT_ready, gT_done, gT_ready = sem("xeT_done"), sem("xeT_ready"), sem("gT_done"), sem("gT_ready")
        xe_ready, silu_ready, hidden_ready, hiddenT_done, hiddenT_ready, y_ready, moe_done = (
            sem("xe_ready"), sem("silu_ready"), sem("hidden_ready"), sem("hiddenT_done"), sem("hiddenT_ready"),
            sem("y_ready"), sem("moe_done"))
        x_moe_ready = sem("x_moe_ready")
        group_done = sem("group_done")
        emptied = {"act": sem("emptied_act"), "dve": sem("emptied_dve")}
        cols_layer = sem("cols_layer")
        l_sq, l_ms, l_std, l_h = sem("l_sq"), sem("l_ms"), sem("l_std"), sem("l_h")
        l_silu, v_ready, pool_sums, pooled_ready = sem("l_silu"), sem("v_ready"), sem("pool_sums"), sem("pooled_ready")
        decay_ready, m2_ready, mult_ready, iv_ready, lru_ready, z_ready = (
            sem("decay_ready"), sem("m2_ready"), sem("mult_ready"), sem("iv_ready"), sem("lru_ready"), sem("z_ready"))
        f_sq, f_ms, f_std, f_h, outT_done, out_ready_act, out_ready_dve, stored = (
            sem("f_sq"), sem("f_ms"), sem("f_std"), sem("f_h"), sem("outT_done"), sem("out_ready_act"),
            sem("out_ready_dve"), sem("stored"))
        dve_first, dve_layer, dve_final = sem("dve_first"), sem("dve_layer"), sem("dve_final")
        pool_first, pool_layer = sem("pool_first"), sem("pool_layer")
        act_layer, act_first = sem("act_layer"), sem("act_first")

        def slot_view(name, k, n):
            return ring[:, ring_plan.slot(name), 0:k * n].rearrange("p (k n) -> p k n", k=k)

        block = ctx.enter_context(nc.Block())

        @block.sync
        def _(sp):
            def load(name, dst, src, turn=None):
                s = ring_plan.slot(name)
                if turn is None:
                    if ring_plan.before(name):
                        sp.wait_ge(tile_done[s], ring_plan.before(name))
                else:
                    sp.wait_ge(tile_done[s], ring_plan.before(name, turn))
                    sp.sem_inc(slot_granted, 1)
                sp.dma_start(dst, src).then_inc(loaded[s], 16)

            def columns(w, first, n):
                return w.rearrange("(k p) n -> p k n", p=P)[:, :, first:first + n]

            for (name, _) in [t for t in first_tiles() if t]:
                kind, i = name
                w = {"ada": a["w_ada"][0], "win": a["w_in"][0], "wout": a["w_out"][0]}[kind]
                load(name, slot_view(name, KD, 512), columns(w, 512 * i, 512))

            with sp.Fori(0, E) as e:
                gate = a["w_gate_e"][0][bass.ds(e, 1)].rearrange("a (k p) n -> p (a k) n", p=P)
                up = a["w_up_e"][0][bass.ds(e, 1)].rearrange("a (k p) n -> p (a k) n", p=P)
                down = a["w_down_e"][0][bass.ds(e, 1)].rearrange("a (k p) n -> p (a k) n", p=P)
                for (name, _) in expert_tiles():
                    kind, q = name
                    if kind == "down":
                        load(name, slot_view(name, 4, D), down[:, 4 * q:4 * q + 4, :], e)
                    else:
                        w = gate if kind == "gate" else up
                        load(name, slot_view(name, KD, 512), w[:, :, 512 * q:512 * q + 512], e)

            held = [None] * SLOTS
            last_group = {}
            for f in range(2):
                for j in range(5):
                    last_group[("upa", f, j)] = ("a", f, 2 * j + 1)
                    last_group[("upb", f, j)] = ("b", f, 2 * j + 1)
                last_group[("upab", f)] = ("b", f, 10)
                for c in range(KD):
                    last_group[("dn", f, c)] = ("dn", f, c // 2)
            last_group |= {("proj", 1): ("lru", 1), ("proj", 2): ("lru", 3), ("proj", 3): ("gelu", 0),
                           ("proj", 0): ("pool", 1), "small": ("pmix", 1), ("proj", 4): ("gelu", 2),
                           ("proj", 5): ("gelu", 4), "pup": ("pup", 3), ("lup", 0): ("lup", 1),
                           ("lup", 1): ("lup", 2), ("lup", 2): ("lup", 3), ("lout", 0): ("out", 1),
                           ("lout", 1): ("out", 3)}
            last_group |= {("proj", 6 + i): ("g", 2 * i + 1) for i in range(4)}
            for tile in layer_tiles():
                if tile:
                    held[ring_plan.slot(tile[0])] = tile[0]
            last_of_layer = list(held)

            with sp.Fori(0, LAYERS) as l:
                def one(arg):
                    return a[arg][bass.ds(l, 1)]

                def rows(arg, n=P):
                    return one(arg).rearrange("a (k p) n -> p (a k) n", p=n)

                def grouped(arg):
                    return one(arg).rearrange("a h d e -> d (a h) e")

                now = list(last_of_layer)
                seen = [False] * SLOTS
                for tile in layer_tiles():
                    if tile is None:
                        continue
                    name = tile[0]
                    s = ring_plan.slot(name)
                    before = groups.done(last_group[now[s]], l)
                    sp.wait_ge(group_done, before if seen[s] else before - groups.total)
                    sp.sem_inc(slot_granted, 1)
                    now[s], seen[s] = name, True
                    kind = name[0] if isinstance(name, tuple) else name
                    if kind in ("upa", "upb"):
                        w = rows(("ffn1_w_up", "ffn2_w_up")[name[1]])
                        at = 512 * name[2] + (FFN if kind == "upb" else 0)
                        parts = [(slot_view(name, KD, 512), w[:, :, at:at + 512])]
                    elif kind == "upab":
                        w = rows(("ffn1_w_up", "ffn2_w_up")[name[1]])
                        view = slot_view(name, KD, 512)
                        parts = [(view[:, :, 0:256], w[:, :, 2560:FFN]),
                                 (view[:, :, 256:512], w[:, :, FFN + 2560:2 * FFN])]
                    elif kind == "dn":
                        w = rows(("ffn1_w_down", "ffn2_w_down")[name[1]])
                        parts = [(slot_view(name, FK, P), w[:, :, P * name[2]:P * name[2] + P])]
                    elif kind == "proj":
                        parts = [(slot_view(name, KD, 512), rows("w_in_2")[:, :, 512 * name[1]:512 * name[1] + 512])]
                    elif kind == "small":
                        view = slot_view(name, 2 * HEADS + POOLS, P)
                        parts = [(view[:, 0:HEADS, :], grouped("lru_w_a")),
                                 (view[:, HEADS:2 * HEADS, :], grouped("lru_w_x")),
                                 (view[:, 2 * HEADS:, :], grouped("pool_w"))]
                    elif kind == "pup":
                        parts = [(slot_view(name, POOLS, D), rows("w_pool_up"))]
                    elif kind == "lup":
                        n = 384 if name[1] < 2 else 256
                        parts = [(slot_view(name, HEADS, n), rows("w_lru_up")[:, :, 384 * name[1]:384 * name[1] + n])]
                    else:
                        parts = [(slot_view(name, KD, 512), rows("w_out_2")[:, :, 512 * name[1]:512 * name[1] + 512])]
                    for dst, src in parts:
                        sp.dma_start(dst, src).then_inc(loaded[s], 16)

            for t in range(TT):
                sp.wait_ge(out_ready_act, t + 1)
                sp.wait_ge(out_ready_dve, t + 1)
                sp.dma_start(out[0].rearrange("(t p) d -> p t d", p=P)[:, t, :], out_tok[:, t, :]).then_inc(stored, 16)
            sp.wait_ge(stored, 16 * TT)

        @block.gpsimd
        def _(pool):
            step = Steps(pool, pool_first)
            step(pool.memset(ident[:], 0.0))
            pool.affine_select(out=ident[:], in_=ident[:], compare_op=ALU.not_equal, fill=1.0, base=0,
                               pattern=[[-1, P]], channel_multiplier=1).then_inc(ident_ready, 1)
            pool.memset(mean_d[:], 1.0 / D)
            pool.memset(mean_v[:], 1.0 / P).then_inc(consts_ready, 1)
            pool.iota(rel.rearrange("p (t f) -> p t f", t=TT), pattern=[[-P, TT], [1, S]], base=0,
                      channel_multiplier=-1, allow_small_or_imprecise_dtypes=True)
            pool.iota(reli.bitcast(I32).rearrange("p (t f) -> p t f", t=TT), pattern=[[-P, TT], [1, S]], base=0,
                      channel_multiplier=-1).then_inc(rel_ready, 1)
            pool.iota(t_col, pattern=[[P, TT]], base=0, channel_multiplier=1, allow_small_or_imprecise_dtypes=True)
            pool.iota(pool_fix[:], pattern=[[0, POOLS], [1, 16]], base=1, channel_multiplier=0,
                      allow_small_or_imprecise_dtypes=True)
            pool.memset(upad[:, :, 0:TAPS - 1], 0.0)
            pool.memset(pool_u[:, :, 0:16], 0.0).then_inc(consts_ready, 1)

            with pool.Fori(0, LAYERS) as l:
                step = Steps(pool, pool_layer, 4, l)
                e, n = groups.emptied(("pool", 1), l)
                pool.wait_ge(emptied[e], n)
                T = 16 + S
                step(pool.tensor_tensor(pool_a[:, :, 1:T], pool_u[:, :, 1:T], pool_u[:, :, 0:T - 1], ALU.add))
                step(pool.tensor_tensor(pool_b[:, 1:4, 3:T], pool_a[:, 1:4, 3:T], pool_a[:, 1:4, 1:T - 2], ALU.add))
                step(pool.tensor_tensor(pool_a[:, 2:4, 7:T], pool_b[:, 2:4, 7:T], pool_b[:, 2:4, 3:T - 4], ALU.add))
                step(pool.tensor_tensor(pool_b[:, 3:4, 15:T], pool_a[:, 3:4, 15:T], pool_a[:, 3:4, 7:T - 8], ALU.add))
                pool.sem_inc(pool_sums, 1)
                e, n = groups.emptied(("ix", 4), l)
                pool.wait_ge(emptied[e], n)
                pool.tensor_tensor(igate, igate, v, ALU.mult).then_inc(iv_ready, 1)
                assert step.n == step.per

        @block.tensor
        def _(pe):
            def square_sums(ready, first, dst, done):
                for k in range(KD):
                    if k % 2 == 0:
                        pe.wait_ge(ready, first + k // 2)
                    mm = pe.matmul(dst, mean_d[:], h[:, k, :], start=(k == 0), stop=(k == KD - 1))
                mm.then_inc(done, 1)

            pe.wait_ge(ident_ready, 1)
            pe.wait_ge(rows_loaded, 16 * (len(FIRST_ROWS) + LAYERS * len(LAYER_ROWS)))
            pe.transpose(bank[0][:, 0:n_first], rows_in[0:n_first, 0, :], ident[0:n_first, 0:n_first])
            for l in range(LAYERS):
                mm = pe.transpose(bank[0][:, P * (1 + l):P * (1 + l) + n_layer], rows_in[0:n_layer, 1 + l, :],
                                  ident[0:n_layer, 0:n_layer])
            mm.then_inc(colsT_done, 1)
            pe.wait_ge(x_loaded, 16)
            for c in range(KD):
                for t in range(TT):
                    mm = pe.transpose(bank[1 + c // 2][:, S * (c % 2) + P * t:S * (c % 2) + P * (t + 1)],
                                      x_tok[:, t, P * c:P * (c + 1)], ident[:])
                if c % 2:
                    mm.then_inc(xT_done, 1)
            pe.wait_ge(consts_ready, 1)
            square_sums(sq_ready, 1, bank[5][:, 0:S], ms_done)

            def modulation(i):
                rows = mod_bank(i)[:, 0:P]
                if i >= 2:
                    pe.wait_ge(mod_ready, i - 1 if i < 4 else i)
                if i == 0:
                    pe.wait_ge(silu_c_ready, 1)
                name = ("ada", i)
                pe.wait_ge(loaded[ring_plan.slot(name)], ring_plan.loaded(name))
                w = slot_view(name, KD, 512)
                for k in range(KD):
                    for g in range(4):
                        mm = pe.matmul(rows[32 * g:32 * g + 32, :], silu_c[:, k, :], w[:, k, P * g:P * (g + 1)],
                                       start=(k == 0), stop=(k == KD - 1), skip_group_check=True)
                mm.then_inc(tile_done[ring_plan.slot(name)], 1)

            def modulation_columns(i):
                pe.wait_ge(modrow_ready, i + 1)
                pe.transpose(mod_bank(i)[:, P:2 * P], modrow[:, i % 2, :],
                             ident[:]).then_inc(modT_done, 1)

            for i in range(4):
                modulation(i)
                modulation_columns(i)

            for i in range(6):
                name = ("win", i)
                pe.wait_ge(loaded[ring_plan.slot(name)], ring_plan.loaded(name))
                if i == 1:
                    pe.wait_ge(x_ready, 4)
                if i >= 2:
                    pe.wait_ge(proj_ready, i - 1)
                w = slot_view(name, KD, 512)
                dst = two_banks[i % 2]
                if i in (1, 5):
                    for t in range(TT):
                        for k in range(KD):
                            mm = pe.matmul(dst[:, 512 * t:512 * (t + 1)], h[:, k, P * t:P * (t + 1)], w[:, k, :],
                                           start=(k == 0), stop=(k == KD - 1))
                else:
                    for c in range(4):
                        for k in range(KD):
                            if i == 0 and c == 0:
                                pe.wait_ge(h_ready, k + 1)
                            mm = pe.matmul(dst[:, S * c:S * (c + 1)], w[:, k, P * c:P * (c + 1)], h[:, k, :],
                                           start=(k == 0), stop=(k == KD - 1))
                mm.then_inc(tile_done[ring_plan.slot(name)], 1)

            pe.wait_ge(proj_ready, 6)

            def ret_scores(hd):
                at, c = RET_QK * (hd % 2), hd // 2
                if hd >= 2:
                    pe.wait_ge(pret_ready, hd - 1)
                for s in range(TT):
                    mm = pe.matmul(bank[4 + hd % 2][:, S * s:S * (s + 1)],
                                   rqk[at:at + RET_QK, 2 + c, P * s:P * (s + 1)], rqk[at:at + RET_QK, c, :],
                                   start=True, stop=True)
                mm.then_inc(ret_scored, 1)

            def ret_values(hd):
                pe.wait_ge(pret_ready, hd + 1)
                for s in range(TT):
                    mm = pe.matmul(two_banks[0][:, S * hd:S * (hd + 1)], rv[:, s, P * hd:P * (hd + 1)],
                                   pret[:, hd % 2, s, :], start=(s == 0), stop=(s == TT - 1))
                mm.then_inc(ret_done, 1)

            ret_scores(0)
            ret_scores(1)
            for hd in range(RET_HEADS):
                ret_values(hd)
                if hd + 2 < RET_HEADS:
                    ret_scores(hd + 2)

            def group_mean(src, ready, dst, done):
                for b in range(2):
                    pe.wait_ge(ready, b + 1)
                    mm = pe.matmul(dst[:, 512 * b:512 * (b + 1)], mean_v[:], src[:, 512 * b:512 * (b + 1)],
                                   start=True, stop=True)
                mm.then_inc(done, 1)

            def att_scores(hd):
                at, c = ATT_DIM * (hd % 2), hd // 2
                if hd >= 2:
                    pe.wait_ge(att_max_ready, hd - 1)
                for t in range(TT):
                    mm = pe.matmul(bank[4 + hd % 2][:, S * t:S * (t + 1)], aq[at:at + ATT_DIM, c, P * t:P * (t + 1)],
                                   ak[at:at + ATT_DIM, c, :], start=True, stop=True)
                mm.then_inc(att_scored, 1)

            def att_transpose(hd):
                pe.wait_ge(att_p_ready, hd + 1)
                if hd >= 1:
                    pe.wait_ge(att_pT_ready, hd)
                for s in range(TT):
                    for t in range(TT):
                        mm = pe.transpose(bank[6][:, S * s + P * t:S * s + P * (t + 1)],
                                          p_att[:, hd % 2, t, P * s:P * (s + 1)], ident[:])
                mm.then_inc(att_pT_done, 1)

            def att_values(hd):
                at, c = ATT_DIM * (hd % 2), hd // 2
                pe.wait_ge(att_pT_ready, hd + 1)
                for s in range(TT):
                    mm = pe.matmul(two_banks[1][at:at + ATT_DIM, S * c:S * (c + 1)],
                                   av[:, s, ATT_DIM * hd:ATT_DIM * (hd + 1)], pT_att[:, s, :],
                                   start=(s == 0), stop=(s == TT - 1), skip_group_check=True)
                mm.then_inc(att_done, 1)

            pe.wait_ge(pret_ready, RET_HEADS)
            att_scores(0)
            group_mean(gn_, ret_copied, two_banks[1], gmean_done)
            att_scores(1)
            for hd in range(ATT_HEADS):
                modulation(4 + hd)
                att_transpose(hd)
                if hd + 2 < ATT_HEADS:
                    att_scores(hd + 2)
                modulation_columns(4 + hd)
                if hd == 0:
                    group_mean(gsq_, gsq_ready, two_banks[0], gvar_done)
                    pe.wait_ge(centred_ready, 2)
                att_values(hd)

            for i in range(2):
                name = ("wout", i)
                pe.wait_ge(loaded[ring_plan.slot(name)], ring_plan.loaded(name))
                w = slot_view(name, KD, 512)
                for c in range(4):
                    for k in range(KD):
                        if i == 0 and c == 0 and k == 0:
                            pe.wait_ge(yret_ready, 4)
                        if i == 0 and c == 0 and k == 4:
                            pe.wait_ge(yatt_ready, 1)
                        mm = pe.matmul(two_banks[i][:, S * c:S * (c + 1)], w[:, k, P * c:P * (c + 1)], mixin[:, k, :],
                                       start=(k == 0), stop=(k == KD - 1))
                mm.then_inc(tile_done[ring_plan.slot(name)], 1)
            square_sums(sq_ready, 5, bank[5][:, 0:S], ms_done)
            square_sums(sq_ready, 9, bank[5][:, 0:S], ms_done)

            pe.wait_ge(misc_loaded, 48)
            for t in range(TT):
                for k in range(KD):
                    if t == 0:
                        pe.wait_ge(h_ready, KD + k + 1)
                    mm = pe.matmul(bank[4][:, E * t:E * (t + 1)], h[:, k, P * t:P * (t + 1)], w_router[:, k, :],
                                   start=(k == 0), stop=(k == KD - 1))
            mm.then_inc(logits_done, 1)
            for t in range(TT):
                for c in range(KD):
                    mm = pe.transpose(bank[2 * t + c // 4][:, P * (c % 4):P * (c % 4 + 1)], h[:, c, P * t:P * (t + 1)],
                                      ident[:])
                    if c % 4 == 3:
                        mm.then_inc(htokT_done, 1)
            pe.wait_ge(aff_ready, 1)
            for t in range(TT):
                mm = pe.transpose(bank[5][0:E, P * t:P * (t + 1)], aff[:, t, :], ident[:])
            mm.then_inc(affT_done, 1)
            pe.wait_ge(spread_ready, 1)
            pe.matmul(bank[6], ones_e, spread.rearrange("p e c -> p (e c)"), start=True, stop=True).then_inc(index_done, 1)

            pe.wait_ge(onehot_ready, 1)
            pe.wait_ge(htok_ready, 4)
            for k in range(KD):
                if k >= 4:
                    pe.wait_ge(xeT_ready, k - 3)
                for t in range(TT):
                    mm = pe.matmul(bank[k % 4], h_tok[:, t, P * k:P * (k + 1)], onehot[:, t, :],
                                   start=(t == 0), stop=(t == TT - 1))
                mm.then_inc(xeT_done, 1)
            for b in range(E // 2):
                pe.wait_ge(weighted_ready, 2 * b // (E // 2) + 1)
                if b < 4:
                    pe.wait_ge(xeT_ready, 5 + b)
                else:
                    pe.wait_ge(gT_ready, b - 3)
                for e in range(2 * b, 2 * b + 2):
                    for t in range(TT):
                        at = S * (e % 2) + P * t
                        mm = pe.transpose(bank[b % 4][:, at:at + P], weighted[e // 8][:, t, e % 8, :], ident[:])
                mm.then_inc(gT_done, 1)
            for b in range(4):
                pe.matmul(bank[4 + b], zeros[:, 0:P], zeros, start=True, stop=True)

            pe.wait_ge(gT_ready, E // 2)
            with pe.Fori(0, E) as e:
                def hidden_products(q):
                    pe.wait_ge(hidden_ready, 4 * e + (q + 1))
                    for half, kind in enumerate(("gate", "up")):
                        name = (kind, q)
                        pe.wait_ge(loaded[ring_plan.slot(name)], ring_plan.loaded(name, e))
                        w = slot_view(name, KD, 512)
                        for k in range(KD):
                            for g in range(4):
                                mm = pe.matmul(bank[q % 2][32 * g:32 * g + 32, P * half:P * (half + 1)], xe[:, k, :],
                                               w[:, k, P * g:P * (g + 1)], start=(k == 0), stop=(k == KD - 1),
                                               skip_group_check=True)
                        mm.then_inc(tile_done[ring_plan.slot(name)], 1)

                def hidden_transpose(q):
                    if q == 0:
                        pe.wait_ge(y_ready, e + 1)
                    pe.wait_ge(hidden_ready, 4 * e + (q + 3))
                    pe.transpose(bank[2 + q % 2][:, 0:P], hidden[:, q % 2, :], ident[:]).then_inc(hiddenT_done, 1)

                def down_products(k):
                    name = ("down", k)
                    if k == 0:
                        pe.wait_ge(hiddenT_ready, 4 * e + FB)
                    pe.wait_ge(loaded[ring_plan.slot(name)], ring_plan.loaded(name, e))
                    w = slot_view(name, 4, D)
                    for half in range(2):
                        for c in range(4):
                            mm = pe.matmul(two_banks[1][32 * c:32 * c + 32, 512 * half:512 * (half + 1)],
                                           hiddenT[:, k, 32 * c:32 * c + 32], w[:, c, 512 * half:512 * (half + 1)],
                                           start=(k == 0), stop=(k == FB - 1), skip_group_check=True)
                    mm.then_inc(tile_done[ring_plan.slot(name)], 1)

                pe.wait_ge(xe_ready, e + 1)
                hidden_products(0)
                hidden_products(1)
                hidden_transpose(0)
                hidden_products(2)
                hidden_transpose(1)
                hidden_products(3)
                hidden_transpose(2)
                hidden_transpose(3)
                for k in range(FB):
                    down_products(k)
                pe.wait_ge(y_ready, e + 2)
                for c in range(KD):
                    mm = pe.matmul(moe_acc[:, c, :], y_part[:, P * c:P * (c + 1)], gT_[:, bass.ds(e * S, S)],
                                   start=False, stop=True, skip_group_check=True)
                mm.then_inc(moe_done, 1)

            pe.sem_inc(group_done, groups.total)
            square_sums(sq_ready, 13, bank[0][:, 0:S], ms_done)

            with pe.Fori(0, LAYERS) as l:
                def tile(name, k, n):
                    pe.wait_ge(loaded[ring_plan.slot(name)], ring_plan.loaded(name, l))
                    return slot_view(name, k, n)

                def open_group(name):
                    e, n = groups.bank_free(name, l)
                    pe.wait_ge(emptied[e], n)
                    return bank[groups.bank(name)]

                def wait_emptied(name):
                    e, n = groups.emptied(name, l)
                    pe.wait_ge(emptied[e], n)

                def pair(name, w, cols, src, n_k, before_k=None):
                    dst = open_group(name)
                    for b, col in enumerate(cols):
                        for k in range(n_k):
                            if before_k and b == 0:
                                before_k(k)
                            mm = pe.matmul(dst[:, S * b:S * (b + 1)], w[:, k, P * col:P * (col + 1)], src[:, k, :],
                                           start=(k == 0), stop=(k == n_k - 1))
                    mm.then_inc(group_done, 1)

                def norm(i):
                    for k in range(KD):
                        if k % 2 == 0:
                            pe.wait_ge(l_sq, l * 12 + (4 * i + k // 2 + 1))
                        mm = pe.matmul(bank[7][:, 0:S], mean_d[:], h[:, k, :], start=(k == 0), stop=(k == KD - 1))
                    mm.then_inc(l_ms, 1)

                def ffn(f, i):
                    norm(i)

                    def h_chunk(k):
                        pe.wait_ge(l_h, l * 24 + (8 * i + k + 1))

                    for j in range(5):
                        for kind, part in (("upa", "a"), ("upb", "b")):
                            w = tile((kind, f, j), KD, 512)
                            for q in range(2):
                                pair((part, f, 2 * j + q), w, (2 * q, 2 * q + 1), h, KD,
                                     h_chunk if j == 0 and kind == "upa" and q == 0 else None)
                    w = tile(("upab", f), KD, 512)
                    pair(("a", f, 10), w, (0, 1), h, KD)
                    pair(("b", f, 10), w, (2, 3), h, KD)
                    for q in range(4):
                        dst = open_group(("dn", f, q))
                        for b in range(2):
                            w = tile(("dn", f, 2 * q + b), FK, P)
                            for k in range(FK):
                                if q == 0 and b == 0 and k % 2 == 0:
                                    wait_emptied(("b", f, k // 2))
                                mm = pe.matmul(dst[:, S * b:S * (b + 1)], w[:, k, :], u[:, k, :],
                                               start=(k == 0), stop=(k == FK - 1))
                        mm.then_inc(group_done, 1)

                ffn(0, 0)

                norm(1)

                def h_chunk(k):
                    pe.wait_ge(l_h, l * 24 + (8 + k + 1))

                for i in (1, 2):
                    w = tile(("proj", i), KD, 512)
                    for q in range(2):
                        pair(("lru", 2 * (i - 1) + q), w, (2 * q, 2 * q + 1), h, KD,
                             h_chunk if i == 1 and q == 0 else None)
                w = tile(("proj", 3), KD, 512)
                pair(("lru", 4), w, (0, 1), h, KD)
                pair(("gelu", 0), w, (2, 3), h, KD)
                w = tile(("proj", 0), KD, 512)
                for q in range(2):
                    pair(("pool", q), w, (2 * q, 2 * q + 1), h, KD)

                def per_head(name, w, first, src, heads):
                    dst = open_group(name)
                    for b, hd in enumerate(heads):
                        mm = pe.matmul(dst[:, S * b:S * (b + 1)], w[:, first + hd, :], src[:, hd, :],
                                       start=True, stop=True)
                    mm.then_inc(group_done, 1)

                w = tile("small", 2 * HEADS + POOLS, P)
                for q in range(5):
                    pe.wait_ge(v_ready, l * 5 + (q + 1))
                    per_head(("ra", q), w, 0, v, (2 * q, 2 * q + 1))
                for q in range(5):
                    per_head(("ix", q), w, HEADS, v, (2 * q, 2 * q + 1))
                pe.wait_ge(pooled_ready, l + 1)
                for q in range(2):
                    per_head(("pmix", q), w, 2 * HEADS, pooled, (2 * q, 2 * q + 1))
                for i in (4, 5):
                    w = tile(("proj", i), KD, 512)
                    for q in range(2):
                        pair(("gelu", 1 + 2 * (i - 4) + q), w, (2 * q, 2 * q + 1), h, KD)
                for i in range(4):
                    w = tile(("proj", 6 + i), KD, 512)
                    for q in range(2):
                        pair(("g", 2 * i + q), w, (2 * q, 2 * q + 1), h, KD)
                w = tile("pup", POOLS, D)
                wait_emptied(("pmix", 1))
                for q in range(4):
                    pair(("pup", q), w, (2 * q, 2 * q + 1), pool_mix, POOLS)
                pe.wait_ge(lru_ready, l + 1)
                lup = [None] * 3
                for q in range(4):
                    dst = open_group(("lup", q))
                    for b in range(2):
                        t, col = divmod(2 * q + b, 3)
                        if lup[t] is None:
                            lup[t] = tile(("lup", t), HEADS, 384 if t < 2 else 256)
                        for k in range(HEADS):
                            mm = pe.matmul(dst[:, S * b:S * (b + 1)], lup[t][:, k, P * col:P * (col + 1)],
                                           gel[:, k, :], start=(k == 0), stop=(k == HEADS - 1))
                    mm.then_inc(group_done, 1)
                for i in range(2):
                    w = tile(("lout", i), KD, 512)
                    for q in range(2):
                        def z_chunk(k):
                            if i == 0 and q == 0 and k % 2 == 0:
                                pe.wait_ge(z_ready, l * 4 + (k // 2 + 1))
                        pair(("out", 2 * i + q), w, (2 * q, 2 * q + 1), gs[:, 8:16, :], KD, z_chunk)

                ffn(1, 2)

            square_sums(f_sq, 1, bank[7][:, 0:S], f_ms)
            for t in range(TT):
                for c in range(KD):
                    if t == 0:
                        pe.wait_ge(f_h, c + 1)
                    mm = pe.transpose(bank[2 * t + c // 4][:, P * (c % 4):P * (c % 4 + 1)], h[:, c, P * t:P * (t + 1)],
                                      ident[:])
                    if c % 4 == 3:
                        mm.then_inc(outT_done, 1)

        @block.scalar
        def _(act):
            step = Steps(act, act_first)
            act.dma_start(x_tok, a["x"][0].rearrange("(t p) d -> p t d", p=P)).then_inc(x_loaded, 16)
            for name, n in FIRST_ROWS:
                src = a[name][0] if name != "final_norm" else a[name]
                act.dma_start(rows_in[fo[name]:fo[name] + n, 0, :], src.rearrange("(c p) -> c p", p=P)).then_inc(rows_loaded, 16)
            for l in range(LAYERS):
                for name, n in LAYER_ROWS:
                    src = a[name][l]
                    if name == "conv_w":
                        src = src.rearrange("k (c p) -> (k c) p", p=P)
                    elif name not in ("lru_b_a", "lru_b_x", "pool_b"):
                        src = src.rearrange("(c p) -> c p", p=P)
                    act.dma_start(rows_in[lo[name]:lo[name] + n, 1 + l, :], src).then_inc(rows_loaded, 16)
            for i, name in enumerate(("ret_decay_fwd", "ret_decay_bwd")):
                act.dma_start(decay_in[:, 4 * i:4 * i + 4], a[name].to_broadcast([P, 4])).then_inc(misc_loaded, 16)
            act.dma_start(w_router, a["w_router"][0].rearrange("(k p) e -> p k e", p=P)).then_inc(misc_loaded, 16)

            def root(ms, done, n, ready, eps=EPS):
                act.wait_ge(done, n)
                act.activation(std[:], ms, ACT.Sqrt, bias=eps).then_inc(ready, 1)

            act.wait_ge(cols_ready, 1)
            act.activation(silu_c, first_cols[:, fo["c"]:fo["c"] + KD].unsqueeze(2).broadcast_to([P, KD, 32]),
                           ACT.Silu).then_inc(silu_c_ready, 1)
            for b in range(4):
                act.wait_ge(x_ready, b + 1)
                act.activation(h[:, 2 * b:2 * b + 2, :], x[:, 2 * b:2 * b + 2, :], ACT.Square).then_inc(sq_ready, 1)
            root(bank[5][:, 0:S], ms_done, 1, std_ready)
            act.wait_ge(softexp_ready, 1)
            act.activation(soft[:, 1, :], soft[:, 0, :], ACT.Exp, scale=-1.0).then_inc(softexp_ready, 1)
            for hd in range(RET_HEADS):
                act.wait_ge(dret_arg, hd + 1)
                act.activation(dret[:, hd, :], dret[:, hd, :], ACT.Exp).then_inc(dret_ready, 1)
            for k in range(KD):
                act.wait_ge(scaled_ready, k + 1)
                act.activation(h[:, k, :], h[:, k, :], ACT.Identity, bias=mod[:, k:k + 1]).then_inc(h_ready, 1)

            for i, (dst, func) in enumerate(((None, None), (rv_, ACT.Copy), (rg_, ACT.Silu), (aq_, None),
                                             (ak_, ACT.Copy), (av_, ACT.Copy))):
                name = ("win", i)
                act.wait_ge(tile_done[ring_plan.slot(name)], ring_plan.done(name))
                src = two_banks[i % 2]
                if i == 0:
                    act.activation(rqk_[:, 0:512], src[:, 0:512], ACT.Copy)
                    act.mul(rqk_[:, 512:1024], src[:, 512:1024], QK_SCALE).then_inc(proj_ready, 1)
                elif i == 3:
                    act.mul(dst, src, QK_SCALE).then_inc(proj_ready, 1)
                else:
                    act.activation(dst, src, func).then_inc(proj_ready, 1)

            for b in range(2):
                act.wait_ge(ret_done, 2 * b + 2)
                act.copy(gn_[:, 512 * b:512 * (b + 1)], two_banks[0][:, 512 * b:512 * (b + 1)]).then_inc(ret_copied, 1)
            for b in range(2):
                act.wait_ge(centred_ready, b + 1)
                act.activation(gsq_[:, 512 * b:512 * (b + 1)], gn_[:, 512 * b:512 * (b + 1)], ACT.Square).then_inc(gsq_ready, 1)

            def att_softmax(hd):
                act.wait_ge(att_max_ready, hd + 1)
                for t in range(TT):
                    ins = act.activation(s_att[:, hd % 2, t, :], s_att[:, hd % 2, t, :], ACT.Exp,
                                         bias=att_max[:, hd % 2, t:t + 1])
                ins.then_inc(att_exp, 1)

            def att_copy(hd):
                act.wait_ge(att_pT_done, hd + 1)
                if hd >= 1:
                    act.wait_ge(att_done, hd)
                act.copy(patt_, bank[6]).then_inc(att_pT_ready, 1)

            att_softmax(0)
            for hd in range(ATT_HEADS):
                if hd + 1 < ATT_HEADS:
                    att_softmax(hd + 1)
                att_copy(hd)
                if hd == 0:
                    act.wait_ge(gvar_done, 1)
                    act.activation(gsq_, two_banks[0], ACT.Sqrt, bias=GN_EPS).then_inc(gstd_ready, 1)
            act.wait_ge(att_done, ATT_HEADS)
            act.wait_ge(yret_ready, 4)
            act.copy(mixin[:, 4:8, :].rearrange("p c t -> p (c t)"), two_banks[1]).then_inc(yatt_ready, 1)

            for b in range(4):
                name = ("wout", b // 2)
                act.wait_ge(tile_done[ring_plan.slot(name)], ring_plan.done(name))
                act.activation(h[:, 2 * b:2 * b + 2, :].rearrange("p c t -> p (c t)"),
                               two_banks[b // 2][:, 512 * (b % 2):512 * (b % 2 + 1)], ACT.Square).then_inc(sq_ready, 1)
            root(bank[5][:, 0:S], ms_done, 2, std_ready)
            for b in range(4):
                act.wait_ge(x_ready, 4 + 2 * b + 2)
                act.activation(h[:, 2 * b:2 * b + 2, :], x[:, 2 * b:2 * b + 2, :], ACT.Square).then_inc(sq_ready, 1)
            root(bank[5][:, 0:S], ms_done, 3, std_ready)
            for k in range(KD):
                act.wait_ge(scaled_ready, KD + k + 1)
                act.activation(h[:, k, :], h[:, k, :], ACT.Identity, bias=mod[:, 24 + k:25 + k]).then_inc(h_ready, 1)

            act.wait_ge(lmax_ready, 1)
            for t in range(TT):
                ins = act.activation(aff[:, t, :], bank[4][:, E * t:E * (t + 1)], ACT.Exp, bias=lmax[:, t:t + 1],
                                     accum_out=lsum[:, t:t + 1])
            ins.then_inc(lexp_ready, 1)
            for b in range(4):
                act.wait_ge(htokT_done, b + 1)
                act.copy(h_tok[:, b // 2, 512 * (b % 2):512 * (b % 2 + 1)], bank[b]).then_inc(htok_ready, 1)
            for k in range(KD):
                act.wait_ge(xeT_done, k + 1)
                act.copy(xeT[:, k, :], bank[k % 4]).then_inc(xeT_ready, 1)
            for b in range(E // 2):
                act.wait_ge(gT_done, b + 1)
                act.copy(gT_[:, 512 * b:512 * (b + 1)], bank[b % 4]).then_inc(gT_ready, 1)
            act.sem_inc(y_ready, 1)

            with act.Fori(0, E) as e:
                def silu(q):
                    name = ("up", q)
                    act.wait_ge(tile_done[ring_plan.slot(name)], ring_plan.done(name, e))
                    act.activation(silu_gate[:, q % 2, :], bank[q % 2][:, 0:P], ACT.Silu).then_inc(silu_ready, 1)

                def copy_hidden(q):
                    act.wait_ge(hiddenT_done, 4 * e + (q + 1))
                    act.copy(hiddenT[:, q, :], bank[2 + q % 2][:, 0:P]).then_inc(hiddenT_ready, 1)

                silu(0)
                silu(1)
                copy_hidden(0)
                silu(2)
                copy_hidden(1)
                silu(3)
                copy_hidden(2)
                copy_hidden(3)
                name = ("down", FB - 1)
                act.wait_ge(tile_done[ring_plan.slot(name)], ring_plan.done(name, e))
                act.copy(y_part, two_banks[1]).then_inc(y_ready, 1)

            act.wait_ge(moe_done, E)
            for b in range(4):
                act.activation(h[:, 2 * b:2 * b + 2, :], moe_acc[:, 2 * b:2 * b + 2, :], ACT.Square).then_inc(sq_ready, 1)
            root(bank[0][:, 0:S], ms_done, 4, std_ready)
            act.wait_ge(x_moe_ready, KD)
            act.sem_inc(emptied["act"], groups.per["act"])

            with act.Fori(0, LAYERS) as l:
                step = Steps(act, act_layer, 1, l)

                def done(name):
                    act.wait_ge(group_done, groups.done(name, l))
                    return bank[groups.bank(name)]

                def wait_emptied(name):
                    e, n = groups.emptied(name, l)
                    act.wait_ge(emptied[e], n)

                def norm(i, written):
                    for b in range(4):
                        if written:
                            wait_emptied((*written, b))
                        act.activation(h[:, 2 * b:2 * b + 2, :], x[:, 2 * b:2 * b + 2, :], ACT.Square).then_inc(l_sq, 1)
                    act.wait_ge(l_ms, l * 3 + (i + 1))
                    act.activation(std[:], bank[7][:, 0:S], ACT.Sqrt, bias=EPS).then_inc(l_std, 1)

                def ffn(f, i, written):
                    norm(i, written)
                    for j in range(11):
                        src = done(("a", f, j))
                        if j >= 4:
                            wait_emptied(("b", f, j - 4))
                        act.activation(silu_a[:, j % 4, :], src, ACT.Silu).then_inc(emptied["act"], 1)

                act.wait_ge(cols_layer, l + 1)
                ffn(0, 0, None)

                norm(1, ("dn", 0))
                cw, cb = lo["conv_w"], lo["conv_b"]
                for g in range(5):
                    src = done(("lru", g))
                    act.copy(upad[:, 2 * g:2 * g + 2, TAPS - 1:], src.rearrange("p (c t) -> p c t", c=2))
                    for b in range(2):
                        c = 2 * g + b
                        ins = act.activation(v[:, c, :], src[:, S * b:S * (b + 1)], ACT.Identity,
                                             scale=lc[:, cw + 3 * HEADS + c:cw + 3 * HEADS + c + 1],
                                             bias=lc[:, cb + c:cb + c + 1])
                    ins.then_inc(emptied["act"], 1)
                src = done(("gelu", 0))
                act.activation(gel_[:, 0:512], src, ACT.Gelu_apprx_tanh).then_inc(emptied["act"], 1)
                for g in range(2):
                    src = done(("pool", g))
                    act.copy(pool_u[:, 2 * g:2 * g + 2, 16:], src.rearrange("p (c t) -> p c t", c=2)).then_inc(emptied["act"], 1)
                for part, dst, b0 in (("ra", rgate, lo["lru_b_a"]), ("ix", igate, lo["lru_b_x"])):
                    for g in range(5):
                        src = done((part, g))
                        for b in range(2):
                            c = 2 * g + b
                            ins = act.activation(dst[:, c, :], src[:, S * b:S * (b + 1)], ACT.Sigmoid,
                                                 bias=lc[:, b0 + c:b0 + c + 1])
                        ins.then_inc(emptied["act"], 1)
                wait_emptied(("ra", 4))
                for c in range(HEADS):
                    ins = act.activation(decay[:, c, :], rgate[:, c, :], ACT.Exp, scale=lc[:, n_layer + c:n_layer + c + 1])
                step(ins)
                for c in range(HEADS):
                    ins = act.activation(rgate[:, c, :], rgate[:, c, :], ACT.Tanh,
                                         scale=lc[:, n_layer + HEADS + c:n_layer + HEADS + c + 1])
                ins.then_inc(decay_ready, 1)
                for g in range(1, 5):
                    src = done(("gelu", g))
                    act.activation(gel_[:, 512 * g:512 * (g + 1)], src, ACT.Gelu_apprx_tanh).then_inc(emptied["act"], 1)
                act.wait_ge(m2_ready, l + 1)
                act.activation(r_, r_, ACT.Sqrt).then_inc(mult_ready, 1)
                for g in range(8):
                    src = done(("g", g))
                    act.activation(gs_[:, 512 * g:512 * (g + 1)], src, ACT.Sigmoid).then_inc(emptied["act"], 1)

                ffn(1, 2, ("out",))
                for b in range(4):
                    wait_emptied(("dn", 1, b))

            for b in range(4):
                act.activation(h[:, 2 * b:2 * b + 2, :], x[:, 2 * b:2 * b + 2, :], ACT.Square).then_inc(f_sq, 1)
            root(bank[7][:, 0:S], f_ms, 1, f_std)
            for t in range(TT):
                act.wait_ge(outT_done, 2 * t + 1)
                act.copy(out_tok[:, t, 0:512], bank[2 * t]).then_inc(out_ready_act, 1)

        @block.vector
        def _(dve):
            step = Steps(dve, dve_first)
            relf, relint = rel, reli.bitcast(I32)

            dve.wait_ge(rel_ready, 1)
            step(dve.scalar_tensor_tensor(out=dist, in0=relf, scalar=-1.0, in1=relf, op0=ALU.mult, op1=ALU.max))
            step(dve.tensor_scalar(mult_, dist, float(NEAR), None, ALU.is_le))
            for dilation in (4, 16):
                step(dve.tensor_scalar(keep.bitcast(I32), relint, dilation - 1, None, ALU.bitwise_and))
                step(dve.scalar_tensor_tensor(out=mult_, in0=keep.bitcast(I32), scalar=0.0, in1=mult_,
                                              op0=ALU.is_equal, op1=ALU.add))
            step(dve.tensor_scalar(negdist_, mult_, 0.0, NEG, ALU.is_equal, ALU.mult))
            step(dve.tensor_tensor(negdist_, negdist_, dist, ALU.subtract))

            dve.wait_ge(colsT_done, 1)
            step(dve.tensor_copy(first_cols[:], bank[0][:, 0:n_first]))
            for l in range(LAYERS):
                step(dve.tensor_copy(layer_cols[:, n_layer * l:n_layer * (l + 1)],
                                     bank[0][:, P * (1 + l):P * (1 + l) + n_layer]))
            dve.sem_inc(cols_ready, 1)
            for b in range(4):
                dve.wait_ge(xT_done, b + 1)
                dve.tensor_copy(x[:, 2 * b:2 * b + 2, :].rearrange("p c t -> p (c t)"), bank[1 + b]).then_inc(x_ready, 1)

            dve.wait_ge(misc_loaded, 48)
            for l in range(LAYERS):
                at = n_layer * l + lo["lru_lambda"]
                step(dve.tensor_copy(decay_in[:, 8 + HEADS * l:8 + HEADS * (l + 1)], layer_cols[:, at:at + HEADS]))
            dve.scalar_tensor_tensor(out=soft[:, 0, :], in0=decay_in[:], scalar=-1.0, in1=decay_in[:],
                                     op0=ALU.mult, op1=ALU.max).then_inc(softexp_ready, 1)
            dve.wait_ge(softexp_ready, 2)
            step(dve.tensor_scalar(soft[:, 2, :], soft[:, 1, :], 2.0, None, ALU.add))
            step(dve.reciprocal(soft[:, 3, :], soft[:, 2, :]))
            step(dve.tensor_tensor(soft[:, 2, :], soft[:, 1, :], soft[:, 3, :], ALU.mult))
            step(dve.tensor_tensor(soft[:, 3, :], soft[:, 2, :], soft[:, 2, :], ALU.mult))
            step(dve.tensor_scalar(soft[:, 4, :], soft[:, 3, :], 1.0 / 19.0, None, ALU.mult))
            for n in (17, 15, 13, 11, 9, 7, 5, 3):
                step(dve.scalar_tensor_tensor(out=soft[:, 4, :], in0=soft[:, 4, :], scalar=1.0 / n, in1=soft[:, 3, :],
                                              op0=ALU.add, op1=ALU.mult))
            step(dve.scalar_tensor_tensor(out=soft[:, 4, :], in0=soft[:, 4, :], scalar=1.0, in1=soft[:, 2, :],
                                          op0=ALU.add, op1=ALU.mult))
            step(dve.tensor_scalar(soft[:, 5, :], decay_in[:], -1.0, 0.0, ALU.mult, ALU.max))
            step(dve.scalar_tensor_tensor(out=soft[:, 5, :], in0=soft[:, 4, :], scalar=2.0, in1=soft[:, 5, :],
                                          op0=ALU.mult, op1=ALU.add))
            sp = soft[:, 5, :]
            step(dve.tensor_scalar(nsp8[:, 0, :], sp[:, 8:], -LRU_C, None, ALU.mult))
            step(dve.tensor_scalar(nsp8[:, 1, :], sp[:, 8:], LRU_C, None, ALU.mult))
            for hd in range(RET_HEADS):
                step(dve.tensor_scalar(dist, relf, 0.0, sp[:, hd:hd + 1], ALU.max, ALU.mult))
                step(dve.tensor_scalar(dret[:, hd, :], relf, 0.0, sp[:, 4 + hd:5 + hd], ALU.min, ALU.mult))
                dve.tensor_tensor(dret[:, hd, :], dret[:, hd, :], dist, ALU.subtract).then_inc(dret_arg, 1)
                if hd + 1 < RET_HEADS:
                    dve.wait_ge(dret_arg, hd + 1)
            dve.wait_ge(consts_ready, 2)
            for g, w in enumerate(POOL_WINDOWS):
                step(dve.tensor_scalar(pool_fix[:, g, :], pool_fix[:, g, :], float(w), None, ALU.min))
            step(dve.reciprocal(inv_count[:], pool_fix[:]))

            def modulation(i):
                half = mod_bank(i)
                name = ("ada", i)
                dve.wait_ge(tile_done[ring_plan.slot(name)], ring_plan.done(name))
                dve.tensor_copy(modrow[:, i % 2, :], half[:, 0:P]).then_inc(modrow_ready, 1)

            def modulation_columns(i):
                half = mod_bank(i)
                dve.wait_ge(modT_done, i + 1)
                at = fo["b_ada"] + 4 * i
                dve.tensor_tensor(mod[:, 4 * i:4 * i + 4], half[:, P:2 * P:32], first_cols[:, at:at + 4],
                                  ALU.add).then_inc(mod_ready, 1)

            def inverse_root(ready, n):
                dve.wait_ge(ready, n)
                step(dve.reciprocal(rstd[:], std[:]))

            inverse_root(std_ready, 1)
            for i in range(4):
                modulation(i)
                modulation_columns(i)
            dve.wait_ge(mod_ready, 4)
            step(dve.scalar_tensor_tensor(out=gains[:, 0, :], in0=mod[:, 8:16], scalar=1.0,
                                          in1=first_cols[:, fo["g_pre_mix"]:fo["g_pre_mix"] + KD], op0=ALU.add, op1=ALU.mult))
            dve.wait_ge(x_ready, 4)
            for k in range(KD):
                dve.scalar_tensor_tensor(out=h[:, k, :], in0=x[:, k, :], scalar=gains[:, 0, k:k + 1], in1=rstd[:],
                                         op0=ALU.mult, op1=ALU.mult).then_inc(scaled_ready, 1)

            dve.wait_ge(dret_ready, RET_HEADS)
            for hd in range(RET_HEADS):
                dve.wait_ge(ret_scored, hd + 1)
                if hd >= 2:
                    dve.wait_ge(ret_done, hd - 1)
                dve.tensor_tensor(pret[:, hd % 2].rearrange("p s t -> p (s t)"), bank[4 + hd % 2], dret[:, hd, :],
                                  ALU.mult).then_inc(pret_ready, 1)

            def att_scores(hd):
                dve.wait_ge(att_scored, hd + 1)
                sc = s_att[:, hd % 2].rearrange("p t s -> p (t s)")
                step(dve.scalar_tensor_tensor(out=sc, in0=negdist_, scalar=2.0 ** -(hd + 1), in1=bank[4 + hd % 2],
                                              op0=ALU.mult, op1=ALU.add))
                dve.tensor_reduce(att_max[:, hd % 2, :], s_att[:, hd % 2], AX.X, ALU.max,
                                  negate=True).then_inc(att_max_ready, 1)

            def att_weights(hd):
                dve.wait_ge(att_exp, hd + 1)
                if hd >= 2:
                    dve.wait_ge(att_pT_done, hd - 1)
                for t in range(TT):
                    step(dve.tensor_tensor_reduce(p_att[:, hd % 2, t, :], s_att[:, hd % 2, t, :], mult_[:, S * t:S * (t + 1)],
                                                  1.0, 0.0, ALU.mult, ALU.add, att_sum[:, hd % 2, t:t + 1]))
                step(dve.reciprocal(att_inv[:, hd % 2, :], att_sum[:, hd % 2, :]))
                for t in range(TT):
                    ins = dve.tensor_scalar(p_att[:, hd % 2, t, :], p_att[:, hd % 2, t, :], att_inv[:, hd % 2, t:t + 1],
                                            None, ALU.mult)
                ins.then_inc(att_p_ready, 1)

            att_scores(0)
            dve.wait_ge(gmean_done, 1)
            for b in range(2):
                dve.wait_ge(ret_copied, b + 1)
                dve.tensor_tensor(gn_[:, 512 * b:512 * (b + 1)], gn_[:, 512 * b:512 * (b + 1)],
                                  two_banks[1][:, 512 * b:512 * (b + 1)], ALU.subtract).then_inc(centred_ready, 1)
            att_scores(1)
            for hd in range(ATT_HEADS):
                att_weights(hd)
                if hd + 2 < ATT_HEADS:
                    att_scores(hd + 2)
                modulation(4 + hd)
                modulation_columns(4 + hd)
                if hd == 1:
                    dve.wait_ge(gstd_ready, 1)
                    step(dve.reciprocal(pret_, gsq_))
                    step(dve.tensor_tensor(pret_, pret_, gn_, ALU.mult))
                    for c in range(4):
                        dve.tensor_tensor(mixin[:, c, :], pret_[:, S * c:S * (c + 1)], rg[:, c, :], ALU.mult).then_inc(yret_ready, 1)
            dve.wait_ge(mod_ready, 12)
            for i, at, name, plus in ((1, 16, "g_post_mix", 0.0), (2, 32, "g_pre_ffn", 1.0), (3, 40, "g_post_ffn", 0.0)):
                step(dve.scalar_tensor_tensor(out=gains[:, i, :], in0=mod[:, at:at + KD], scalar=plus,
                                              in1=first_cols[:, fo[name]:fo[name] + KD], op0=ALU.add, op1=ALU.mult))

            inverse_root(std_ready, 2)
            for k in range(KD):
                src = two_banks[k // 4][:, S * (k % 4):S * (k % 4 + 1)]
                step(dve.scalar_tensor_tensor(out=mix[:, k, :], in0=src, scalar=gains[:, 1, k:k + 1], in1=rstd[:],
                                              op0=ALU.mult, op1=ALU.mult))
                dve.tensor_tensor(x[:, k, :], x[:, k, :], mix[:, k, :], ALU.add).then_inc(x_ready, 1)
            inverse_root(std_ready, 3)
            dve.wait_ge(x_ready, 4 + KD)
            for k in range(KD):
                dve.scalar_tensor_tensor(out=h[:, k, :], in0=x[:, k, :], scalar=gains[:, 2, k:k + 1], in1=rstd[:],
                                         op0=ALU.mult, op1=ALU.mult).then_inc(scaled_ready, 1)

            step(dve.memset(ones_e, 1.0))
            step(dve.memset(zeros, 0.0))
            dve.wait_ge(logits_done, 1)
            dve.tensor_reduce(lmax, bank[4][:, 0:TT * E].rearrange("p (t e) -> p t e", t=TT), AX.X, ALU.max,
                              negate=True).then_inc(lmax_ready, 1)
            dve.wait_ge(lexp_ready, 1)
            step(dve.reciprocal(linv, lsum))
            for t in range(TT):
                ins = dve.tensor_scalar(aff[:, t, :], aff[:, t, :], linv[:, t:t + 1], None, ALU.mult)
            ins.then_inc(aff_ready, 1)
            dve.wait_ge(affT_done, 1)
            step(dve.tensor_copy(affT, bank[5][0:E, 0:S]))
            now, then = affT, affW
            for r in range(CAP // 8):
                best = top[:, 8 * r:8 * r + 8]
                step(dve.max(best, now))
                step(dve.max_index(topi[:, 8 * r:8 * r + 8], best, now))
                if r + 1 < CAP // 8:
                    step(dve.match_replace(then, best, now, -1.0))
                    now, then = then, now
            step(dve.tensor_copy(topf, topi))
            dve.tensor_tensor(spread, ident[0:E, 0:E].unsqueeze(2).broadcast_to([E, E, CAP]),
                              topf.unsqueeze(1).broadcast_to([E, E, CAP]), ALU.mult).then_inc(spread_ready, 1)
            dve.wait_ge(index_done, 1)
            for t in range(TT):
                ins = dve.tensor_scalar(onehot[:, t, :], bank[6], t_col[:, t:t + 1], None, ALU.is_equal)
            ins.then_inc(onehot_ready, 1)
            dve.wait_ge(onehot_ready, 1)
            dve.wait_ge(aff_ready, 1)
            for half in range(2):
                if half:
                    dve.wait_ge(xeT_done, KD)
                for t in range(TT):
                    cols = onehot[:, t, 256 * half:256 * (half + 1)].rearrange("p (e c) -> p e c", c=CAP)
                    ins = dve.tensor_tensor(
                        weighted[half][:, t].rearrange("p e (g c) -> p e g c", g=4),
                        cols.unsqueeze(2).broadcast_to([P, 8, 4, CAP]),
                        aff[:, t, 8 * half:8 * (half + 1)].unsqueeze(2).unsqueeze(3).broadcast_to([P, 8, 4, CAP]), ALU.mult)
                ins.then_inc(weighted_ready, 1)
            dve.sem_inc(hidden_ready, 2)
            dve.wait_ge(xeT_ready, KD)

            with dve.Fori(0, E) as e:
                name = ("up", FB - 1)
                s = ring_plan.slot(name)
                dve.wait_ge(tile_done[s], ring_plan.done(name, e) - ring_plan.per["expert"][1][s])
                dve.tensor_copy(xe, xeT[:, :, bass.ds(e * CAP, CAP)]).then_inc(xe_ready, 1)
                for q in range(FB):
                    dve.wait_ge(silu_ready, 4 * e + (q + 1))
                    dve.tensor_tensor(hidden[:, q % 2, :], silu_gate[:, q % 2, :], bank[q % 2][:, P:2 * P],
                                      ALU.mult).then_inc(hidden_ready, 1)

            inverse_root(std_ready, 4)
            for k in range(KD):
                step(dve.scalar_tensor_tensor(out=y_part[:, 0:S] if k % 2 else y_part[:, S:2 * S], in0=moe_acc[:, k, :],
                                              scalar=gains[:, 3, k:k + 1], in1=rstd[:], op0=ALU.mult, op1=ALU.mult))
                dve.tensor_tensor(x[:, k, :], x[:, k, :], y_part[:, 0:S] if k % 2 else y_part[:, S:2 * S],
                                  ALU.add).then_inc(x_moe_ready, 1)
            dve.wait_ge(x_moe_ready, KD)
            dve.sem_inc(emptied["dve"], groups.per["dve"])

            with dve.Fori(0, LAYERS) as l:
                step = Steps(dve, dve_layer, 20, l)

                def done(name):
                    dve.wait_ge(group_done, groups.done(name, l))
                    return bank[groups.bank(name)]

                def wait_emptied(name):
                    e, n = groups.emptied(name, l)
                    dve.wait_ge(emptied[e], n)

                def norm(i, at):
                    dve.wait_ge(l_std, l * 3 + (i + 1))
                    step(dve.reciprocal(rstd[:], std[:]))
                    for k in range(KD):
                        dve.scalar_tensor_tensor(out=h[:, k, :], in0=x[:, k, :], scalar=lc[:, at + k:at + k + 1],
                                                 in1=rstd[:], op0=ALU.mult, op1=ALU.mult).then_inc(l_h, 1)

                def ffn(f, i, at):
                    norm(i, at)
                    for j in range(11):
                        src = done(("b", f, j))
                        wait_emptied(("a", f, j))
                        dve.tensor_tensor(u_[:, 512 * j:512 * (j + 1)], src, silu_a[:, j % 4, :],
                                          ALU.mult).then_inc(emptied["dve"], 1)
                    for q in range(4):
                        src = done(("dn", f, q))
                        xs = x[:, 2 * q:2 * q + 2, :].rearrange("p c t -> p (c t)")
                        dve.scalar_tensor_tensor(out=xs, in0=src, scalar=0.5, in1=xs, op0=ALU.mult,
                                                 op1=ALU.add).then_inc(emptied["dve"], 1)
                    for q in range(4):
                        wait_emptied(("dn", f, q))

                step(dve.tensor_copy(lc[:, 0:n_layer], layer_cols[:, bass.ds(l * n_layer, n_layer)]))
                step(dve.tensor_copy(lc[:, n_layer:n_layer + HEADS], nsp8[:, 0, bass.ds(l * HEADS, HEADS)]))
                dve.tensor_copy(lc[:, n_layer + HEADS:], nsp8[:, 1, bass.ds(l * HEADS, HEADS)]).then_inc(cols_layer, 1)
                dve.wait_ge(cols_layer, l + 1)
                ffn(0, 0, lo["norm_ffn1"])

                norm(1, lo["norm_mix"])
                cw = lo["conv_w"]
                for g in range(5):
                    wait_emptied(("lru", g))
                    for k in range(TAPS - 1):
                        for c in (2 * g, 2 * g + 1):
                            ins = dve.scalar_tensor_tensor(
                                out=v[:, c, :], in0=upad[:, c, k:k + S], scalar=lc[:, cw + HEADS * k + c:cw + HEADS * k + c + 1],
                                in1=v[:, c, :], op0=ALU.mult, op1=ALU.add)
                        if k < TAPS - 2:
                            step(ins)
                    ins.then_inc(v_ready, 1)
                dve.wait_ge(pool_sums, l + 1)
                sums = (pool_a, pool_b, pool_a, pool_b)
                for g, w in enumerate(POOL_WINDOWS):
                    dve.tensor_tensor(pool_fix[:, g, :], sums[g][:, g, 16:32], inv_count[:, g, :], ALU.mult)
                    ins = dve.scalar_tensor_tensor(out=pooled[:, g, :], in0=sums[g][:, g, 16:], scalar=1.0 / w,
                                                   in1=pool_u[:, g, 16:], op0=ALU.mult, op1=ALU.subtract)
                step(ins)
                dve.tensor_tensor(pooled[:, :, 0:16], pool_fix[:], pool_u[:, :, 16:32], ALU.subtract).then_inc(pooled_ready, 1)
                for g in range(2):
                    src = done(("pmix", g))
                    for b in range(2):
                        c = 2 * g + b
                        ins = dve.tensor_scalar(pool_mix[:, c, :], src[:, S * b:S * (b + 1)],
                                                lc[:, lo["pool_b"] + c:lo["pool_b"] + c + 1],
                                                lc[:, lo["pool_scale"] + c:lo["pool_scale"] + c + 1], ALU.add, ALU.mult)
                    ins.then_inc(emptied["dve"], 1)
                dve.wait_ge(decay_ready, l + 1)
                a2 = upad[:, :, TAPS - 1:]
                step(dve.tensor_tensor(a2, decay, decay, ALU.mult))
                dve.scalar_tensor_tensor(out=rgate, in0=a2, scalar=1.0, in1=rgate, op0=ALU.add,
                                         op1=ALU.mult).then_inc(m2_ready, 1)
                step(dve.memset(decay[:, :, 0:1], 0.0))
                dve.wait_ge(mult_ready, l + 1)
                dve.wait_ge(iv_ready, l + 1)
                step(dve.tensor_tensor(i_, i_, r_, ALU.mult))
                step(dve.tensor_tensor_scan(v_, a_, i_, 0.0, ALU.mult, ALU.add))
                wait_emptied(("gelu", 4))
                dve.tensor_tensor(gel_, gel_, v_, ALU.mult).then_inc(lru_ready, 1)
                for q in range(4):
                    src = done(("pup", q))
                    wait_emptied(("g", q))
                    gq = gs_[:, 512 * q:512 * (q + 1)]
                    dve.tensor_tensor(gq, src, gq, ALU.mult).then_inc(emptied["dve"], 1)
                for q in range(4):
                    src = done(("lup", q))
                    wait_emptied(("g", 4 + q))
                    gq, zq = gs_[:, 512 * q:512 * (q + 1)], gs_[:, 512 * (4 + q):512 * (5 + q)]
                    dve.tensor_tensor(zq, src, zq, ALU.mult).then_inc(emptied["dve"], 1)
                    wait_emptied(("lup", q))
                    dve.tensor_tensor(zq, zq, gq, ALU.add).then_inc(z_ready, 1)
                for q in range(4):
                    src = done(("out", q))
                    xs = x[:, 2 * q:2 * q + 2, :].rearrange("p c t -> p (c t)")
                    dve.tensor_tensor(xs, src, xs, ALU.add).then_inc(emptied["dve"], 1)
                for q in range(4):
                    wait_emptied(("out", q))

                ffn(1, 2, lo["norm_ffn2"])
                assert step.n == step.per

            step = Steps(dve, dve_final)
            dve.wait_ge(f_std, 1)
            step(dve.reciprocal(rstd[:], std[:]))
            at = fo["final_norm"]
            for k in range(KD):
                dve.scalar_tensor_tensor(out=h[:, k, :], in0=x[:, k, :], scalar=first_cols[:, at + k:at + k + 1],
                                         in1=rstd[:], op0=ALU.mult, op1=ALU.mult).then_inc(f_h, 1)
            for t in range(TT):
                dve.wait_ge(outT_done, 2 * t + 2)
                dve.tensor_copy(out_tok[:, t, 512:1024], bank[2 * t + 1]).then_inc(out_ready_dve, 1)


_INS = [(n, n) for n in ("x", "c", "w_ada", "b_ada", "g_pre_mix", "g_post_mix", "g_pre_ffn", "g_post_ffn", "w_in",
                         "ret_decay_fwd", "ret_decay_bwd", "w_out", "w_router", "w_gate_e", "w_up_e", "w_down_e")]
_INS += [(n, n if n in ("w_in_2", "w_out_2") else n[:-2]) for n in (
    "norm_ffn1_2", "ffn1_w_up_2", "ffn1_w_down_2", "norm_mix_2", "w_in_2", "pool_w_2", "pool_b_2", "pool_scale_2",
    "w_pool_up_2", "conv_w_2", "conv_b_2", "lru_w_a_2", "lru_b_a_2", "lru_w_x_2", "lru_b_x_2", "lru_lambda_2",
    "w_lru_up_2", "w_out_2", "norm_ffn2_2", "ffn2_w_up_2", "ffn2_w_down_2", "final_norm_2")]


def kernel(**inputs):
    import numpy as _np
    import concourse.bacc as _bacc
    from concourse import mybir as _mybir
    from concourse.bass_utils import run_bass_kernel_spmd as _run

    nc = _bacc.Bacc("TRN2", target_bir_lowering=False, num_devices=1)
    arrays, args = {}, {}
    for name, own in _INS:
        arr = _np.ascontiguousarray(inputs[name])
        arrays[f"in_{name}_dram"] = arr
        args[own] = nc.dram_tensor(f"in_{name}_dram", arr.shape, _mybir.dt.from_np(arr.dtype), kind="ExternalInput").ap()
    out = nc.dram_tensor("out_0_dram", (1, S, D), F32, kind="ExternalOutput").ap()
    block_kernel(nc, args, out)
    r = _run(nc, [arrays], core_ids=[0])
    return r.results[0]["out_0_dram"]
```

```python
from contextlib import ExitStack

import numpy as np
import concourse.bass as bass
from concourse import mybir

F32 = mybir.dt.float32
F32R = mybir.dt.float32r
BF16 = mybir.dt.bfloat16
I32 = mybir.dt.int32
U32 = mybir.dt.uint32
ALU = mybir.AluOpType
ACT = mybir.ActivationFunctionType
AX = mybir.AxisListType

P = 128
D = 1024
S = 256
KD = D // P
TT = S // P
EPS = 1e-6
GN_EPS = 1e-5

RET_HEADS, RET_QK = 4, 64
ATT_HEADS, ATT_DIM = 8, 64
QK_SCALE = 0.125
NEAR = 64
NEG = -1e30

E, CAP, FF = 16, 32, 2048
FB = FF // 512
LAYERS = 2
FFN = 2816
FK = FFN // P
HEADS = 10
POOLS = 4
POOL_WINDOWS = (2, 4, 8, 16)
TAPS = 4
LRU_C = 8.0

SLOTS = 6
SLOT = 4096
LAYER_SLOTS = 4
HI_SLOTS = SLOTS - LAYER_SLOTS
BANKS = 6


class Ring:

    def __init__(self, first, expert, layer):
        self.at = {}
        loads, uses = [0] * SLOTS, [0] * SLOTS
        self.per = {}
        for phase, tiles, turns, slots in (("first", first, 1, SLOTS), ("expert", expert, E, SLOTS),
                                           ("layer", layer, LAYERS, LAYER_SLOTS)):
            assert len(tiles) % slots == 0
            own_loads, own_uses = [0] * SLOTS, [0] * SLOTS
            for i, tile in enumerate(tiles):
                if tile is None:
                    continue
                name, dmas = tile
                s = i % slots
                own_loads[s] += dmas
                self.at[name] = (phase, s, loads[s] + own_loads[s], uses[s] + own_uses[s])
                own_uses[s] += 1
            self.per[phase] = (own_loads, own_uses)
            loads = [a + turns * b for a, b in zip(loads, own_loads)]
            uses = [a + turns * b for a, b in zip(uses, own_uses)]
            if phase == "expert":
                self.end_of_experts = uses

    def slot(self, name):
        return self.at[name][1]

    def loaded(self, name, turn=0):
        phase, s, loads, _ = self.at[name]
        return turn * (16 * self.per[phase][0][s]) + 16 * loads

    def before(self, name, turn=0):
        phase, s, _, uses = self.at[name]
        return turn * self.per[phase][1][s] + uses

    def done(self, name, turn=0):
        phase, s, _, uses = self.at[name]
        return turn * self.per[phase][1][s] + uses + 1


def first_tiles():
    ada = [(("ada", i), 1) for i in range(12)]
    win = [(("win", i), 1) for i in range(6)]
    wout = [(("wout", i), 1) for i in range(2)]
    return ada[:4] + win + ada[4:] + wout + [None] * 4


def expert_tiles():
    pairs = [((kind, q), 1) for q in range(FB) for kind in ("gate", "up")]
    return pairs + [(("down", k), 1) for k in range(FB)]


def layer_tiles():
    def ffn(f):
        up = [((kind, f, j), 1, 2) for j in range(5) for kind in ("upa", "upb")]
        return up + [(("upab", f), 2, 2)] + [(("dn", f, c), 1, 1) for c in range(KD)]

    mixer = [(("proj", i), 1, 2) for i in (1, 2, 3, 0)] + [("small", 3, 0)] + [(("proj", i), 1, 2) for i in range(4, 10)]
    mixer += [("pup", 1, 0)] + [(("lup", i), 1, 1) for i in range(4)] + [(("lout", i), 1, 2) for i in range(2)]
    return ffn(0) + mixer + ffn(1)


def last_groups():
    last = {}
    for f in range(2):
        for j in range(5):
            last[("upa", f, j)] = ("a", f, 2 * j + 1)
            last[("upb", f, j)] = ("b", f, 2 * j + 1)
        last[("upab", f)] = ("b", f, 10)
        for c in range(KD):
            last[("dn", f, c)] = ("dn", f, c)
    last |= {("proj", 1): ("lru", 1), ("proj", 2): ("lru", 3), ("proj", 3): ("gelu", 0), ("proj", 0): ("pool", 1),
             "small": ("pmix", 1), ("proj", 4): ("gelu", 2), ("proj", 5): ("gelu", 4), "pup": ("pup", 3)}
    last |= {("proj", 6 + i): ("g", 2 * i + 1) for i in range(4)}
    last |= {("lup", i): ("lup", 2 * i + 1) for i in range(4)}
    return last | {("lout", 0): ("out", 1), ("lout", 1): ("out", 3)}


def layer_groups():
    def ffn(f):
        g = []
        for j in range(5):
            g += [(("a", f, 2 * j), "act"), (("a", f, 2 * j + 1), "act")]
            g += [(("b", f, 2 * j), "dve"), (("b", f, 2 * j + 1), "dve")]
        return g + [(("a", f, 10), "act"), (("b", f, 10), "dve")] + [(("dn", f, c), "dve") for c in range(KD)]

    mixer = [(("lru", g), "act") for g in range(5)] + [(("gelu", 0), "act")]
    mixer += [(("pool", g), "act") for g in range(2)]
    mixer += [(("ra", g), "act") for g in range(5)] + [(("ix", g), "act") for g in range(5)]
    mixer += [(("pmix", g), "dve") for g in range(2)] + [(("gelu", g), "act") for g in range(1, 5)]
    mixer += [(("g", g), "act") for g in range(8)]
    mixer += [(("pup", g), "dve") for g in range(4)] + [(("lup", g), "dve") for g in range(8)]
    mixer += [(("out", g), "dve") for g in range(4)]
    return ffn(0) + mixer + ffn(1)


class Groups:

    def __init__(self, groups):
        self.n = {name: i for i, (name, _) in enumerate(groups)}
        self.engine = [e for _, e in groups]
        self.total = len(groups)
        assert self.total % BANKS == 0
        self.per = {e: self.engine.count(e) for e in ("act", "dve")}

    def bank(self, name):
        return self.n[name] % BANKS

    def done(self, name, layer):
        return layer * self.total + (self.total + self.n[name] + 1)

    def emptied(self, name, layer):
        n = self.n[name]
        e = self.engine[n]
        return e, layer * self.per[e] + (self.per[e] + self.engine[:n + 1].count(e))

    def bank_free(self, name, layer):
        n = self.n[name] - BANKS
        if n >= 0:
            e = self.engine[n]
            return e, layer * self.per[e] + (self.per[e] + self.engine[:n + 1].count(e))
        e = self.engine[n + self.total]
        return e, layer * self.per[e] + self.engine[:n + self.total + 1].count(e)


class Splits:

    def __init__(self, tiles):
        self.tiles = [(name, units) for name, _, units in tiles if units]
        self.at, n = {}, 0
        for i, (name, units) in enumerate(self.tiles):
            self.at[name] = (i, n)
            n += units
        self.total = n
        assert len(self.tiles) % HI_SLOTS == 0

    def hi_slot(self, name):
        return self.at[name][0] % HI_SLOTS

    def ready(self, name, unit, layer):
        return layer * self.total + (self.at[name][1] + unit + 1)

    def before(self, name):
        i = self.at[name][0] - HI_SLOTS
        return self.tiles[i][0], i < 0


class Steps:

    def __init__(self, eng, sem, per=0, turn=0):
        self.eng, self.sem, self.per, self.turn, self.n = eng, sem, per, turn, 0

    def __call__(self, instruction):
        self.n += 1
        instruction.then_inc(self.sem, 1)
        if self.per:
            self.eng.wait_ge(self.sem, self.turn * self.per + self.n)
        else:
            self.eng.wait_ge(self.sem, self.n)


FIRST_ROWS = (("c", 8), ("b_ada", 48), ("g_pre_mix", 8), ("g_post_mix", 8), ("g_pre_ffn", 8),
              ("g_post_ffn", 8), ("final_norm", 8))
LAYER_ROWS = (("norm_ffn1", 8), ("norm_mix", 8), ("norm_ffn2", 8), ("conv_w", 40), ("conv_b", 10),
              ("lru_b_a", 10), ("lru_b_x", 10), ("lru_lambda", 10), ("pool_b", 4), ("pool_scale", 4))


def offsets(rows):
    at, out = 0, {}
    for name, n in rows:
        out[name] = at
        at += n
    return out, at


def block_kernel(nc, a, out):
    ring_plan = Ring(first_tiles(), expert_tiles(), [tile[:2] for tile in layer_tiles()])
    splits, last_group = Splits(layer_tiles()), last_groups()
    groups = Groups(layer_groups())
    fo, n_first = offsets(FIRST_ROWS)
    lo, n_layer = offsets(LAYER_ROWS)

    ctx = ExitStack()
    with ctx:
        def sb(name, shape, dt=F32):
            return ctx.enter_context(nc.sbuf_tensor(name, shape, dt))

        def sem(name):
            return ctx.enter_context(nc.semaphore(name))

        WORK = 17664
        with nc.sbuf_tensor("ring", [P, SLOTS, SLOT], F32) as ring, nc.sbuf_tensor("h", [P, KD, S], F32) as h, \
                nc.sbuf_tensor("work", [P, WORK], F32) as work:
            pass
        ring_r, h_lo, work_r = (sb("ring_r", [P, SLOTS, SLOT], F32R), sb("h_lo", [P, KD, S], F32R),
                                sb("work_r", [P, WORK], F32R))
        h_hi = sb("h_hi", [P, KD, S], F32R)
        x = sb("x", [P, KD, S])
        std = sb("std", [P, S])
        rstd = sb("rstd", [P, S])
        ident = sb("ident", [P, P])
        mean_d = sb("mean_d", [P, P])
        mean_v = sb("mean_v", [P, P])
        first_cols = sb("first_cols", [P, n_first])
        layer_cols = sb("layer_cols", [P, LAYERS * n_layer])
        lc = sb("lc", [P, n_layer + 2 * HEADS])
        decay_in = sb("decay_in", [P, 8 + LAYERS * HEADS])
        soft = sb("soft", [P, 6, 8 + LAYERS * HEADS])
        nsp8 = sb("nsp8", [P, 2, LAYERS * HEADS])
        mod = sb("mod", [P, 48])
        gains = sb("gains", [P, 4, KD])
        inv_count = sb("inv_count", [P, POOLS, 16])
        pool_fix = sb("pool_fix", [P, POOLS, 16])
        pool_u = sb("pool_u", [P, POOLS, 16 + S])
        def carve(sizes):
            at, parts = 0, []
            for n in sizes:
                parts.append(work[:, at:at + n])
                at += n
            assert at <= WORK, at
            return parts

        (x_tok_, rqk_, rv_, rg_, aq_, ak_, av_, dret_, negdist_, mult_, pret_, s_, p_, patt_, gn_, gsq_,
         modrow_, sc_, wr_, small_) = carve(
            (2048, 1024, 1024, 1024, 1024, 1024, 1024, 2048, 512, 512, 1024, 1024, 1024, 512, 1024, 1024,
             256, 256, 128, 64))
        x_tok = x_tok_.rearrange("p (t d) -> p t d", t=TT)
        rows_in = gn_.rearrange("p (n r) -> p n r", r=P)
        rqk = rqk_.rearrange("p (c t) -> p c t", c=4)
        rv = rv_.rearrange("p (t v) -> p t v", t=TT)
        rg = rg_.rearrange("p (c t) -> p c t", c=4)
        aq = aq_.rearrange("p (c t) -> p c t", c=4)
        ak = ak_.rearrange("p (c t) -> p c t", c=4)
        av = av_.rearrange("p (t v) -> p t v", t=TT)
        dret = dret_.rearrange("p (h n) -> p h n", h=RET_HEADS)
        pret = pret_.rearrange("p (b s t) -> p b s t", b=2, s=TT)
        s_att = s_.rearrange("p (b t s) -> p b t s", b=2, t=TT)
        p_att = p_.rearrange("p (b t s) -> p b t s", b=2, t=TT)
        pT_att = patt_.rearrange("p (s t) -> p s t", s=TT)
        mixin = x_tok_.rearrange("p (c t) -> p c t", c=KD)
        gn = gn_.rearrange("p (c t) -> p c t", c=4)
        gsq = gsq_.rearrange("p (c t) -> p c t", c=4)
        modrow = modrow_.rearrange("p (b n) -> p b n", b=2)
        silu_c = sc_.rearrange("p (k m) -> p k m", k=KD)
        w_router = wr_.rearrange("p (k e) -> p k e", k=KD)
        att_max = small_[:, 0:4].rearrange("p (b t) -> p b t", b=2)
        att_sum = small_[:, 4:8].rearrange("p (b t) -> p b t", b=2)
        att_inv = small_[:, 8:12].rearrange("p (b t) -> p b t", b=2)
        mix = work[:, 2048:4096].rearrange("p (c t) -> p c t", c=KD)
        rel = p_[:, 0:512]
        dist = p_[:, 512:1024]
        keep = s_[:, 0:512]
        reli = s_[:, 512:1024]
        (xeT_, gT_, h_tok_, onehot_, weighted_, xe_, sg_, hg_, hT_, yp_, route_, zeros_) = carve(
            (KD * E * CAP, E * S, TT * D, TT * E * CAP, TT * E // 2 * P, KD * CAP, 256, 256, FB * P, D, 1024, 256))
        xeT = xeT_.rearrange("p (k n) -> p k n", k=KD)
        h_tok = h_tok_.rearrange("p (t d) -> p t d", t=TT)
        onehot = onehot_.rearrange("p (t n) -> p t n", t=TT)
        weighted = [part.rearrange("p (t e n) -> p t e n", t=TT, n=P) for part in (weighted_, h_tok_)]
        xe = xe_.rearrange("p (k n) -> p k n", k=KD)
        silu_gate = sg_.rearrange("p (b n) -> p b n", b=2)
        hidden = hg_.rearrange("p (b n) -> p b n", b=2)
        hiddenT = hT_.rearrange("p (q n) -> p q n", q=FB)
        y_part = yp_
        zeros = zeros_.bitcast(BF16)
        (u_, sa_, _) = carve((FK * S, 4 * 512, FK * S))
        u_lo, u_hi = work_r[:, 0:FK * S], work_r[:, FK * S + 4 * 512:2 * FK * S + 4 * 512]
        silu_a = sa_.rearrange("p (b n) -> p b n", b=4)
        (v_, i_, a_, r_, gel_, gs_) = carve((HEADS * S,) * 2 + (HEADS * (S + TAPS - 1),) + (HEADS * S,) * 2 + (16 * S,))
        v = v_.rearrange("p (c t) -> p c t", c=HEADS)
        igate = i_.rearrange("p (c t) -> p c t", c=HEADS)
        upad = a_.rearrange("p (c t) -> p c t", c=HEADS)
        decay_ = a_[:, 0:HEADS * S]
        decay = decay_.rearrange("p (c t) -> p c t", c=HEADS)
        rgate = r_.rearrange("p (c t) -> p c t", c=HEADS)
        gs = gs_.rearrange("p (c t) -> p c t", c=16)
        gel_at = 4 * HEADS * S + HEADS * (TAPS - 1)
        gel_hi, gel_lo = work_r[:, 2 * HEADS * S:3 * HEADS * S], work_r[:, gel_at:gel_at + HEADS * S]
        gs_at = gel_at + HEADS * S
        z_hi, z_lo = work_r[:, gs_at:gs_at + 8 * S], work_r[:, gs_at + 8 * S:gs_at + 16 * S]
        pool_a = gs_[:, 0:1088].rearrange("p (g t) -> p g t", g=POOLS)
        pool_b = gs_[:, 1088:2176].rearrange("p (g t) -> p g t", g=POOLS)
        pooled = gs_[:, 2176:3200].rearrange("p (g t) -> p g t", g=POOLS)
        decay_sq = gs_[:, 1536:1536 + HEADS * S]
        pool_mix = sb("pool_mix", [P, POOLS, S])
        routing = sb("routing", [P, 64 + 2 * E])
        t_col = routing[:, 0:2]
        lsum = routing[:, 2:4]
        lmax = routing[:, 4:6]
        linv = routing[:, 6:8]
        aff = routing[:, 64:64 + 2 * E].rearrange("p (t e) -> p t e", t=TT)
        affT = route_[0:E, 0:256]
        affW = route_[0:E, 256:512]
        top = route_[0:E, 512:544]
        topi = route_[0:E, 544:576].bitcast(U32)
        topf = route_[0:E, 576:608]
        spread = yp_[0:E, 0:512].rearrange("p (e c) -> p e c", e=E)
        ones_e = hT_[0:E, 0:P]
        out_tok = work[:, 0:2048].rearrange("p (t d) -> p t d", t=TT)

        psum = ctx.enter_context(nc.psum_tensor("psum", [P, 8 * 512], F32))
        bank = [psum[:, 512 * b:512 * (b + 1)] for b in range(8)]
        two_banks = [psum[:, 1024 * b:1024 * (b + 1)] for b in range(4)]
        moe_acc = psum[:, 2048:4096].rearrange("p (c t) -> p c t", c=KD)

        def mod_bank(i):
            return bank[6 + i % 2] if i < 4 else bank[7]

        loaded = [sem(f"loaded{s}") for s in range(SLOTS)]
        tile_done = [sem(f"tile_done{s}") for s in range(SLOTS)]
        slot_granted = sem("slot_granted")
        x_loaded, rows_loaded, misc_loaded = sem("x_loaded"), sem("rows_loaded"), sem("misc_loaded")
        ident_ready, consts_ready, rel_ready = sem("ident_ready"), sem("consts_ready"), sem("rel_ready")
        colsT_done, cols_ready = sem("colsT_done"), sem("cols_ready")
        xT_done, x_ready, sq_ready, ms_done = sem("xT_done"), sem("x_ready"), sem("sq_ready"), sem("ms_done")
        std_ready, scaled_ready, h_ready = sem("std_ready"), sem("scaled_ready"), sem("h_ready")
        silu_c_ready, modrow_ready, modT_done, mod_ready = (
            sem("silu_c_ready"), sem("modrow_ready"), sem("modT_done"), sem("mod_ready"))
        softexp_ready, soft_ready = sem("softexp_ready"), sem("soft_ready")
        dret_arg, dret_ready, masks_ready = sem("dret_arg"), sem("dret_ready"), sem("masks_ready")
        proj_ready = sem("proj_ready")
        ret_scored, pret_ready, ret_done, ret_copied = (
            sem("ret_scored"), sem("pret_ready"), sem("ret_done"), sem("ret_copied"))
        gmean_done, centred_ready, gsq_ready, gvar_done, gstd_ready, yret_ready = (
            sem("gmean_done"), sem("centred_ready"), sem("gsq_ready"), sem("gvar_done"), sem("gstd_ready"),
            sem("yret_ready"))
        att_scored, att_max_ready, att_exp, att_p_ready, att_pT_done, att_pT_ready, att_done, yatt_ready = (
            sem("att_scored"), sem("att_max_ready"), sem("att_exp"), sem("att_p_ready"), sem("att_pT_done"),
            sem("att_pT_ready"), sem("att_done"), sem("yatt_ready"))
        mix_ready = sem("mix_ready")
        htokT_done, htok_ready, logits_done, lmax_ready, lexp_ready, aff_ready = (
            sem("htokT_done"), sem("htok_ready"), sem("logits_done"), sem("lmax_ready"), sem("lexp_ready"),
            sem("aff_ready"))
        affT_done, spread_ready, index_done, onehot_ready, weighted_ready = (
            sem("affT_done"), sem("spread_ready"), sem("index_done"), sem("onehot_ready"), sem("weighted_ready"))
        xeT_done, xeT_ready, gT_done, gT_ready = sem("xeT_done"), sem("xeT_ready"), sem("gT_done"), sem("gT_ready")
        xe_ready, silu_ready, hidden_ready, hiddenT_done, hiddenT_ready, y_ready, moe_done = (
            sem("xe_ready"), sem("silu_ready"), sem("hidden_ready"), sem("hiddenT_done"), sem("hiddenT_ready"),
            sem("y_ready"), sem("moe_done"))
        x_moe_ready = sem("x_moe_ready")
        group_done = sem("group_done")
        emptied = {"act": sem("emptied_act"), "dve": sem("emptied_dve")}
        cols_layer = sem("cols_layer")
        hi_ready, lo_ready = sem("hi_ready"), sem("lo_ready")
        l_sq, l_ms, l_std = sem("l_sq"), sem("l_ms"), sem("l_std")
        h_scaled, h_hi_ready, h_lo_ready = sem("h_scaled"), sem("h_hi_ready"), sem("h_lo_ready")
        u_hi_ready, u_lo_ready = sem("u_hi_ready"), sem("u_lo_ready")
        gel_hi_ready, z_hi_ready, z_lo_ready = sem("gel_hi_ready"), sem("z_hi_ready"), sem("z_lo_ready")
        v_ready, pool_sums, pooled_ready = sem("v_ready"), sem("pool_sums"), sem("pooled_ready")
        decay_ready, m2_ready, mult_ready, iv_ready, lru_ready, z_ready = (
            sem("decay_ready"), sem("m2_ready"), sem("mult_ready"), sem("iv_ready"), sem("lru_ready"), sem("z_ready"))
        f_h, outT_done, out_ready_act, out_ready_dve, stored = (
            sem("f_h"), sem("outT_done"), sem("out_ready_act"), sem("out_ready_dve"), sem("stored"))
        dve_first, dve_layer, dve_final = sem("dve_first"), sem("dve_layer"), sem("dve_final")
        pool_first, pool_layer = sem("pool_first"), sem("pool_layer")
        act_layer, act_first = sem("act_layer"), sem("act_first")

        def slot_view(name, k, n):
            return ring[:, ring_plan.slot(name), 0:k * n].rearrange("p (k n) -> p k n", k=k)

        def parts_of(name):
            kind = name[0]
            if kind == "dn":
                return FK, P, P
            if kind == "lup":
                return HEADS, 2 * P, 2 * P
            return KD, 512, 256

        def unit_view(buffer, slot, name, unit):
            k, n, width = parts_of(name)
            tile = buffer[:, slot, 0:k * n].rearrange("p (k n) -> p k n", k=k)
            return tile[:, :, width * unit:width * (unit + 1)]

        def raw_unit(name, unit):
            return unit_view(ring, ring_plan.slot(name), name, unit)

        def lo_unit(name, unit):
            return unit_view(ring_r, ring_plan.slot(name), name, unit)

        def hi_unit(name, unit):
            return unit_view(ring_r, LAYER_SLOTS + splits.hi_slot(name), name, unit)

        block = ctx.enter_context(nc.Block())

        @block.sync
        def _(sp):
            def load(name, dst, src, turn=None):
                s = ring_plan.slot(name)
                if turn is None:
                    if ring_plan.before(name):
                        sp.wait_ge(tile_done[s], ring_plan.before(name))
                else:
                    sp.wait_ge(tile_done[s], ring_plan.before(name, turn))
                    sp.sem_inc(slot_granted, 1)
                sp.dma_start(dst, src).then_inc(loaded[s], 16)

            def columns(w, first, n):
                return w.rearrange("(k p) n -> p k n", p=P)[:, :, first:first + n]

            for (name, _) in [t for t in first_tiles() if t]:
                kind, i = name
                w = {"ada": a["w_ada"][0], "win": a["w_in"][0], "wout": a["w_out"][0]}[kind]
                load(name, slot_view(name, KD, 512), columns(w, 512 * i, 512))

            with sp.Fori(0, E) as e:
                gate = a["w_gate_e"][0][bass.ds(e, 1)].rearrange("a (k p) n -> p (a k) n", p=P)
                up = a["w_up_e"][0][bass.ds(e, 1)].rearrange("a (k p) n -> p (a k) n", p=P)
                down = a["w_down_e"][0][bass.ds(e, 1)].rearrange("a (k p) n -> p (a k) n", p=P)
                for (name, _) in expert_tiles():
                    kind, q = name
                    if kind == "down":
                        load(name, slot_view(name, 4, D), down[:, 4 * q:4 * q + 4, :], e)
                    else:
                        w = gate if kind == "gate" else up
                        load(name, slot_view(name, KD, 512), w[:, :, 512 * q:512 * q + 512], e)

            held = [None] * LAYER_SLOTS
            for tile in layer_tiles():
                held[ring_plan.slot(tile[0])] = tile[0]

            with sp.Fori(0, LAYERS) as l:
                def one(arg):
                    return a[arg][bass.ds(l, 1)]

                def rows(arg, n=P):
                    return one(arg).rearrange("a (k p) n -> p (a k) n", p=n)

                def grouped(arg):
                    return one(arg).rearrange("a h d e -> d (a h) e")

                now = list(held)
                seen = [False] * LAYER_SLOTS
                for name, _, _ in layer_tiles():
                    s = ring_plan.slot(name)
                    before = groups.done(last_group[now[s]], l)
                    if not seen[s]:
                        sp.wait_ge(tile_done[s], ring_plan.end_of_experts[s])
                    sp.wait_ge(group_done, before if seen[s] else before - groups.total)
                    sp.sem_inc(slot_granted, 1)
                    now[s], seen[s] = name, True
                    kind = name[0] if isinstance(name, tuple) else name
                    if kind in ("upa", "upb"):
                        w = rows(("ffn1_w_up", "ffn2_w_up")[name[1]])
                        at = 512 * name[2] + (FFN if kind == "upb" else 0)
                        parts = [(slot_view(name, KD, 512), w[:, :, at:at + 512])]
                    elif kind == "upab":
                        w = rows(("ffn1_w_up", "ffn2_w_up")[name[1]])
                        view = slot_view(name, KD, 512)
                        parts = [(view[:, :, 0:256], w[:, :, 2560:FFN]),
                                 (view[:, :, 256:512], w[:, :, FFN + 2560:2 * FFN])]
                    elif kind == "dn":
                        w = rows(("ffn1_w_down", "ffn2_w_down")[name[1]])
                        parts = [(slot_view(name, FK, P), w[:, :, P * name[2]:P * name[2] + P])]
                    elif kind == "proj":
                        parts = [(slot_view(name, KD, 512), rows("w_in_2")[:, :, 512 * name[1]:512 * name[1] + 512])]
                    elif kind == "small":
                        view = slot_view(name, 2 * HEADS + POOLS, P)
                        parts = [(view[:, 0:HEADS, :], grouped("lru_w_a")),
                                 (view[:, HEADS:2 * HEADS, :], grouped("lru_w_x")),
                                 (view[:, 2 * HEADS:, :], grouped("pool_w"))]
                    elif kind == "pup":
                        parts = [(slot_view(name, POOLS, D), rows("w_pool_up"))]
                    elif kind == "lup":
                        parts = [(slot_view(name, HEADS, 256), rows("w_lru_up")[:, :, 256 * name[1]:256 * name[1] + 256])]
                    else:
                        parts = [(slot_view(name, KD, 512), rows("w_out_2")[:, :, 512 * name[1]:512 * name[1] + 512])]
                    for dst, src in parts:
                        sp.dma_start(dst, src).then_inc(loaded[s], 16)

            for t in range(TT):
                sp.wait_ge(out_ready_act, t + 1)
                sp.wait_ge(out_ready_dve, t + 1)
                sp.dma_start(out[0].rearrange("(t p) d -> p t d", p=P)[:, t, :], out_tok[:, t, :]).then_inc(stored, 16)
            sp.wait_ge(stored, 16 * TT)

        @block.gpsimd
        def _(pool):
            step = Steps(pool, pool_first)
            step(pool.memset(ident[:], 0.0))
            pool.affine_select(out=ident[:], in_=ident[:], compare_op=ALU.not_equal, fill=1.0, base=0,
                               pattern=[[-1, P]], channel_multiplier=1).then_inc(ident_ready, 1)
            pool.memset(mean_d[:], 1.0 / D)
            pool.memset(mean_v[:], 1.0 / P).then_inc(consts_ready, 1)
            pool.iota(rel.rearrange("p (t f) -> p t f", t=TT), pattern=[[-P, TT], [1, S]], base=0,
                      channel_multiplier=-1, allow_small_or_imprecise_dtypes=True)
            pool.iota(reli.bitcast(I32).rearrange("p (t f) -> p t f", t=TT), pattern=[[-P, TT], [1, S]], base=0,
                      channel_multiplier=-1).then_inc(rel_ready, 1)
            pool.iota(t_col, pattern=[[P, TT]], base=0, channel_multiplier=1, allow_small_or_imprecise_dtypes=True)
            pool.iota(pool_fix[:], pattern=[[0, POOLS], [1, 16]], base=1, channel_multiplier=0,
                      allow_small_or_imprecise_dtypes=True)
            pool.memset(pool_u[:, :, 0:16], 0.0).then_inc(consts_ready, 1)

            with pool.Fori(0, LAYERS) as l:
                step = Steps(pool, pool_layer, 4, l)
                e, n = groups.emptied(("pool", 1), l)
                pool.wait_ge(emptied[e], n)
                T = 16 + S
                step(pool.tensor_tensor(pool_a[:, :, 1:T], pool_u[:, :, 1:T], pool_u[:, :, 0:T - 1], ALU.add))
                step(pool.tensor_tensor(pool_b[:, 1:4, 3:T], pool_a[:, 1:4, 3:T], pool_a[:, 1:4, 1:T - 2], ALU.add))
                step(pool.tensor_tensor(pool_a[:, 2:4, 7:T], pool_b[:, 2:4, 7:T], pool_b[:, 2:4, 3:T - 4], ALU.add))
                step(pool.tensor_tensor(pool_b[:, 3:4, 15:T], pool_a[:, 3:4, 15:T], pool_a[:, 3:4, 7:T - 8], ALU.add))
                pool.sem_inc(pool_sums, 1)
                e, n = groups.emptied(("ix", 4), l)
                pool.wait_ge(emptied[e], n)
                pool.tensor_tensor(igate, igate, v, ALU.mult).then_inc(iv_ready, 1)
                assert step.n == step.per

        @block.tensor
        def _(pe):
            def square_sums(ready, first, dst, done):
                for k in range(KD):
                    if k % 2 == 0:
                        pe.wait_ge(ready, first + k // 2)
                    mm = pe.matmul(dst, mean_d[:], h[:, k, :], start=(k == 0), stop=(k == KD - 1))
                mm.then_inc(done, 1)

            pe.sem_inc(group_done, groups.total)
            pe.wait_ge(ident_ready, 1)
            pe.wait_ge(rows_loaded, 16 * (len(FIRST_ROWS) + LAYERS * len(LAYER_ROWS)))
            pe.transpose(bank[0][:, 0:n_first], rows_in[0:n_first, 0, :], ident[0:n_first, 0:n_first])
            for l in range(LAYERS):
                mm = pe.transpose(bank[0][:, P * (1 + l):P * (1 + l) + n_layer], rows_in[0:n_layer, 1 + l, :],
                                  ident[0:n_layer, 0:n_layer])
            mm.then_inc(colsT_done, 1)
            pe.wait_ge(x_loaded, 16)
            for c in range(KD):
                for t in range(TT):
                    mm = pe.transpose(bank[1 + c // 2][:, S * (c % 2) + P * t:S * (c % 2) + P * (t + 1)],
                                      x_tok[:, t, P * c:P * (c + 1)], ident[:])
                if c % 2:
                    mm.then_inc(xT_done, 1)
            pe.wait_ge(consts_ready, 1)
            square_sums(sq_ready, 1, bank[5][:, 0:S], ms_done)

            def modulation(i):
                rows = mod_bank(i)[:, 0:P]
                if i >= 2:
                    pe.wait_ge(mod_ready, i - 1 if i < 4 else i)
                if i == 0:
                    pe.wait_ge(silu_c_ready, 1)
                name = ("ada", i)
                pe.wait_ge(loaded[ring_plan.slot(name)], ring_plan.loaded(name))
                w = slot_view(name, KD, 512)
                for k in range(KD):
                    for g in range(4):
                        mm = pe.matmul(rows[32 * g:32 * g + 32, :], silu_c[:, k, :], w[:, k, P * g:P * (g + 1)],
                                       start=(k == 0), stop=(k == KD - 1), skip_group_check=True)
                mm.then_inc(tile_done[ring_plan.slot(name)], 1)

            def modulation_columns(i):
                pe.wait_ge(modrow_ready, i + 1)
                pe.transpose(mod_bank(i)[:, P:2 * P], modrow[:, i % 2, :],
                             ident[:]).then_inc(modT_done, 1)

            for i in range(4):
                modulation(i)
                modulation_columns(i)

            for i in range(6):
                name = ("win", i)
                pe.wait_ge(loaded[ring_plan.slot(name)], ring_plan.loaded(name))
                if i == 1:
                    pe.wait_ge(x_ready, 4)
                if i >= 2:
                    pe.wait_ge(proj_ready, i - 1)
                w = slot_view(name, KD, 512)
                dst = two_banks[i % 2]
                if i in (1, 5):
                    for t in range(TT):
                        for k in range(KD):
                            mm = pe.matmul(dst[:, 512 * t:512 * (t + 1)], h[:, k, P * t:P * (t + 1)], w[:, k, :],
                                           start=(k == 0), stop=(k == KD - 1))
                else:
                    for c in range(4):
                        for k in range(KD):
                            if i == 0 and c == 0:
                                pe.wait_ge(h_ready, k + 1)
                            mm = pe.matmul(dst[:, S * c:S * (c + 1)], w[:, k, P * c:P * (c + 1)], h[:, k, :],
                                           start=(k == 0), stop=(k == KD - 1))
                mm.then_inc(tile_done[ring_plan.slot(name)], 1)

            pe.wait_ge(proj_ready, 6)

            def ret_scores(hd):
                at, c = RET_QK * (hd % 2), hd // 2
                if hd >= 2:
                    pe.wait_ge(pret_ready, hd - 1)
                for s in range(TT):
                    mm = pe.matmul(bank[4 + hd % 2][:, S * s:S * (s + 1)],
                                   rqk[at:at + RET_QK, 2 + c, P * s:P * (s + 1)], rqk[at:at + RET_QK, c, :],
                                   start=True, stop=True)
                mm.then_inc(ret_scored, 1)

            def ret_values(hd):
                pe.wait_ge(pret_ready, hd + 1)
                for s in range(TT):
                    mm = pe.matmul(two_banks[0][:, S * hd:S * (hd + 1)], rv[:, s, P * hd:P * (hd + 1)],
                                   pret[:, hd % 2, s, :], start=(s == 0), stop=(s == TT - 1))
                mm.then_inc(ret_done, 1)

            ret_scores(0)
            ret_scores(1)
            for hd in range(RET_HEADS):
                ret_values(hd)
                if hd + 2 < RET_HEADS:
                    ret_scores(hd + 2)

            def group_mean(src, ready, dst, done):
                for b in range(2):
                    pe.wait_ge(ready, b + 1)
                    mm = pe.matmul(dst[:, 512 * b:512 * (b + 1)], mean_v[:], src[:, 512 * b:512 * (b + 1)],
                                   start=True, stop=True)
                mm.then_inc(done, 1)

            def att_scores(hd):
                at, c = ATT_DIM * (hd % 2), hd // 2
                if hd >= 2:
                    pe.wait_ge(att_max_ready, hd - 1)
                for t in range(TT):
                    mm = pe.matmul(bank[4 + hd % 2][:, S * t:S * (t + 1)], aq[at:at + ATT_DIM, c, P * t:P * (t + 1)],
                                   ak[at:at + ATT_DIM, c, :], start=True, stop=True)
                mm.then_inc(att_scored, 1)

            def att_transpose(hd):
                pe.wait_ge(att_p_ready, hd + 1)
                if hd >= 1:
                    pe.wait_ge(att_pT_ready, hd)
                for s in range(TT):
                    for t in range(TT):
                        mm = pe.transpose(bank[6][:, S * s + P * t:S * s + P * (t + 1)],
                                          p_att[:, hd % 2, t, P * s:P * (s + 1)], ident[:])
                mm.then_inc(att_pT_done, 1)

            def att_values(hd):
                at, c = ATT_DIM * (hd % 2), hd // 2
                pe.wait_ge(att_pT_ready, hd + 1)
                for s in range(TT):
                    mm = pe.matmul(two_banks[1][at:at + ATT_DIM, S * c:S * (c + 1)],
                                   av[:, s, ATT_DIM * hd:ATT_DIM * (hd + 1)], pT_att[:, s, :],
                                   start=(s == 0), stop=(s == TT - 1), skip_group_check=True)
                mm.then_inc(att_done, 1)

            pe.wait_ge(pret_ready, RET_HEADS)
            att_scores(0)
            group_mean(gn_, ret_copied, two_banks[1], gmean_done)
            att_scores(1)
            for hd in range(ATT_HEADS):
                modulation(4 + hd)
                att_transpose(hd)
                if hd + 2 < ATT_HEADS:
                    att_scores(hd + 2)
                modulation_columns(4 + hd)
                if hd == 0:
                    group_mean(gsq_, gsq_ready, two_banks[0], gvar_done)
                    pe.wait_ge(centred_ready, 2)
                att_values(hd)

            for i in range(2):
                name = ("wout", i)
                pe.wait_ge(loaded[ring_plan.slot(name)], ring_plan.loaded(name))
                w = slot_view(name, KD, 512)
                for c in range(4):
                    for k in range(KD):
                        if i == 0 and c == 0 and k == 0:
                            pe.wait_ge(yret_ready, 4)
                        if i == 0 and c == 0 and k == 4:
                            pe.wait_ge(yatt_ready, 1)
                        mm = pe.matmul(two_banks[i][:, S * c:S * (c + 1)], w[:, k, P * c:P * (c + 1)], mixin[:, k, :],
                                       start=(k == 0), stop=(k == KD - 1))
                mm.then_inc(tile_done[ring_plan.slot(name)], 1)
            square_sums(sq_ready, 5, bank[5][:, 0:S], ms_done)
            square_sums(sq_ready, 9, bank[5][:, 0:S], ms_done)

            pe.wait_ge(misc_loaded, 48)
            for t in range(TT):
                for k in range(KD):
                    if t == 0:
                        pe.wait_ge(h_ready, KD + k + 1)
                    mm = pe.matmul(bank[4][:, E * t:E * (t + 1)], h[:, k, P * t:P * (t + 1)], w_router[:, k, :],
                                   start=(k == 0), stop=(k == KD - 1))
            mm.then_inc(logits_done, 1)
            for t in range(TT):
                for c in range(KD):
                    mm = pe.transpose(bank[2 * t + c // 4][:, P * (c % 4):P * (c % 4 + 1)], h[:, c, P * t:P * (t + 1)],
                                      ident[:])
                    if c % 4 == 3:
                        mm.then_inc(htokT_done, 1)
            pe.wait_ge(aff_ready, 1)
            for t in range(TT):
                mm = pe.transpose(bank[5][0:E, P * t:P * (t + 1)], aff[:, t, :], ident[:])
            mm.then_inc(affT_done, 1)
            pe.wait_ge(spread_ready, 1)
            pe.matmul(bank[6], ones_e, spread.rearrange("p e c -> p (e c)"), start=True, stop=True).then_inc(index_done, 1)

            pe.wait_ge(onehot_ready, 1)
            pe.wait_ge(htok_ready, 4)
            for k in range(KD):
                if k >= 4:
                    pe.wait_ge(xeT_ready, k - 3)
                for t in range(TT):
                    mm = pe.matmul(bank[k % 4], h_tok[:, t, P * k:P * (k + 1)], onehot[:, t, :],
                                   start=(t == 0), stop=(t == TT - 1))
                mm.then_inc(xeT_done, 1)
            for b in range(E // 2):
                pe.wait_ge(weighted_ready, 2 * b // (E // 2) + 1)
                if b < 4:
                    pe.wait_ge(xeT_ready, 5 + b)
                else:
                    pe.wait_ge(gT_ready, b - 3)
                for e in range(2 * b, 2 * b + 2):
                    for t in range(TT):
                        at = S * (e % 2) + P * t
                        mm = pe.transpose(bank[b % 4][:, at:at + P], weighted[e // 8][:, t, e % 8, :], ident[:])
                mm.then_inc(gT_done, 1)
            for b in range(4):
                pe.matmul(bank[4 + b], zeros[:, 0:P], zeros, start=True, stop=True)

            pe.wait_ge(gT_ready, E // 2)
            with pe.Fori(0, E) as e:
                def hidden_products(q):
                    pe.wait_ge(hidden_ready, 4 * e + (q + 1))
                    for half, kind in enumerate(("gate", "up")):
                        name = (kind, q)
                        pe.wait_ge(loaded[ring_plan.slot(name)], ring_plan.loaded(name, e))
                        w = slot_view(name, KD, 512)
                        for k in range(KD):
                            for g in range(4):
                                mm = pe.matmul(bank[q % 2][32 * g:32 * g + 32, P * half:P * (half + 1)], xe[:, k, :],
                                               w[:, k, P * g:P * (g + 1)], start=(k == 0), stop=(k == KD - 1),
                                               skip_group_check=True)
                        mm.then_inc(tile_done[ring_plan.slot(name)], 1)

                def hidden_transpose(q):
                    if q == 0:
                        pe.wait_ge(y_ready, e + 1)
                    pe.wait_ge(hidden_ready, 4 * e + (q + 3))
                    pe.transpose(bank[2 + q % 2][:, 0:P], hidden[:, q % 2, :], ident[:]).then_inc(hiddenT_done, 1)

                def down_products(k):
                    name = ("down", k)
                    if k == 0:
                        pe.wait_ge(hiddenT_ready, 4 * e + FB)
                    pe.wait_ge(loaded[ring_plan.slot(name)], ring_plan.loaded(name, e))
                    w = slot_view(name, 4, D)
                    for half in range(2):
                        for c in range(4):
                            mm = pe.matmul(two_banks[1][32 * c:32 * c + 32, 512 * half:512 * (half + 1)],
                                           hiddenT[:, k, 32 * c:32 * c + 32], w[:, c, 512 * half:512 * (half + 1)],
                                           start=(k == 0), stop=(k == FB - 1), skip_group_check=True)
                    mm.then_inc(tile_done[ring_plan.slot(name)], 1)

                pe.wait_ge(xe_ready, e + 1)
                hidden_products(0)
                hidden_products(1)
                hidden_transpose(0)
                hidden_products(2)
                hidden_transpose(1)
                hidden_products(3)
                hidden_transpose(2)
                hidden_transpose(3)
                for k in range(FB):
                    down_products(k)
                pe.wait_ge(y_ready, e + 2)
                for c in range(KD):
                    mm = pe.matmul(moe_acc[:, c, :], y_part[:, P * c:P * (c + 1)], gT_[:, bass.ds(e * S, S)],
                                   start=False, stop=True, skip_group_check=True)
                mm.then_inc(moe_done, 1)

            square_sums(sq_ready, 13, bank[0][:, 0:S], ms_done)

            def norm(n):
                for k in range(KD):
                    pe.wait_ge(l_sq, KD * n + (k + 1))
                    mm = pe.matmul(bank[7][:, 0:S], mean_d[:], h[:, k, :], start=(k == 0), stop=(k == KD - 1))
                mm.then_inc(l_ms, 1)

            norm(0)

            with pe.Fori(0, LAYERS) as l:
                def tile(name, k, n):
                    pe.wait_ge(loaded[ring_plan.slot(name)], ring_plan.loaded(name, l))
                    return slot_view(name, k, n)

                def open_group(name):
                    e, n = groups.bank_free(name, l)
                    pe.wait_ge(emptied[e], n)
                    return bank[groups.bank(name)]

                def wait_emptied(name):
                    e, n = groups.emptied(name, l)
                    pe.wait_ge(emptied[e], n)

                def three_passes(group, tile_name, unit, hi, lo, blocks, before_k=None, first=0):
                    dst = open_group(group)
                    pe.wait_ge(lo_ready, splits.ready(tile_name, unit, l))
                    n_k = parts_of(tile_name)[0]
                    w_hi, w_lo = hi_unit(tile_name, unit), lo_unit(tile_name, unit)
                    for b in range(blocks):
                        out_b, cols = dst[:, S * b:S * (b + 1)], slice(P * (first + b), P * (first + b + 1))
                        for k in range(n_k):
                            if before_k and b == 0:
                                before_k(k)
                            tokens = slice(S * k, S * (k + 1))
                            pe.matmul(out_b, w_hi[:, k, cols], hi[:, tokens], start=(k == 0), stop=False)
                            pe.matmul(out_b, w_hi[:, k, cols], lo[:, tokens], start=False, stop=False)
                            mm = pe.matmul(out_b, w_lo[:, k, cols], hi[:, tokens], start=False, stop=(k == n_k - 1))
                    mm.then_inc(group_done, 1)

                h_hi_, h_lo_ = h_hi.rearrange("p c t -> p (c t)"), h_lo.rearrange("p c t -> p (c t)")

                def project(group, tile_name, unit, i=None):
                    def h_chunk(k):
                        pe.wait_ge(h_lo_ready, l * 24 + (8 * i + k + 1))

                    three_passes(group, tile_name, unit, h_hi_, h_lo_, 2, None if i is None else h_chunk)

                def ffn(f, i):
                    for j in range(5):
                        for kind, part in (("upa", "a"), ("upb", "b")):
                            for q in range(2):
                                project((part, f, 2 * j + q), (kind, f, j), q,
                                        i if j == 0 and kind == "upa" and q == 0 else None)
                    project(("a", f, 10), ("upab", f), 0)
                    project(("b", f, 10), ("upab", f), 1)

                    def u_chunk(k):
                        if k % 2 == 0:
                            pe.wait_ge(u_lo_ready, l * 22 + (11 * f + k // 2 + 1))

                    for c in range(KD):
                        three_passes(("dn", f, c), ("dn", f, c), 0, u_hi, u_lo, 1, u_chunk if c == 0 else None)
                    norm(3 * l + (i + 1))

                ffn(0, 0)

                for i in (1, 2):
                    for q in range(2):
                        project(("lru", 2 * (i - 1) + q), ("proj", i), q, 1 if i == 1 and q == 0 else None)
                project(("lru", 4), ("proj", 3), 0)
                project(("gelu", 0), ("proj", 3), 1)
                for q in range(2):
                    project(("pool", q), ("proj", 0), q)

                def per_head(name, w, first, src, heads):
                    dst = open_group(name)
                    for b, hd in enumerate(heads):
                        mm = pe.matmul(dst[:, S * b:S * (b + 1)], w[:, first + hd, :], src[:, hd, :],
                                       start=True, stop=True)
                    mm.then_inc(group_done, 1)

                w = tile("small", 2 * HEADS + POOLS, P)
                for q in range(5):
                    pe.wait_ge(v_ready, l * 5 + (q + 1))
                    per_head(("ra", q), w, 0, v, (2 * q, 2 * q + 1))
                for q in range(5):
                    per_head(("ix", q), w, HEADS, v, (2 * q, 2 * q + 1))
                pe.wait_ge(pooled_ready, l + 1)
                for q in range(2):
                    per_head(("pmix", q), w, 2 * HEADS, pooled, (2 * q, 2 * q + 1))
                for i in (4, 5):
                    for q in range(2):
                        project(("gelu", 1 + 2 * (i - 4) + q), ("proj", i), q)
                for i in range(4):
                    for q in range(2):
                        project(("g", 2 * i + q), ("proj", 6 + i), q)
                w = tile("pup", POOLS, D)
                wait_emptied(("pmix", 1))
                for q in range(4):
                    dst = open_group(("pup", q))
                    for b in range(2):
                        for k in range(POOLS):
                            mm = pe.matmul(dst[:, S * b:S * (b + 1)], w[:, k, P * (2 * q + b):P * (2 * q + b + 1)],
                                           pool_mix[:, k, :], start=(k == 0), stop=(k == POOLS - 1))
                    mm.then_inc(group_done, 1)
                pe.wait_ge(lru_ready, 2 * l + 2)
                for c in range(KD):
                    three_passes(("lup", c), ("lup", c // 2), 0, gel_hi, gel_lo, 1, first=c % 2)

                def z_chunk(k):
                    pe.wait_ge(z_lo_ready, l * 8 + (k + 1))

                for i in range(2):
                    for q in range(2):
                        three_passes(("out", 2 * i + q), ("lout", i), q, z_hi, z_lo, 2,
                                     z_chunk if i == 0 and q == 0 else None)
                norm(3 * l + 2)

                ffn(1, 2)

            for t in range(TT):
                for c in range(KD):
                    if t == 0:
                        pe.wait_ge(f_h, c + 1)
                    mm = pe.transpose(bank[2 * t + c // 4][:, P * (c % 4):P * (c % 4 + 1)], h[:, c, P * t:P * (t + 1)],
                                      ident[:])
                    if c % 4 == 3:
                        mm.then_inc(outT_done, 1)

        @block.scalar
        def _(act):
            step = Steps(act, act_first)
            act.dma_start(x_tok, a["x"][0].rearrange("(t p) d -> p t d", p=P)).then_inc(x_loaded, 16)
            for name, n in FIRST_ROWS:
                src = a[name][0] if name != "final_norm" else a[name]
                act.dma_start(rows_in[fo[name]:fo[name] + n, 0, :], src.rearrange("(c p) -> c p", p=P)).then_inc(rows_loaded, 16)
            for l in range(LAYERS):
                for name, n in LAYER_ROWS:
                    src = a[name][l]
                    if name == "conv_w":
                        src = src.rearrange("k (c p) -> (k c) p", p=P)
                    elif name not in ("lru_b_a", "lru_b_x", "pool_b"):
                        src = src.rearrange("(c p) -> c p", p=P)
                    act.dma_start(rows_in[lo[name]:lo[name] + n, 1 + l, :], src).then_inc(rows_loaded, 16)
            for i, name in enumerate(("ret_decay_fwd", "ret_decay_bwd")):
                act.dma_start(decay_in[:, 4 * i:4 * i + 4], a[name].to_broadcast([P, 4])).then_inc(misc_loaded, 16)
            act.dma_start(w_router, a["w_router"][0].rearrange("(k p) e -> p k e", p=P)).then_inc(misc_loaded, 16)

            def root(ms, done, n, ready, eps=EPS):
                act.wait_ge(done, n)
                act.activation(std[:], ms, ACT.Sqrt, bias=eps).then_inc(ready, 1)

            act.wait_ge(cols_ready, 1)
            act.activation(silu_c, first_cols[:, fo["c"]:fo["c"] + KD].unsqueeze(2).broadcast_to([P, KD, 32]),
                           ACT.Silu).then_inc(silu_c_ready, 1)
            for b in range(4):
                act.wait_ge(x_ready, b + 1)
                act.activation(h[:, 2 * b:2 * b + 2, :], x[:, 2 * b:2 * b + 2, :], ACT.Square).then_inc(sq_ready, 1)
            root(bank[5][:, 0:S], ms_done, 1, std_ready)
            act.wait_ge(softexp_ready, 1)
            act.activation(soft[:, 1, :], soft[:, 0, :], ACT.Exp, scale=-1.0).then_inc(softexp_ready, 1)
            for hd in range(RET_HEADS):
                act.wait_ge(dret_arg, hd + 1)
                act.activation(dret[:, hd, :], dret[:, hd, :], ACT.Exp).then_inc(dret_ready, 1)
            for k in range(KD):
                act.wait_ge(scaled_ready, k + 1)
                act.activation(h[:, k, :], h[:, k, :], ACT.Identity, bias=mod[:, k:k + 1]).then_inc(h_ready, 1)

            for i, (dst, func) in enumerate(((None, None), (rv_, ACT.Copy), (rg_, ACT.Silu), (aq_, None),
                                             (ak_, ACT.Copy), (av_, ACT.Copy))):
                name = ("win", i)
                act.wait_ge(tile_done[ring_plan.slot(name)], ring_plan.done(name))
                src = two_banks[i % 2]
                if i == 0:
                    act.activation(rqk_[:, 0:512], src[:, 0:512], ACT.Copy)
                    act.mul(rqk_[:, 512:1024], src[:, 512:1024], QK_SCALE).then_inc(proj_ready, 1)
                elif i == 3:
                    act.mul(dst, src, QK_SCALE).then_inc(proj_ready, 1)
                else:
                    act.activation(dst, src, func).then_inc(proj_ready, 1)

            for b in range(2):
                act.wait_ge(ret_done, 2 * b + 2)
                act.copy(gn_[:, 512 * b:512 * (b + 1)], two_banks[0][:, 512 * b:512 * (b + 1)]).then_inc(ret_copied, 1)
            for b in range(2):
                act.wait_ge(centred_ready, b + 1)
                act.activation(gsq_[:, 512 * b:512 * (b + 1)], gn_[:, 512 * b:512 * (b + 1)], ACT.Square).then_inc(gsq_ready, 1)

            def att_softmax(hd):
                act.wait_ge(att_max_ready, hd + 1)
                for t in range(TT):
                    ins = act.activation(s_att[:, hd % 2, t, :], s_att[:, hd % 2, t, :], ACT.Exp,
                                         bias=att_max[:, hd % 2, t:t + 1])
                ins.then_inc(att_exp, 1)

            def att_copy(hd):
                act.wait_ge(att_pT_done, hd + 1)
                if hd >= 1:
                    act.wait_ge(att_done, hd)
                act.copy(patt_, bank[6]).then_inc(att_pT_ready, 1)

            att_softmax(0)
            for hd in range(ATT_HEADS):
                if hd + 1 < ATT_HEADS:
                    att_softmax(hd + 1)
                att_copy(hd)
                if hd == 0:
                    act.wait_ge(gvar_done, 1)
                    act.activation(gsq_, two_banks[0], ACT.Sqrt, bias=GN_EPS).then_inc(gstd_ready, 1)
            act.wait_ge(att_done, ATT_HEADS)
            act.wait_ge(yret_ready, 4)
            act.copy(mixin[:, 4:8, :].rearrange("p c t -> p (c t)"), two_banks[1]).then_inc(yatt_ready, 1)

            for b in range(4):
                name = ("wout", b // 2)
                act.wait_ge(tile_done[ring_plan.slot(name)], ring_plan.done(name))
                act.activation(h[:, 2 * b:2 * b + 2, :].rearrange("p c t -> p (c t)"),
                               two_banks[b // 2][:, 512 * (b % 2):512 * (b % 2 + 1)], ACT.Square).then_inc(sq_ready, 1)
            root(bank[5][:, 0:S], ms_done, 2, std_ready)
            for b in range(4):
                act.wait_ge(x_ready, 4 + 2 * b + 2)
                act.activation(h[:, 2 * b:2 * b + 2, :], x[:, 2 * b:2 * b + 2, :], ACT.Square).then_inc(sq_ready, 1)
            root(bank[5][:, 0:S], ms_done, 3, std_ready)
            for k in range(KD):
                act.wait_ge(scaled_ready, KD + k + 1)
                act.activation(h[:, k, :], h[:, k, :], ACT.Identity, bias=mod[:, 24 + k:25 + k]).then_inc(h_ready, 1)

            act.wait_ge(lmax_ready, 1)
            for t in range(TT):
                ins = act.activation(aff[:, t, :], bank[4][:, E * t:E * (t + 1)], ACT.Exp, bias=lmax[:, t:t + 1],
                                     accum_out=lsum[:, t:t + 1])
            ins.then_inc(lexp_ready, 1)
            for b in range(4):
                act.wait_ge(htokT_done, b + 1)
                act.copy(h_tok[:, b // 2, 512 * (b % 2):512 * (b % 2 + 1)], bank[b]).then_inc(htok_ready, 1)
            for k in range(KD):
                act.wait_ge(xeT_done, k + 1)
                act.copy(xeT[:, k, :], bank[k % 4]).then_inc(xeT_ready, 1)
            for b in range(E // 2):
                act.wait_ge(gT_done, b + 1)
                act.copy(gT_[:, 512 * b:512 * (b + 1)], bank[b % 4]).then_inc(gT_ready, 1)
            act.sem_inc(y_ready, 1)

            with act.Fori(0, E) as e:
                def silu(q):
                    name = ("up", q)
                    act.wait_ge(tile_done[ring_plan.slot(name)], ring_plan.done(name, e))
                    act.activation(silu_gate[:, q % 2, :], bank[q % 2][:, 0:P], ACT.Silu).then_inc(silu_ready, 1)

                def copy_hidden(q):
                    act.wait_ge(hiddenT_done, 4 * e + (q + 1))
                    act.copy(hiddenT[:, q, :], bank[2 + q % 2][:, 0:P]).then_inc(hiddenT_ready, 1)

                silu(0)
                silu(1)
                copy_hidden(0)
                silu(2)
                copy_hidden(1)
                silu(3)
                copy_hidden(2)
                copy_hidden(3)
                name = ("down", FB - 1)
                act.wait_ge(tile_done[ring_plan.slot(name)], ring_plan.done(name, e))
                act.copy(y_part, two_banks[1]).then_inc(y_ready, 1)

            act.wait_ge(moe_done, E)
            for b in range(4):
                act.activation(h[:, 2 * b:2 * b + 2, :], moe_acc[:, 2 * b:2 * b + 2, :], ACT.Square).then_inc(sq_ready, 1)
            root(bank[0][:, 0:S], ms_done, 4, std_ready)
            act.wait_ge(x_moe_ready, KD)
            act.sem_inc(emptied["act"], groups.per["act"])

            def square(k):
                act.activation(h[:, k, :], x[:, k, :], ACT.Square).then_inc(l_sq, 1)

            def layer_root(n):
                act.wait_ge(l_ms, n + 1)
                act.activation(std[:], bank[7][:, 0:S], ACT.Sqrt, bias=EPS).then_inc(l_std, 1)

            for k in range(KD):
                square(k)
            layer_root(0)

            with act.Fori(0, LAYERS) as l:
                step = Steps(act, act_layer, 1, l)

                def done(name):
                    act.wait_ge(group_done, groups.done(name, l))
                    return bank[groups.bank(name)]

                def wait_emptied(name):
                    e, n = groups.emptied(name, l)
                    act.wait_ge(emptied[e], n)

                def split(name):
                    before, in_last_layer = splits.before(name)
                    if in_last_layer:
                        s = LAYER_SLOTS + splits.hi_slot(name)
                        act.wait_ge(tile_done[s], ring_plan.end_of_experts[s])
                    value = groups.done(last_group[before], l)
                    act.wait_ge(group_done, value - groups.total if in_last_layer else value)
                    act.wait_ge(loaded[ring_plan.slot(name)], ring_plan.loaded(name, l))
                    for unit in range(dict(splits.tiles)[name]):
                        act.copy(hi_unit(name, unit), raw_unit(name, unit)).then_inc(hi_ready, 1)

                def h_high(i):
                    for k in range(KD):
                        act.wait_ge(h_scaled, l * 24 + (8 * i + k + 1))
                        act.copy(h_hi[:, k, :], h[:, k, :]).then_inc(h_hi_ready, 1)

                def ffn(f, i, after):
                    def silu(j):
                        src = done(("a", f, j))
                        if j >= 4:
                            wait_emptied(("b", f, j - 4))
                        act.activation(silu_a[:, j % 4, :], src, ACT.Silu).then_inc(emptied["act"], 1)

                    def u_high(j):
                        wait_emptied(("b", f, j))
                        act.copy(u_hi[:, 512 * j:512 * (j + 1)], u_[:, 512 * j:512 * (j + 1)]).then_inc(u_hi_ready, 1)

                    h_high(i)
                    for j in range(5):
                        split(("upb", f, j))
                        if j:
                            u_high(2 * j - 2)
                            u_high(2 * j - 1)
                        silu(2 * j)
                        silu(2 * j + 1)
                        split(("upa", f, j + 1) if j < 4 else ("upab", f))
                    split(("dn", f, 0))
                    u_high(8)
                    u_high(9)
                    silu(10)
                    u_high(10)
                    for c in range(KD):
                        if c + 1 < KD:
                            split(("dn", f, c + 1))
                        elif after:
                            split(after)
                        if c:
                            wait_emptied(("dn", f, c - 1))
                            square(c - 1)
                    wait_emptied(("dn", f, KD - 1))
                    square(KD - 1)
                    layer_root(3 * l + (i + 1))

                split(("upa", 0, 0))
                ffn(0, 0, ("proj", 1))

                cw, cb = lo["conv_w"], lo["conv_b"]

                def lru_input(g):
                    src = done(("lru", g))
                    act.copy(upad[:, 2 * g:2 * g + 2, TAPS - 1:], src.rearrange("p (c t) -> p c t", c=2))
                    for b in range(2):
                        c = 2 * g + b
                        ins = act.activation(v[:, c, :], src[:, S * b:S * (b + 1)], ACT.Identity,
                                             scale=lc[:, cw + 3 * HEADS + c:cw + 3 * HEADS + c + 1],
                                             bias=lc[:, cb + c:cb + c + 1])
                    ins.then_inc(emptied["act"], 1)

                def gelu(g):
                    src = done(("gelu", g))
                    act.activation(gel_[:, 512 * g:512 * (g + 1)], src, ACT.Gelu_apprx_tanh).then_inc(emptied["act"], 1)

                def gate(g):
                    src = done(("g", g))
                    act.activation(gs_[:, 512 * g:512 * (g + 1)], src, ACT.Sigmoid).then_inc(emptied["act"], 1)

                h_high(1)
                split(("proj", 2))
                lru_input(0)
                lru_input(1)
                split(("proj", 3))
                lru_input(2)
                lru_input(3)
                split(("proj", 0))
                lru_input(4)
                gelu(0)
                split(("proj", 4))
                for g in range(2):
                    src = done(("pool", g))
                    act.copy(pool_u[:, 2 * g:2 * g + 2, 16:], src.rearrange("p (c t) -> p c t", c=2)).then_inc(emptied["act"], 1)
                for part, dst, b0 in (("ra", rgate, lo["lru_b_a"]), ("ix", igate, lo["lru_b_x"])):
                    for g in range(5):
                        src = done((part, g))
                        for b in range(2):
                            c = 2 * g + b
                            ins = act.activation(dst[:, c, :], src[:, S * b:S * (b + 1)], ACT.Sigmoid,
                                                 bias=lc[:, b0 + c:b0 + c + 1])
                        ins.then_inc(emptied["act"], 1)
                split(("proj", 5))
                wait_emptied(("ra", 4))
                for c in range(HEADS):
                    ins = act.activation(decay[:, c, :], rgate[:, c, :], ACT.Exp, scale=lc[:, n_layer + c:n_layer + c + 1])
                step(ins)
                gelu(1)
                gelu(2)
                split(("proj", 6))
                for c in range(HEADS):
                    ins = act.activation(rgate[:, c, :], rgate[:, c, :], ACT.Tanh,
                                         scale=lc[:, n_layer + HEADS + c:n_layer + HEADS + c + 1])
                ins.then_inc(decay_ready, 1)
                gelu(3)
                gelu(4)
                split(("proj", 7))
                gate(0)
                gate(1)
                split(("proj", 8))
                act.wait_ge(m2_ready, l + 1)
                act.activation(r_, r_, ACT.Sqrt).then_inc(mult_ready, 1)
                gate(2)
                gate(3)
                split(("proj", 9))
                gate(4)
                gate(5)
                split(("lup", 0))
                gate(6)
                gate(7)
                act.wait_ge(lru_ready, 2 * l + 1)
                act.copy(gel_hi, gel_).then_inc(gel_hi_ready, 1)

                def z_high(c):
                    act.wait_ge(z_ready, l * 8 + (c + 1))
                    act.copy(z_hi[:, S * c:S * (c + 1)], gs[:, 8 + c, :]).then_inc(z_hi_ready, 1)

                for i in range(4):
                    split(("lup", i + 1) if i < 3 else ("lout", 0))
                    if i:
                        z_high(2 * i - 2)
                        z_high(2 * i - 1)
                z_high(6)
                z_high(7)
                split(("lout", 1))
                for i in range(2):
                    if i:
                        split(("upa", 1, 0))
                    for q in (2 * i, 2 * i + 1):
                        wait_emptied(("out", q))
                        square(2 * q)
                        square(2 * q + 1)
                layer_root(3 * l + 2)

                ffn(1, 2, None)

            for t in range(TT):
                act.wait_ge(outT_done, 2 * t + 1)
                act.copy(out_tok[:, t, 0:512], bank[2 * t]).then_inc(out_ready_act, 1)

        @block.vector
        def _(dve):
            step = Steps(dve, dve_first)
            relf, relint = rel, reli.bitcast(I32)

            dve.wait_ge(rel_ready, 1)
            step(dve.scalar_tensor_tensor(out=dist, in0=relf, scalar=-1.0, in1=relf, op0=ALU.mult, op1=ALU.max))
            step(dve.tensor_scalar(mult_, dist, float(NEAR), None, ALU.is_le))
            for dilation in (4, 16):
                step(dve.tensor_scalar(keep.bitcast(I32), relint, dilation - 1, None, ALU.bitwise_and))
                step(dve.scalar_tensor_tensor(out=mult_, in0=keep.bitcast(I32), scalar=0.0, in1=mult_,
                                              op0=ALU.is_equal, op1=ALU.add))
            step(dve.tensor_scalar(negdist_, mult_, 0.0, NEG, ALU.is_equal, ALU.mult))
            step(dve.tensor_tensor(negdist_, negdist_, dist, ALU.subtract))

            dve.wait_ge(colsT_done, 1)
            step(dve.tensor_copy(first_cols[:], bank[0][:, 0:n_first]))
            for l in range(LAYERS):
                step(dve.tensor_copy(layer_cols[:, n_layer * l:n_layer * (l + 1)],
                                     bank[0][:, P * (1 + l):P * (1 + l) + n_layer]))
            dve.sem_inc(cols_ready, 1)
            for b in range(4):
                dve.wait_ge(xT_done, b + 1)
                dve.tensor_copy(x[:, 2 * b:2 * b + 2, :].rearrange("p c t -> p (c t)"), bank[1 + b]).then_inc(x_ready, 1)

            dve.wait_ge(misc_loaded, 48)
            for l in range(LAYERS):
                at = n_layer * l + lo["lru_lambda"]
                step(dve.tensor_copy(decay_in[:, 8 + HEADS * l:8 + HEADS * (l + 1)], layer_cols[:, at:at + HEADS]))
            dve.scalar_tensor_tensor(out=soft[:, 0, :], in0=decay_in[:], scalar=-1.0, in1=decay_in[:],
                                     op0=ALU.mult, op1=ALU.max).then_inc(softexp_ready, 1)
            dve.wait_ge(softexp_ready, 2)
            step(dve.tensor_scalar(soft[:, 2, :], soft[:, 1, :], 2.0, None, ALU.add))
            step(dve.reciprocal(soft[:, 3, :], soft[:, 2, :]))
            step(dve.tensor_tensor(soft[:, 2, :], soft[:, 1, :], soft[:, 3, :], ALU.mult))
            step(dve.tensor_tensor(soft[:, 3, :], soft[:, 2, :], soft[:, 2, :], ALU.mult))
            step(dve.tensor_scalar(soft[:, 4, :], soft[:, 3, :], 1.0 / 19.0, None, ALU.mult))
            for n in (17, 15, 13, 11, 9, 7, 5, 3):
                step(dve.scalar_tensor_tensor(out=soft[:, 4, :], in0=soft[:, 4, :], scalar=1.0 / n, in1=soft[:, 3, :],
                                              op0=ALU.add, op1=ALU.mult))
            step(dve.scalar_tensor_tensor(out=soft[:, 4, :], in0=soft[:, 4, :], scalar=1.0, in1=soft[:, 2, :],
                                          op0=ALU.add, op1=ALU.mult))
            step(dve.tensor_scalar(soft[:, 5, :], decay_in[:], -1.0, 0.0, ALU.mult, ALU.max))
            step(dve.scalar_tensor_tensor(out=soft[:, 5, :], in0=soft[:, 4, :], scalar=2.0, in1=soft[:, 5, :],
                                          op0=ALU.mult, op1=ALU.add))
            sp = soft[:, 5, :]
            step(dve.tensor_scalar(nsp8[:, 0, :], sp[:, 8:], -LRU_C, None, ALU.mult))
            step(dve.tensor_scalar(nsp8[:, 1, :], sp[:, 8:], LRU_C, None, ALU.mult))
            for hd in range(RET_HEADS):
                step(dve.tensor_scalar(dist, relf, 0.0, sp[:, hd:hd + 1], ALU.max, ALU.mult))
                step(dve.tensor_scalar(dret[:, hd, :], relf, 0.0, sp[:, 4 + hd:5 + hd], ALU.min, ALU.mult))
                dve.tensor_tensor(dret[:, hd, :], dret[:, hd, :], dist, ALU.subtract).then_inc(dret_arg, 1)
                if hd + 1 < RET_HEADS:
                    dve.wait_ge(dret_arg, hd + 1)
            dve.wait_ge(consts_ready, 2)
            for g, w in enumerate(POOL_WINDOWS):
                step(dve.tensor_scalar(pool_fix[:, g, :], pool_fix[:, g, :], float(w), None, ALU.min))
            step(dve.reciprocal(inv_count[:], pool_fix[:]))

            def modulation(i):
                half = mod_bank(i)
                name = ("ada", i)
                dve.wait_ge(tile_done[ring_plan.slot(name)], ring_plan.done(name))
                dve.tensor_copy(modrow[:, i % 2, :], half[:, 0:P]).then_inc(modrow_ready, 1)

            def modulation_columns(i):
                half = mod_bank(i)
                dve.wait_ge(modT_done, i + 1)
                at = fo["b_ada"] + 4 * i
                dve.tensor_tensor(mod[:, 4 * i:4 * i + 4], half[:, P:2 * P:32], first_cols[:, at:at + 4],
                                  ALU.add).then_inc(mod_ready, 1)

            def inverse_root(ready, n):
                dve.wait_ge(ready, n)
                step(dve.reciprocal(rstd[:], std[:]))

            inverse_root(std_ready, 1)
            for i in range(4):
                modulation(i)
                modulation_columns(i)
            dve.wait_ge(mod_ready, 4)
            step(dve.scalar_tensor_tensor(out=gains[:, 0, :], in0=mod[:, 8:16], scalar=1.0,
                                          in1=first_cols[:, fo["g_pre_mix"]:fo["g_pre_mix"] + KD], op0=ALU.add, op1=ALU.mult))
            dve.wait_ge(x_ready, 4)
            for k in range(KD):
                dve.scalar_tensor_tensor(out=h[:, k, :], in0=x[:, k, :], scalar=gains[:, 0, k:k + 1], in1=rstd[:],
                                         op0=ALU.mult, op1=ALU.mult).then_inc(scaled_ready, 1)

            dve.wait_ge(dret_ready, RET_HEADS)
            for hd in range(RET_HEADS):
                dve.wait_ge(ret_scored, hd + 1)
                if hd >= 2:
                    dve.wait_ge(ret_done, hd - 1)
                dve.tensor_tensor(pret[:, hd % 2].rearrange("p s t -> p (s t)"), bank[4 + hd % 2], dret[:, hd, :],
                                  ALU.mult).then_inc(pret_ready, 1)

            def att_scores(hd):
                dve.wait_ge(att_scored, hd + 1)
                sc = s_att[:, hd % 2].rearrange("p t s -> p (t s)")
                step(dve.scalar_tensor_tensor(out=sc, in0=negdist_, scalar=2.0 ** -(hd + 1), in1=bank[4 + hd % 2],
                                              op0=ALU.mult, op1=ALU.add))
                dve.tensor_reduce(att_max[:, hd % 2, :], s_att[:, hd % 2], AX.X, ALU.max,
                                  negate=True).then_inc(att_max_ready, 1)

            def att_weights(hd):
                dve.wait_ge(att_exp, hd + 1)
                if hd >= 2:
                    dve.wait_ge(att_pT_done, hd - 1)
                for t in range(TT):
                    step(dve.tensor_tensor_reduce(p_att[:, hd % 2, t, :], s_att[:, hd % 2, t, :], mult_[:, S * t:S * (t + 1)],
                                                  1.0, 0.0, ALU.mult, ALU.add, att_sum[:, hd % 2, t:t + 1]))
                step(dve.reciprocal(att_inv[:, hd % 2, :], att_sum[:, hd % 2, :]))
                for t in range(TT):
                    ins = dve.tensor_scalar(p_att[:, hd % 2, t, :], p_att[:, hd % 2, t, :], att_inv[:, hd % 2, t:t + 1],
                                            None, ALU.mult)
                ins.then_inc(att_p_ready, 1)

            att_scores(0)
            dve.wait_ge(gmean_done, 1)
            for b in range(2):
                dve.wait_ge(ret_copied, b + 1)
                dve.tensor_tensor(gn_[:, 512 * b:512 * (b + 1)], gn_[:, 512 * b:512 * (b + 1)],
                                  two_banks[1][:, 512 * b:512 * (b + 1)], ALU.subtract).then_inc(centred_ready, 1)
            att_scores(1)
            for hd in range(ATT_HEADS):
                att_weights(hd)
                if hd + 2 < ATT_HEADS:
                    att_scores(hd + 2)
                modulation(4 + hd)
                modulation_columns(4 + hd)
                if hd == 1:
                    dve.wait_ge(gstd_ready, 1)
                    step(dve.reciprocal(pret_, gsq_))
                    step(dve.tensor_tensor(pret_, pret_, gn_, ALU.mult))
                    for c in range(4):
                        dve.tensor_tensor(mixin[:, c, :], pret_[:, S * c:S * (c + 1)], rg[:, c, :], ALU.mult).then_inc(yret_ready, 1)
            dve.wait_ge(mod_ready, 12)
            for i, at, name, plus in ((1, 16, "g_post_mix", 0.0), (2, 32, "g_pre_ffn", 1.0), (3, 40, "g_post_ffn", 0.0)):
                step(dve.scalar_tensor_tensor(out=gains[:, i, :], in0=mod[:, at:at + KD], scalar=plus,
                                              in1=first_cols[:, fo[name]:fo[name] + KD], op0=ALU.add, op1=ALU.mult))

            inverse_root(std_ready, 2)
            for k in range(KD):
                src = two_banks[k // 4][:, S * (k % 4):S * (k % 4 + 1)]
                step(dve.scalar_tensor_tensor(out=mix[:, k, :], in0=src, scalar=gains[:, 1, k:k + 1], in1=rstd[:],
                                              op0=ALU.mult, op1=ALU.mult))
                dve.tensor_tensor(x[:, k, :], x[:, k, :], mix[:, k, :], ALU.add).then_inc(x_ready, 1)
            inverse_root(std_ready, 3)
            dve.wait_ge(x_ready, 4 + KD)
            for k in range(KD):
                dve.scalar_tensor_tensor(out=h[:, k, :], in0=x[:, k, :], scalar=gains[:, 2, k:k + 1], in1=rstd[:],
                                         op0=ALU.mult, op1=ALU.mult).then_inc(scaled_ready, 1)

            step(dve.memset(ones_e, 1.0))
            step(dve.memset(zeros, 0.0))
            dve.wait_ge(logits_done, 1)
            dve.tensor_reduce(lmax, bank[4][:, 0:TT * E].rearrange("p (t e) -> p t e", t=TT), AX.X, ALU.max,
                              negate=True).then_inc(lmax_ready, 1)
            dve.wait_ge(lexp_ready, 1)
            step(dve.reciprocal(linv, lsum))
            for t in range(TT):
                ins = dve.tensor_scalar(aff[:, t, :], aff[:, t, :], linv[:, t:t + 1], None, ALU.mult)
            ins.then_inc(aff_ready, 1)
            dve.wait_ge(affT_done, 1)
            step(dve.tensor_copy(affT, bank[5][0:E, 0:S]))
            now, then = affT, affW
            for r in range(CAP // 8):
                best = top[:, 8 * r:8 * r + 8]
                step(dve.max(best, now))
                step(dve.max_index(topi[:, 8 * r:8 * r + 8], best, now))
                if r + 1 < CAP // 8:
                    step(dve.match_replace(then, best, now, -1.0))
                    now, then = then, now
            step(dve.tensor_copy(topf, topi))
            dve.tensor_tensor(spread, ident[0:E, 0:E].unsqueeze(2).broadcast_to([E, E, CAP]),
                              topf.unsqueeze(1).broadcast_to([E, E, CAP]), ALU.mult).then_inc(spread_ready, 1)
            dve.wait_ge(index_done, 1)
            for t in range(TT):
                ins = dve.tensor_scalar(onehot[:, t, :], bank[6], t_col[:, t:t + 1], None, ALU.is_equal)
            ins.then_inc(onehot_ready, 1)
            dve.wait_ge(onehot_ready, 1)
            dve.wait_ge(aff_ready, 1)
            for half in range(2):
                if half:
                    dve.wait_ge(xeT_done, KD)
                for t in range(TT):
                    cols = onehot[:, t, 256 * half:256 * (half + 1)].rearrange("p (e c) -> p e c", c=CAP)
                    ins = dve.tensor_tensor(
                        weighted[half][:, t].rearrange("p e (g c) -> p e g c", g=4),
                        cols.unsqueeze(2).broadcast_to([P, 8, 4, CAP]),
                        aff[:, t, 8 * half:8 * (half + 1)].unsqueeze(2).unsqueeze(3).broadcast_to([P, 8, 4, CAP]), ALU.mult)
                ins.then_inc(weighted_ready, 1)
            dve.sem_inc(hidden_ready, 2)
            dve.wait_ge(xeT_ready, KD)

            with dve.Fori(0, E) as e:
                name = ("up", FB - 1)
                s = ring_plan.slot(name)
                dve.wait_ge(tile_done[s], ring_plan.done(name, e) - ring_plan.per["expert"][1][s])
                dve.tensor_copy(xe, xeT[:, :, bass.ds(e * CAP, CAP)]).then_inc(xe_ready, 1)
                for q in range(FB):
                    dve.wait_ge(silu_ready, 4 * e + (q + 1))
                    dve.tensor_tensor(hidden[:, q % 2, :], silu_gate[:, q % 2, :], bank[q % 2][:, P:2 * P],
                                      ALU.mult).then_inc(hidden_ready, 1)

            inverse_root(std_ready, 4)
            for k in range(KD):
                step(dve.scalar_tensor_tensor(out=y_part[:, 0:S] if k % 2 else y_part[:, S:2 * S], in0=moe_acc[:, k, :],
                                              scalar=gains[:, 3, k:k + 1], in1=rstd[:], op0=ALU.mult, op1=ALU.mult))
                dve.tensor_tensor(x[:, k, :], x[:, k, :], y_part[:, 0:S] if k % 2 else y_part[:, S:2 * S],
                                  ALU.add).then_inc(x_moe_ready, 1)
            dve.wait_ge(x_moe_ready, KD)
            dve.sem_inc(emptied["dve"], groups.per["dve"])

            with dve.Fori(0, LAYERS) as l:
                step = Steps(dve, dve_layer, 21, l)

                def done(name):
                    dve.wait_ge(group_done, groups.done(name, l))
                    return bank[groups.bank(name)]

                def wait_emptied(name):
                    e, n = groups.emptied(name, l)
                    dve.wait_ge(emptied[e], n)

                def split(name):
                    for unit in range(dict(splits.tiles)[name]):
                        dve.wait_ge(hi_ready, splits.ready(name, unit, l))
                        dve.tensor_tensor(lo_unit(name, unit), raw_unit(name, unit), hi_unit(name, unit).bitcast(F32),
                                          ALU.subtract).then_inc(lo_ready, 1)

                def norm(i, at):
                    dve.wait_ge(l_std, 3 * l + (i + 1))
                    step(dve.reciprocal(rstd[:], std[:]))
                    for k in range(KD + 1):
                        if k < KD:
                            dve.scalar_tensor_tensor(out=h[:, k, :], in0=x[:, k, :], scalar=lc[:, at + k:at + k + 1],
                                                     in1=rstd[:], op0=ALU.mult, op1=ALU.mult).then_inc(h_scaled, 1)
                        if k:
                            dve.wait_ge(h_hi_ready, l * 24 + (8 * i + k))
                            dve.tensor_tensor(h_lo[:, k - 1, :], h[:, k - 1, :], h_hi[:, k - 1, :].bitcast(F32),
                                              ALU.subtract).then_inc(h_lo_ready, 1)

                def ffn(f, i, at, after):
                    def gated(j):
                        src = done(("b", f, j))
                        wait_emptied(("a", f, j))
                        dve.tensor_tensor(u_[:, 512 * j:512 * (j + 1)], src, silu_a[:, j % 4, :],
                                          ALU.mult).then_inc(emptied["dve"], 1)

                    def u_low(j):
                        dve.wait_ge(u_hi_ready, l * 22 + (11 * f + j + 1))
                        part = slice(512 * j, 512 * (j + 1))
                        dve.tensor_tensor(u_lo[:, part], u_[:, part], u_hi[:, part].bitcast(F32),
                                          ALU.subtract).then_inc(u_lo_ready, 1)

                    norm(i, at)
                    if f == 0:
                        split(("upa", f, 0))
                    for j in range(5):
                        split(("upb", f, j))
                        if j:
                            u_low(2 * j - 2)
                            u_low(2 * j - 1)
                        split(("upa", f, j + 1) if j < 4 else ("upab", f))
                        gated(2 * j)
                        gated(2 * j + 1)
                    split(("dn", f, 0))
                    u_low(8)
                    u_low(9)
                    gated(10)
                    u_low(10)
                    for c in range(KD):
                        if c + 1 < KD:
                            split(("dn", f, c + 1))
                        elif after:
                            split(after)
                        src = done(("dn", f, c))
                        dve.scalar_tensor_tensor(out=x[:, c, :], in0=src[:, 0:S], scalar=0.5, in1=x[:, c, :], op0=ALU.mult,
                                                 op1=ALU.add).then_inc(emptied["dve"], 1)
                    wait_emptied(("dn", f, KD - 1))

                step(dve.tensor_copy(lc[:, 0:n_layer], layer_cols[:, bass.ds(l * n_layer, n_layer)]))
                step(dve.tensor_copy(lc[:, n_layer:n_layer + HEADS], nsp8[:, 0, bass.ds(l * HEADS, HEADS)]))
                dve.tensor_copy(lc[:, n_layer + HEADS:], nsp8[:, 1, bass.ds(l * HEADS, HEADS)]).then_inc(cols_layer, 1)
                dve.wait_ge(cols_layer, l + 1)
                ffn(0, 0, lo["norm_ffn1"], ("proj", 1))

                cw = lo["conv_w"]

                def conv(g):
                    wait_emptied(("lru", g))
                    for k in range(TAPS - 1):
                        for c in (2 * g, 2 * g + 1):
                            ins = dve.scalar_tensor_tensor(
                                out=v[:, c, :], in0=upad[:, c, k:k + S], scalar=lc[:, cw + HEADS * k + c:cw + HEADS * k + c + 1],
                                in1=v[:, c, :], op0=ALU.mult, op1=ALU.add)
                        if k < TAPS - 2:
                            step(ins)
                    ins.then_inc(v_ready, 1)

                norm(1, lo["norm_mix"])
                step(dve.memset(upad[:, :, 0:TAPS - 1], 0.0))
                split(("proj", 2))
                conv(0)
                split(("proj", 3))
                conv(1)
                conv(2)
                split(("proj", 0))
                conv(3)
                conv(4)
                split(("proj", 4))
                dve.wait_ge(pool_sums, l + 1)
                sums = (pool_a, pool_b, pool_a, pool_b)
                for g, w in enumerate(POOL_WINDOWS):
                    dve.tensor_tensor(pool_fix[:, g, :], sums[g][:, g, 16:32], inv_count[:, g, :], ALU.mult)
                    ins = dve.scalar_tensor_tensor(out=pooled[:, g, :], in0=sums[g][:, g, 16:], scalar=1.0 / w,
                                                   in1=pool_u[:, g, 16:], op0=ALU.mult, op1=ALU.subtract)
                step(ins)
                dve.tensor_tensor(pooled[:, :, 0:16], pool_fix[:], pool_u[:, :, 16:32], ALU.subtract).then_inc(pooled_ready, 1)
                for g in range(2):
                    src = done(("pmix", g))
                    for b in range(2):
                        c = 2 * g + b
                        ins = dve.tensor_scalar(pool_mix[:, c, :], src[:, S * b:S * (b + 1)],
                                                lc[:, lo["pool_b"] + c:lo["pool_b"] + c + 1],
                                                lc[:, lo["pool_scale"] + c:lo["pool_scale"] + c + 1], ALU.add, ALU.mult)
                    ins.then_inc(emptied["dve"], 1)
                split(("proj", 5))
                split(("proj", 6))
                dve.wait_ge(decay_ready, l + 1)
                step(dve.tensor_tensor(decay_sq, decay_, decay_, ALU.mult))
                split(("proj", 7))
                dve.scalar_tensor_tensor(out=r_, in0=decay_sq, scalar=1.0, in1=r_, op0=ALU.add,
                                         op1=ALU.mult).then_inc(m2_ready, 1)
                step(dve.memset(decay[:, :, 0:1], 0.0))
                split(("proj", 8))
                dve.wait_ge(mult_ready, l + 1)
                dve.wait_ge(iv_ready, l + 1)
                step(dve.tensor_tensor(i_, i_, r_, ALU.mult))
                split(("proj", 9))
                step(dve.tensor_tensor_scan(v_, decay_, i_, 0.0, ALU.mult, ALU.add))
                split(("lup", 0))
                wait_emptied(("gelu", 4))
                dve.tensor_tensor(gel_, gel_, v_, ALU.mult).then_inc(lru_ready, 1)
                dve.wait_ge(gel_hi_ready, l + 1)
                dve.tensor_tensor(gel_lo, gel_, gel_hi.bitcast(F32), ALU.subtract).then_inc(lru_ready, 1)
                for q in range(4):
                    src = done(("pup", q))
                    wait_emptied(("g", q))
                    gq = gs_[:, 512 * q:512 * (q + 1)]
                    dve.tensor_tensor(gq, src, gq, ALU.mult).then_inc(emptied["dve"], 1)

                def gated_sum(c):
                    src = done(("lup", c))
                    wait_emptied(("g", 4 + c // 2))
                    dve.tensor_tensor(gs[:, 8 + c, :], src[:, 0:S], gs[:, 8 + c, :], ALU.mult).then_inc(emptied["dve"], 1)
                    wait_emptied(("lup", c))
                    dve.tensor_tensor(gs[:, 8 + c, :], gs[:, 8 + c, :], gs[:, c, :], ALU.add).then_inc(z_ready, 1)

                def z_low(c):
                    dve.wait_ge(z_hi_ready, l * 8 + (c + 1))
                    part = slice(S * c, S * (c + 1))
                    dve.tensor_tensor(z_lo[:, part], gs[:, 8 + c, :], z_hi[:, part].bitcast(F32),
                                      ALU.subtract).then_inc(z_lo_ready, 1)

                for i in range(4):
                    split(("lup", i + 1) if i < 3 else ("lout", 0))
                    if i:
                        z_low(2 * i - 2)
                        z_low(2 * i - 1)
                    gated_sum(2 * i)
                    gated_sum(2 * i + 1)
                z_low(6)
                z_low(7)
                split(("lout", 1))
                for i in range(2):
                    if i:
                        split(("upa", 1, 0))
                    for q in (2 * i, 2 * i + 1):
                        src = done(("out", q))
                        xs = x[:, 2 * q:2 * q + 2, :].rearrange("p c t -> p (c t)")
                        dve.tensor_tensor(xs, src, xs, ALU.add).then_inc(emptied["dve"], 1)
                wait_emptied(("out", 3))

                ffn(1, 2, lo["norm_ffn2"], None)
                assert step.n == step.per, step.n

            step = Steps(dve, dve_final)
            dve.wait_ge(l_std, 3 * LAYERS + 1)
            step(dve.reciprocal(rstd[:], std[:]))
            at = fo["final_norm"]
            for k in range(KD):
                dve.scalar_tensor_tensor(out=h[:, k, :], in0=x[:, k, :], scalar=first_cols[:, at + k:at + k + 1],
                                         in1=rstd[:], op0=ALU.mult, op1=ALU.mult).then_inc(f_h, 1)
            for t in range(TT):
                dve.wait_ge(outT_done, 2 * t + 2)
                dve.tensor_copy(out_tok[:, t, 512:1024], bank[2 * t + 1]).then_inc(out_ready_dve, 1)


_INS = [(n, n) for n in ("x", "c", "w_ada", "b_ada", "g_pre_mix", "g_post_mix", "g_pre_ffn", "g_post_ffn", "w_in",
                         "ret_decay_fwd", "ret_decay_bwd", "w_out", "w_router", "w_gate_e", "w_up_e", "w_down_e")]
_INS += [(n, n if n in ("w_in_2", "w_out_2") else n[:-2]) for n in (
    "norm_ffn1_2", "ffn1_w_up_2", "ffn1_w_down_2", "norm_mix_2", "w_in_2", "pool_w_2", "pool_b_2", "pool_scale_2",
    "w_pool_up_2", "conv_w_2", "conv_b_2", "lru_w_a_2", "lru_b_a_2", "lru_w_x_2", "lru_b_x_2", "lru_lambda_2",
    "w_lru_up_2", "w_out_2", "norm_ffn2_2", "ffn2_w_up_2", "ffn2_w_down_2", "final_norm_2")]


def kernel(**inputs):
    import numpy as _np
    import concourse.bacc as _bacc
    from concourse import mybir as _mybir
    from concourse.bass_utils import run_bass_kernel_spmd as _run

    nc = _bacc.Bacc("TRN2", target_bir_lowering=False, num_devices=1)
    arrays, args = {}, {}
    for name, own in _INS:
        arr = _np.ascontiguousarray(inputs[name])
        arrays[f"in_{name}_dram"] = arr
        args[own] = nc.dram_tensor(f"in_{name}_dram", arr.shape, _mybir.dt.from_np(arr.dtype), kind="ExternalInput").ap()
    out = nc.dram_tensor("out_0_dram", (1, S, D), F32, kind="ExternalOutput").ap()
    block_kernel(nc, args, out)
    r = _run(nc, [arrays], core_ids=[0])
    return r.results[0]["out_0_dram"]
```

```python
from contextlib import ExitStack

import numpy as np
import concourse.bass as bass
from concourse import mybir

F32 = mybir.dt.float32
F32R = mybir.dt.float32r
BF16 = mybir.dt.bfloat16
I32 = mybir.dt.int32
U32 = mybir.dt.uint32
ALU = mybir.AluOpType
ACT = mybir.ActivationFunctionType
AX = mybir.AxisListType

P = 128
D = 1024
S = 256
KD = D // P
TT = S // P
EPS = 1e-6
GN_EPS = 1e-5

RET_HEADS, RET_QK = 4, 64
ATT_HEADS, ATT_DIM = 8, 64
QK_SCALE = 0.125
NEAR = 64
NEG = -1e30

E, CAP, FF = 16, 32, 2048
FB = FF // 512
LAYERS = 2
FFN = 2816
FK = FFN // P
HEADS = 10
POOLS = 4
POOL_WINDOWS = (2, 4, 8, 16)
TAPS = 4
LRU_C = 8.0

SLOTS = 9
OUTER_SLOTS = 3
SLOT = 4096
SPLIT_SLOTS = 4
HI_SLOTS = SLOTS - OUTER_SLOTS - SPLIT_SLOTS
BANKS = 6
WARM = 14


class Ring:

    def __init__(self, first, expert, layer):
        self.at = {}
        loads, uses = [0] * SLOTS, [0] * SLOTS
        self.per = {}
        for phase, tiles, turns in (("first", first, 1), ("expert", expert, E), ("layer", layer, LAYERS)):
            own_loads, own_uses = [0] * SLOTS, [0] * SLOTS
            for name, dmas, s in tiles:
                own_loads[s] += dmas
                self.at[name] = (phase, s, loads[s] + own_loads[s], uses[s] + own_uses[s])
                own_uses[s] += 1
            self.per[phase] = (own_loads, own_uses)
            loads = [a + turns * b for a, b in zip(loads, own_loads)]
            uses = [a + turns * b for a, b in zip(uses, own_uses)]
            if phase == "first":
                for s in range(SPLIT_SLOTS, SLOTS):
                    uses[s] += 1
            if phase == "expert":
                self.end_of_experts = uses

    def slot(self, name):
        return self.at[name][1]

    def loaded(self, name, turn=0):
        phase, s, loads, _ = self.at[name]
        return turn * (16 * self.per[phase][0][s]) + 16 * loads

    def before(self, name, turn=0):
        phase, s, _, uses = self.at[name]
        return turn * self.per[phase][1][s] + uses

    def done(self, name, turn=0):
        phase, s, _, uses = self.at[name]
        return turn * self.per[phase][1][s] + uses + 1


def first_tiles():
    order = [("ada", 0), ("ada", 1), ("ada", 2), ("ada", 3), ("win", 0), ("win", 1), ("ada", 4), ("win", 2), ("ada", 5),
             ("win", 3), ("ada", 6), ("win", 4), ("ada", 7), ("win", 5), ("ada", 8), ("wout", 0), ("wout", 1),
             ("ada", 9), ("ada", 10), ("ada", 11)]
    return [(name, 1, 0 if name[0] == "ada" else 2, {18: 2, 19: 1}.get(i, i % SPLIT_SLOTS)) for i, name in enumerate(order)]


EXPERT_SLOTS = (2, 1, 3, 0, 4, 5, 6, 7, 8)
LAYER_SLOTS = (0, 2, 1, 3)


def expert_tiles():
    names = [(kind, q) for kind in ("gate", "up", "down") for q in range(FB)]
    return [(name, 1, EXPERT_SLOTS[i % SLOTS]) for i, name in enumerate(names)]


def layer_tiles():
    def ffn(f):
        up = [((kind, f, j), 1, 2) for j in range(5) for kind in ("upa", "upb")]
        return up + [(("upab", f), 2, 2)] + [(("dn", f, c), 1, 1) for c in range(KD)]

    mixer = [(("proj", i), 1, 2) for i in (1, 2, 3, 0)] + [("small", 3, 0)] + [(("proj", i), 1, 2) for i in range(4, 10)]
    mixer += [(("pup", 0), 1, 2)] + [(("lup", i), 1, 1) for i in range(4)] + [(("lout", i), 1, 2) for i in range(2)]
    tiles = ffn(0) + mixer + ffn(1)
    assert len(tiles) % SPLIT_SLOTS == 0
    return [(*tile, LAYER_SLOTS[i % SPLIT_SLOTS]) for i, tile in enumerate(tiles)]


def last_groups():
    last = {}
    for f in range(2):
        for j in range(5):
            last[("upa", f, j)] = ("a", f, 2 * j + 1)
            last[("upb", f, j)] = ("b", f, 2 * j + 1)
        last[("upab", f)] = ("b", f, 10)
        for c in range(KD):
            last[("dn", f, c)] = ("dn", f, c)
    last |= {("proj", 1): ("lru", 1), ("proj", 2): ("lru", 3), ("proj", 3): ("gelu", 0), ("proj", 0): ("pool", 1),
             "small": ("pmix", 1), ("proj", 4): ("gelu", 2), ("proj", 5): ("gelu", 4), ("pup", 0): ("pup", 3)}
    last |= {("proj", 6 + i): ("g", 2 * i + 1) for i in range(4)}
    last |= {("lup", i): ("lup", 2 * i + 1) for i in range(4)}
    return last | {("lout", 0): ("out", 1), ("lout", 1): ("out", 3)}


def layer_groups():
    def ffn(f):
        g = []
        for j in range(5):
            g += [(("a", f, 2 * j), "act"), (("a", f, 2 * j + 1), "act")]
            g += [(("b", f, 2 * j), "dve"), (("b", f, 2 * j + 1), "dve")]
        return g + [(("a", f, 10), "act"), (("b", f, 10), "dve")] + [(("dn", f, c), "dve") for c in range(KD)]

    mixer = [(("lru", g), "act") for g in range(5)] + [(("gelu", 0), "act")]
    mixer += [(("pool", g), "act") for g in range(2)]
    mixer += [(("ra", g), "act") for g in range(5)] + [(("ix", g), "act") for g in range(5)]
    mixer += [(("pmix", g), "dve") for g in range(2)] + [(("gelu", g), "act") for g in range(1, 5)]
    mixer += [(("g", g), "act") for g in range(8)]
    mixer += [(("pup", g), "dve") for g in range(4)] + [(("lup", g), "dve") for g in range(8)]
    mixer += [(("out", g), "dve") for g in range(4)]
    return ffn(0) + mixer + ffn(1)


class Groups:

    def __init__(self, groups):
        self.n = {name: i for i, (name, _) in enumerate(groups)}
        self.engine = [e for _, e in groups]
        self.total = len(groups)
        assert self.total % BANKS == 0
        self.per = {e: self.engine.count(e) for e in ("act", "dve")}

    def bank(self, name):
        return self.n[name] % BANKS

    def done(self, name, layer):
        return layer * self.total + (self.total + self.n[name] + 1)

    def emptied(self, name, layer):
        n = self.n[name]
        e = self.engine[n]
        return e, layer * self.per[e] + (self.per[e] + self.engine[:n + 1].count(e))

    def bank_free(self, name, layer):
        n = self.n[name] - BANKS
        if n >= 0:
            e = self.engine[n]
            return e, layer * self.per[e] + (self.per[e] + self.engine[:n + 1].count(e))
        e = self.engine[n + self.total]
        return e, layer * self.per[e] + self.engine[:n + self.total + 1].count(e)


class Splits:

    def __init__(self, tiles, passing=None):
        self.tiles = [(name, units) for name, _, units, _ in tiles if units or name == passing]
        self.at, n = {}, 0
        for i, (name, units) in enumerate(self.tiles):
            self.at[name] = (i, n)
            n += units
        self.total = n
        assert len(self.tiles) % HI_SLOTS == 0

    def hi_slot(self, name):
        return self.at[name][0] % HI_SLOTS

    def ready(self, name, unit, layer):
        return layer * self.total + (self.at[name][1] + unit + 1)

    def before(self, name):
        i = self.at[name][0] - HI_SLOTS
        if self.tiles[i][1] == 0:
            i -= HI_SLOTS
        return self.tiles[i][0], i < 0


class Steps:

    def __init__(self, eng, sem, per=0, turn=0):
        self.eng, self.sem, self.per, self.turn, self.n = eng, sem, per, turn, 0

    def __call__(self, instruction):
        self.n += 1
        instruction.then_inc(self.sem, 1)
        if self.per:
            self.eng.wait_ge(self.sem, self.turn * self.per + self.n)
        else:
            self.eng.wait_ge(self.sem, self.n)


FIRST_ROWS = (("c", 8), ("b_ada", 48), ("g_pre_mix", 8), ("g_post_mix", 8), ("g_pre_ffn", 8),
              ("g_post_ffn", 8), ("final_norm", 8))
LAYER_ROWS = (("norm_ffn1", 8), ("norm_mix", 8), ("norm_ffn2", 8), ("conv_w", 40), ("conv_b", 10),
              ("lru_b_a", 10), ("lru_b_x", 10), ("lru_lambda", 10), ("pool_b", 4), ("pool_scale", 4))


def offsets(rows):
    at, out = 0, {}
    for name, n in rows:
        out[name] = at
        at += n
    return out, at


def block_kernel(nc, a, out):
    def without_units(tiles):
        return [(name, dmas, slot) for name, dmas, _, slot in tiles]

    ring_plan = Ring(without_units(first_tiles()), expert_tiles(), without_units(layer_tiles()))
    first_splits, splits, last_group = Splits(first_tiles()), Splits(layer_tiles(), "small"), last_groups()
    groups = Groups(layer_groups())
    fo, n_first = offsets(FIRST_ROWS)
    lo, n_layer = offsets(LAYER_ROWS)

    ctx = ExitStack()
    with ctx:
        def sb(name, shape, dt=F32):
            return ctx.enter_context(nc.sbuf_tensor(name, shape, dt))

        def sem(name):
            return ctx.enter_context(nc.semaphore(name))

        WORK = 17664
        WORK_AND_H_HI = WORK + KD * S
        with nc.sbuf_tensor("ring", [P, SLOTS - OUTER_SLOTS, SLOT], F32) as ring, nc.sbuf_tensor("h", [P, KD, S], F32) as h, \
                nc.sbuf_tensor("work", [P, WORK_AND_H_HI], F32) as work:
            pass
        ring_r, h_lo, work_r = (sb("ring_r", [P, SLOTS - OUTER_SLOTS, SLOT], F32R), sb("h_lo", [P, KD, S], F32R),
                                sb("work_r", [P, WORK_AND_H_HI], F32R))
        h_hi = work_r[:, WORK:].rearrange("p (c t) -> p c t", c=KD)
        pool_mix = sb("pool_mix", [P, POOLS, S])
        rk_odd = sb("rk_odd", [P, 2, S])
        table = sb("table", [P, 1])
        w_router = sb("w_router", [P, KD, E])
        x = sb("x", [P, KD, S])
        ident = sb("ident", [P, P])
        mean_d = sb("mean_d", [P, 1])
        std = sb("std", [P, 8])
        rstd_col = sb("rstd_col", [P, 8])
        rstd_row = sb("rstd_row", [P, S])
        mean_v = sb("mean_v", [P, P])
        first_cols = sb("first_cols", [P, n_first])
        layer_cols = sb("layer_cols", [P, LAYERS * n_layer])
        lc = sb("lc", [P, n_layer + 2 * HEADS])
        decay_in = sb("decay_in", [P, 8 + LAYERS * HEADS])
        soft = sb("soft", [P, 6, 8 + LAYERS * HEADS])
        nsp8 = sb("nsp8", [P, 2, LAYERS * HEADS])
        mod = sb("mod", [P, 48])
        gains = sb("gains", [P, 4, KD])
        inv_count = sb("inv_count", [P, POOLS, 16])
        pool_fix = sb("pool_fix", [P, POOLS, 16])
        pool_u = sb("pool_u", [P, POOLS, 16 + S])
        def carve(sizes):
            at, parts = 0, []
            for n in sizes:
                parts.append(work[:, at:at + n])
                at += n
            assert at <= WORK, at
            return parts

        (x_tok_, rqk_, rv_, rg_, aq_, ak_, av_, dret_, negdist_, mult_, pret_, s_, p_, patt_, gn_, gsq_,
         sel_, sc_, small_) = carve(
            (2048, 1024, 1024, 1024, 1024, 1024, 1024, 2048, 512, 512, 1024, 1024, 1024, 512, 1024, 1024,
             64, 256, 64))
        x_tok = x_tok_.rearrange("p (t d) -> p t d", t=TT)
        rows_in = gn_.rearrange("p (n r) -> p n r", r=P)
        rq = rqk_[:, 0:512].rearrange("p (c t) -> p c t", c=2)
        rk = (rqk_[:, 512:1024].rearrange("p (c t) -> p c t", c=2), rk_odd)
        rv = rv_.rearrange("p (t v) -> p t v", t=TT)
        rg = rg_.rearrange("p (c t) -> p c t", c=4)
        aq = (aq_.rearrange("p (c t) -> p c t", c=4), pool_mix)
        ak = ak_.rearrange("p (c t) -> p c t", c=4)
        av = av_.rearrange("p (t v) -> p t v", t=TT)
        dret = dret_.rearrange("p (h n) -> p h n", h=RET_HEADS)
        pret = pret_.rearrange("p (b s t) -> p b s t", b=2, s=TT)
        s_att = s_.rearrange("p (b t s) -> p b t s", b=2, t=TT)
        p_att = p_.rearrange("p (b t s) -> p b t s", b=2, t=TT)
        pT_att = patt_.rearrange("p (s t) -> p s t", s=TT)
        mixin = x_tok_.rearrange("p (c t) -> p c t", c=KD)
        mixin_lo, mixin_hi = work_r[:, 0:2048], work_r[:, 2048:4096]
        gn = gn_.rearrange("p (c t) -> p c t", c=4)
        gsq = gsq_.rearrange("p (c t) -> p c t", c=4)
        modrow = [pool_u[:, 2 * b:2 * b + 2, 16:] for b in range(2)]
        first_rows = sel_[:, 0:1]
        silu_c = sc_.rearrange("p (k m) -> p k m", k=KD)
        att_max = small_[:, 0:4].rearrange("p (b t) -> p b t", b=2)
        att_sum = small_[:, 4:8].rearrange("p (b t) -> p b t", b=2)
        att_inv = small_[:, 8:12].rearrange("p (b t) -> p b t", b=2)
        mix = work[:, 2048:4096].rearrange("p (c t) -> p c t", c=KD)
        rel = p_[:, 0:512]
        dist = p_[:, 512:1024]
        keep = s_[:, 0:512]
        reli = s_[:, 512:1024]
        sizes = (TT * D, TT * E * CAP, TT * P, KD * CAP, 512, 512, FB * P, D, S, 256)
        experts_end = sum(sizes)
        (h_tok_, onehot_, weighted_, xe_, silu_gate, hidden, hT_, yp_, gT_, zeros_) = carve(sizes)
        route_ = work[:, sum(sizes[:4]):sum(sizes[:6])]
        h_tok = h_tok_.rearrange("p (t d) -> p t d", t=TT)
        onehot = onehot_.rearrange("p (t n) -> p t n", t=TT)
        weighted = weighted_.rearrange("p (t n) -> p t n", t=TT)
        xe = xe_.rearrange("p (k n) -> p k n", k=KD)
        hiddenT = hT_.rearrange("p (q n) -> p q n", q=FB)
        y_part = yp_
        zeros = zeros_.bitcast(BF16)
        (u_, sa_, _) = carve((FK * S, 4 * 512, FK * S))
        u_lo, u_hi = work_r[:, 0:FK * S], work_r[:, FK * S + 4 * 512:2 * FK * S + 4 * 512]
        silu_a = sa_.rearrange("p (b n) -> p b n", b=4)
        (v_, i_, a_, r_, gel_, gs_) = carve((HEADS * S,) * 2 + (HEADS * (S + TAPS - 1),) + (HEADS * S,) * 2 + (16 * S,))
        v = v_.rearrange("p (c t) -> p c t", c=HEADS)
        igate = i_.rearrange("p (c t) -> p c t", c=HEADS)
        upad = a_.rearrange("p (c t) -> p c t", c=HEADS)
        decay_ = a_[:, 0:HEADS * S]
        decay = decay_.rearrange("p (c t) -> p c t", c=HEADS)
        rgate = r_.rearrange("p (c t) -> p c t", c=HEADS)
        gs = gs_.rearrange("p (c t) -> p c t", c=16)
        gel_at = 4 * HEADS * S + HEADS * (TAPS - 1)
        gel_hi, gel_lo = work_r[:, 2 * HEADS * S:3 * HEADS * S], work_r[:, gel_at:gel_at + HEADS * S]
        pool_mix_hi = work_r[:, HEADS * S:(HEADS + POOLS) * S]
        pool_mix_lo = work_r[:, (HEADS + POOLS) * S:(HEADS + 2 * POOLS) * S]
        gs_at = gel_at + HEADS * S
        z_hi, z_lo = work_r[:, gs_at:gs_at + 8 * S], work_r[:, gs_at + 8 * S:gs_at + 16 * S]
        pool_a = gs_[:, 0:1088].rearrange("p (g t) -> p g t", g=POOLS)
        pool_b = gs_[:, 1088:2176].rearrange("p (g t) -> p g t", g=POOLS)
        pooled = gs_[:, 2176:3200].rearrange("p (g t) -> p g t", g=POOLS)
        decay_sq = gs_[:, 1536:1536 + HEADS * S]
        routing = sb("routing", [P, 64 + 2 * E])
        t_col = routing[:, 0:2]
        lsum = routing[:, 2:4]
        lmax = routing[:, 4:6]
        linv = routing[:, 6:8]
        aff = routing[:, 64:64 + 2 * E].rearrange("p (t e) -> p t e", t=TT)
        affT = route_[0:E, 0:256]
        affW = route_[0:E, 256:512]
        top = route_[0:E, 512:544]
        topi = route_[0:E, 544:576].bitcast(U32)
        topf = route_[0:E, 576:608]
        spread = yp_[0:E, 0:256].bitcast(BF16).rearrange("p (e c) -> p e c", e=E)
        ones_e = hT_[0:E, 0:P // 2].bitcast(BF16)
        out_tok = work[:, 0:2048].rearrange("p (t d) -> p t d", t=TT)

        psum = ctx.enter_context(nc.psum_tensor("psum", [P, 8 * 512], F32))
        bank = [psum[:, 512 * b:512 * (b + 1)] for b in range(8)]
        two_banks = [psum[:, 1024 * b:1024 * (b + 1)] for b in range(4)]
        def both_tokens(b):
            return psum[:, 512 * b:512 * (b + 2):512]

        moe_acc = psum[:, 2048:4096].rearrange("p (c t) -> p c t", c=KD)

        def mod_bank(i):
            return bank[6 + i % 2] if i < 9 else bank[7]

        def score_bank(hd):
            return bank[(6 if hd < 2 else 4) + hd % 2]

        loaded = [sem(f"loaded{s}") for s in range(SLOTS)]
        tile_done = [sem(f"tile_done{s}") for s in range(SLOTS)]
        slot_granted = sem("slot_granted")
        x_loaded, rows_loaded, layer_rows_loaded, misc_loaded = (
            sem("x_loaded"), sem("rows_loaded"), sem("layer_rows_loaded"), sem("misc_loaded"))
        ident_ready, consts_ready, rel_ready = sem("ident_ready"), sem("consts_ready"), sem("rel_ready")
        colsT_done, cols_ready, layer_colsT_done = sem("colsT_done"), sem("cols_ready"), sem("layer_colsT_done")
        first_hi_ready, first_lo_ready = sem("first_hi_ready"), sem("first_lo_ready")
        gains_ready, mixin_hi_ready, mixin_lo_ready = sem("gains_ready"), sem("mixin_hi_ready"), sem("mixin_lo_ready")
        xT_done, x_ready, sq_ready, ms_done = sem("xT_done"), sem("x_ready"), sem("sq_ready"), sem("ms_done")
        std_ready, rstd_ready, rstd_spread, scaled_ready, h_ready, first_h_lo = sem("std_ready"), sem("rstd_ready"), sem("rstd_spread"), sem("scaled_ready"), sem("h_ready"), sem("first_h_lo")
        silu_c_ready, modrow_ready, modT_done, mod_ready = (
            sem("silu_c_ready"), sem("modrow_ready"), sem("modT_done"), sem("mod_ready"))
        softexp_ready, soft_ready = sem("softexp_ready"), sem("soft_ready")
        dret_arg, dret_ready, masks_ready = sem("dret_arg"), sem("dret_ready"), sem("masks_ready")
        proj_ready = sem("proj_ready")
        ret_scored, pret_ready, ret_done, ret_copied = (
            sem("ret_scored"), sem("pret_ready"), sem("ret_done"), sem("ret_copied"))
        gmean_done, centred_ready, gsq_ready, gvar_done, gstd_ready, grstd_ready, grstd_spread, yret_ready = (
            sem("gmean_done"), sem("centred_ready"), sem("gsq_ready"), sem("gvar_done"), sem("gstd_ready"),
            sem("grstd_ready"), sem("grstd_spread"), sem("yret_ready"))
        att_scored, att_max_ready, att_exp, att_inv_ready, att_p_ready, att_pT_done, att_pT_ready, att_done = (
            sem("att_scored"), sem("att_max_ready"), sem("att_exp"), sem("att_inv_ready"), sem("att_p_ready"), sem("att_pT_done"),
            sem("att_pT_ready"), sem("att_done"))
        mix_ready = sem("mix_ready")
        htokT_done, htok_ready, logits_done, lmax_ready, lexp_ready, aff_ready = (
            sem("htokT_done"), sem("htok_ready"), sem("logits_done"), sem("lmax_ready"), sem("lexp_ready"),
            sem("aff_ready"))
        affT_done, spread_ready, index_done, onehot_ready, weighted_ready = (
            sem("affT_done"), sem("spread_ready"), sem("index_done"), sem("onehot_ready"), sem("weighted_ready"))
        xe_done, gT_done, gT_ready = sem("xe_done"), sem("gT_done"), sem("gT_ready")
        xe_ready, silu_ready, hidden_ready, hiddenT_done, hiddenT_ready, y_ready, moe_done = (
            sem("xe_ready"), sem("silu_ready"), sem("hidden_ready"), sem("hiddenT_done"), sem("hiddenT_ready"),
            sem("y_ready"), sem("moe_done"))
        x_moe_ready = sem("x_moe_ready")
        group_done = sem("group_done")
        emptied = {"act": sem("emptied_act"), "dve": sem("emptied_dve")}
        cols_layer = sem("cols_layer")
        hi_ready, lo_ready = sem("hi_ready"), sem("lo_ready")
        l_sq, l_sum, l_ms, l_std = sem("l_sq"), sem("l_sum"), sem("l_ms"), sem("l_std")
        l_rstd, l_spread = sem("l_rstd"), sem("l_spread")
        h_scaled, h_hi_ready, h_lo_ready = sem("h_scaled"), sem("h_hi_ready"), sem("h_lo_ready")
        u_hi_ready, u_lo_ready = sem("u_hi_ready"), sem("u_lo_ready")
        scan_done, pool_mix_hi_ready, pool_mix_lo_ready = (
            sem("scan_done"), sem("pool_mix_hi_ready"), sem("pool_mix_lo_ready"))
        gel_hi_ready, z_hi_ready, z_lo_ready = sem("gel_hi_ready"), sem("z_hi_ready"), sem("z_lo_ready")
        v_ready, pool_sums, pooled_ready = sem("v_ready"), sem("pool_sums"), sem("pooled_ready")
        decay_ready, m2_ready, mult_ready, iv_ready, lru_ready, z_ready = (
            sem("decay_ready"), sem("m2_ready"), sem("mult_ready"), sem("iv_ready"), sem("lru_ready"), sem("z_ready"))
        f_h, outT_done, out_ready_act, out_ready_dve, stored = (
            sem("f_h"), sem("outT_done"), sem("out_ready_act"), sem("out_ready_dve"), sem("stored"))
        dve_first, dve_layer, dve_final = sem("dve_first"), sem("dve_layer"), sem("dve_final")
        pool_first, pool_layer = sem("pool_first"), sem("pool_layer")
        act_layer, act_first = sem("act_layer"), sem("act_first")

        OUTER = WORK_AND_H_HI - OUTER_SLOTS * SLOT
        assert experts_end <= OUTER

        def slot_view(name, k, n):
            s = ring_plan.slot(name)
            if s < SLOTS - OUTER_SLOTS:
                memory = ring[:, s, :]
            else:
                at = OUTER + (s - (SLOTS - OUTER_SLOTS)) * SLOT
                memory = work[:, at:at + SLOT]
            return memory[:, 0:k * n].rearrange("p (k n) -> p k n", k=k)

        def parts_of(name):
            kind = name[0]
            if kind == "dn":
                return FK, P, P
            if kind == "lup":
                return HEADS, 2 * P, 2 * P
            if kind == "pup":
                return POOLS, D, D // 2
            return KD, 512, 256

        def unit_view(buffer, slot, name, unit):
            k, n, width = parts_of(name)
            tile = buffer[:, slot, 0:k * n].rearrange("p (k n) -> p k n", k=k)
            return tile[:, :, width * unit:width * (unit + 1)]

        def raw_unit(name, unit):
            return unit_view(ring, ring_plan.slot(name), name, unit)

        def lo_unit(name, unit):
            return unit_view(ring_r, ring_plan.slot(name), name, unit)

        def hi_unit(name, unit):
            plan = first_splits if name in first_splits.at else splits
            return unit_view(ring_r, SPLIT_SLOTS + plan.hi_slot(name), name, unit)

        block = ctx.enter_context(nc.Block())

        @block.sync
        def _(sp):
            def load(name, dst, src, turn=None):
                s = ring_plan.slot(name)
                if turn is None:
                    if ring_plan.before(name):
                        sp.wait_ge(tile_done[s], ring_plan.before(name))
                else:
                    sp.wait_ge(tile_done[s], ring_plan.before(name, turn))
                    sp.sem_inc(slot_granted, 1)
                sp.dma_start(dst, src).then_inc(loaded[s], 16)

            def columns(w, first, n):
                return w.rearrange("(k p) n -> p k n", p=P)[:, :, first:first + n]

            sp.dma_start(x_tok, a["x"][0].rearrange("(t p) d -> p t d", p=P)).then_inc(x_loaded, 16)
            for name, n in FIRST_ROWS:
                src = a[name][0] if name != "final_norm" else a[name]
                sp.dma_start(rows_in[fo[name]:fo[name] + n, 0, :], src.rearrange("(c p) -> c p", p=P)).then_inc(rows_loaded, 16)

            def small_loads():
                for i, name in enumerate(("ret_decay_fwd", "ret_decay_bwd")):
                    sp.dma_start(decay_in[:, 4 * i:4 * i + 4], a[name].to_broadcast([P, 4])).then_inc(misc_loaded, 16)
                for l in range(LAYERS):
                    for name, n in LAYER_ROWS:
                        src = a[name][l]
                        if name == "conv_w":
                            src = src.rearrange("k (c p) -> (k c) p", p=P)
                        elif name not in ("lru_b_a", "lru_b_x", "pool_b"):
                            src = src.rearrange("(c p) -> c p", p=P)
                        sp.dma_start(rows_in[lo[name]:lo[name] + n, 1 + l, :], src).then_inc(layer_rows_loaded, 16)
                sp.dma_start(w_router[:], a["w_router"][0].rearrange("(k p) e -> p k e", p=P)).then_inc(misc_loaded, 16)

            for name, _, _, _ in first_tiles():
                kind, i = name
                w = {"ada": a["w_ada"][0], "win": a["w_in"][0], "wout": a["w_out"][0]}[kind]
                load(name, slot_view(name, KD, 512), columns(w, 512 * i, 512))
                if name == ("win", 1):
                    small_loads()

            with sp.Fori(0, E) as e:
                gate = a["w_gate_e"][0][bass.ds(e, 1)].rearrange("a (p k) n -> p (a k) n", p=P)
                up = a["w_up_e"][0][bass.ds(e, 1)].rearrange("a (p k) n -> p (a k) n", p=P)
                down = a["w_down_e"][0][bass.ds(e, 1)].rearrange("a (q p b) n -> p (a q) b n", p=P, q=FB)
                for name, _, _ in expert_tiles():
                    kind, q = name
                    if kind == "down":
                        load(name, slot_view(name, 4, D), down[:, q], e)
                    else:
                        w = gate if kind == "gate" else up
                        load(name, slot_view(name, 2, FF), w[:, 2 * q:2 * q + 2, :], e)

            held = [None] * SPLIT_SLOTS
            for tile in layer_tiles():
                held[ring_plan.slot(tile[0])] = tile[0]

            with sp.Fori(0, LAYERS) as l:
                def one(arg):
                    return a[arg][bass.ds(l, 1)]

                def rows(arg, n=P):
                    return one(arg).rearrange("a (k p) n -> p (a k) n", p=n)

                def grouped(arg):
                    return one(arg).rearrange("a h d e -> d (a h) e")

                now = list(held)
                seen = [False] * SPLIT_SLOTS
                for name, _, _, _ in layer_tiles():
                    s = ring_plan.slot(name)
                    before = groups.done(last_group[now[s]], l)
                    if not seen[s]:
                        sp.wait_ge(tile_done[s], ring_plan.end_of_experts[s])
                    sp.wait_ge(group_done, before if seen[s] else before - groups.total)
                    sp.sem_inc(slot_granted, 1)
                    now[s], seen[s] = name, True
                    kind = name[0] if isinstance(name, tuple) else name
                    if kind in ("upa", "upb"):
                        w = rows(("ffn1_w_up", "ffn2_w_up")[name[1]])
                        at = 512 * name[2] + (FFN if kind == "upb" else 0)
                        parts = [(slot_view(name, KD, 512), w[:, :, at:at + 512])]
                    elif kind == "upab":
                        w = rows(("ffn1_w_up", "ffn2_w_up")[name[1]])
                        view = slot_view(name, KD, 512)
                        parts = [(view[:, :, 0:256], w[:, :, 2560:FFN]),
                                 (view[:, :, 256:512], w[:, :, FFN + 2560:2 * FFN])]
                    elif kind == "dn":
                        w = rows(("ffn1_w_down", "ffn2_w_down")[name[1]])
                        parts = [(slot_view(name, FK, P), w[:, :, P * name[2]:P * name[2] + P])]
                    elif kind == "proj":
                        parts = [(slot_view(name, KD, 512), rows("w_in_2")[:, :, 512 * name[1]:512 * name[1] + 512])]
                    elif kind == "small":
                        view = slot_view(name, 2 * HEADS + POOLS, P)
                        parts = [(view[:, 0:HEADS, :], grouped("lru_w_a")),
                                 (view[:, HEADS:2 * HEADS, :], grouped("lru_w_x")),
                                 (view[:, 2 * HEADS:, :], grouped("pool_w"))]
                    elif kind == "pup":
                        parts = [(slot_view(name, POOLS, D), rows("w_pool_up"))]
                    elif kind == "lup":
                        parts = [(slot_view(name, HEADS, 256), rows("w_lru_up")[:, :, 256 * name[1]:256 * name[1] + 256])]
                    else:
                        parts = [(slot_view(name, KD, 512), rows("w_out_2")[:, :, 512 * name[1]:512 * name[1] + 512])]
                    for dst, src in parts:
                        sp.dma_start(dst, src).then_inc(loaded[s], 16)

            name = ("upa", 0, 0)
            s = ring_plan.slot(name)
            sp.wait_ge(group_done, groups.done(last_group[held[s]], LAYERS - 1))
            sp.dma_start(slot_view(name, KD, 512), columns(a["ffn1_w_up"][LAYERS - 1], 0, 512)).then_inc(loaded[s], 16)

            for t in range(TT):
                sp.wait_ge(out_ready_act, t + 1)
                sp.wait_ge(out_ready_dve, t + 1)
                sp.dma_start(out[0].rearrange("(t p) d -> p t d", p=P)[:, t, :], out_tok[:, t, :]).then_inc(stored, 16)
            sp.wait_ge(stored, 16 * TT)

        @block.gpsimd
        def _(pool):
            step = Steps(pool, pool_first)
            step(pool.memset(ident[:], 0.0))
            pool.affine_select(out=ident[:], in_=ident[:], compare_op=ALU.not_equal, fill=1.0, base=0,
                               pattern=[[-1, P]], channel_multiplier=1).then_inc(ident_ready, 1)
            pool.memset(mean_d[:], 1.0 / D)
            pool.memset(mean_v[:], 1.0 / P).then_inc(consts_ready, 1)
            pool.iota(rel.rearrange("p (t f) -> p t f", t=TT), pattern=[[-P, TT], [1, S]], base=0,
                      channel_multiplier=-1, allow_small_or_imprecise_dtypes=True)
            pool.iota(reli.bitcast(I32).rearrange("p (t f) -> p t f", t=TT), pattern=[[-P, TT], [1, S]], base=0,
                      channel_multiplier=-1).then_inc(rel_ready, 1)
            pool.iota(t_col, pattern=[[P, TT]], base=0, channel_multiplier=1, allow_small_or_imprecise_dtypes=True)
            pool.iota(pool_fix[:], pattern=[[0, POOLS], [1, 16]], base=1, channel_multiplier=0,
                      allow_small_or_imprecise_dtypes=True)
            step(pool.memset(pool_u[:, :, 0:16], 0.0))
            half = P // 2
            step(pool.memset(rk[0][half:P], 0.0))
            step(pool.memset(rk[1][0:half], 0.0))
            step(pool.memset(aq[0][half:P], 0.0))
            pool.memset(aq[1][0:half], 0.0).then_inc(consts_ready, 1)

            with pool.Fori(0, LAYERS) as l:
                step = Steps(pool, pool_layer, 4, l)
                e, n = groups.emptied(("pool", 1), l)
                pool.wait_ge(emptied[e], n)
                T = 16 + S
                step(pool.tensor_tensor(pool_a[:, :, 1:T], pool_u[:, :, 1:T], pool_u[:, :, 0:T - 1], ALU.add))
                step(pool.tensor_tensor(pool_b[:, 1:4, 3:T], pool_a[:, 1:4, 3:T], pool_a[:, 1:4, 1:T - 2], ALU.add))
                step(pool.tensor_tensor(pool_a[:, 2:4, 7:T], pool_b[:, 2:4, 7:T], pool_b[:, 2:4, 3:T - 4], ALU.add))
                step(pool.tensor_tensor(pool_b[:, 3:4, 15:T], pool_a[:, 3:4, 15:T], pool_a[:, 3:4, 7:T - 8], ALU.add))
                pool.sem_inc(pool_sums, 1)
                e, n = groups.emptied(("ix", 4), l)
                pool.wait_ge(emptied[e], n)
                pool.tensor_tensor(igate, igate, v, ALU.mult).then_inc(iv_ready, 1)
                assert step.n == step.per

        @block.tensor
        def _(pe):
            def square_sums(ready, first, b, done):
                for k in range(KD):
                    if k % 2 == 0:
                        pe.wait_ge(ready, first + k // 2)
                    for t in range(TT):
                        mm = pe.matmul(bank[b + t][:, 0:1], h[:, k, P * t:P * (t + 1)], mean_d[:], start=(k == 0),
                                       stop=(k == KD - 1))
                mm.then_inc(done, 1)

            def spread_columns(ready, n, dst, columns, done):
                pe.wait_ge(ready, n)
                for t in range(columns):
                    mm = pe.matmul(dst[:, P * t:P * (t + 1)], rstd_col[:, t:t + 1].broadcast_to([P, P]), ident[:],
                                   start=True, stop=True)
                mm.then_inc(done, 1)

            pe.sem_inc(group_done, groups.total)
            pe.wait_ge(ident_ready, 1)
            pe.wait_ge(x_loaded, 16)
            for c in range(KD):
                for t in range(TT):
                    mm = pe.transpose(bank[1 + c // 2][:, S * (c % 2) + P * t:S * (c % 2) + P * (t + 1)],
                                      x_tok[:, t, P * c:P * (c + 1)], ident[:])
                if c % 2:
                    mm.then_inc(xT_done, 1)
            pe.wait_ge(rows_loaded, 16 * len(FIRST_ROWS))
            pe.transpose(bank[0][:, 0:n_first], rows_in[0:n_first, 0, :],
                         ident[0:n_first, 0:n_first]).then_inc(colsT_done, 1)
            pe.wait_ge(consts_ready, 1)
            square_sums(sq_ready, 1, 5, ms_done)
            spread_columns(rstd_ready, 1, bank[5], TT, rstd_spread)

            def modulation(i):
                rows = mod_bank(i)
                if i >= 2:
                    pe.wait_ge(mod_ready, i - 1 if i < 9 else i)
                if i == 9:
                    pe.wait_ge(att_max_ready, 2)
                if i == 0:
                    pe.wait_ge(silu_c_ready, 1)
                name = ("ada", i)
                pe.wait_ge(loaded[ring_plan.slot(name)], ring_plan.loaded(name))
                w = slot_view(name, KD, 512)
                for k in range(KD):
                    g = k % 4
                    mm = pe.matmul(rows[32 * g:32 * g + 32, :], silu_c[:, k, :], w[:, k, :],
                                   start=(k < 4), stop=(k >= KD - 4), skip_group_check=True)
                mm.then_inc(tile_done[ring_plan.slot(name)], 1)

            def modulation_columns(i):
                pe.wait_ge(modrow_ready, i + 1)
                for c in range(4):
                    mm = pe.matmul(mod_bank(i)[:, c:c + 1], modrow[i % 2][:, c // 2, P * (c % 2):P * (c % 2 + 1)],
                                   first_rows, start=True, stop=True)
                mm.then_inc(modT_done, 1)

            for i in range(4):
                modulation(i)
                modulation_columns(i)

            def split_products(name, dst, src_hi, src_lo, before_k=None):
                for c in range(4):
                    unit, cols = c // 2, slice(P * (c % 2), P * (c % 2 + 1))
                    if c % 2 == 0:
                        pe.wait_ge(first_lo_ready, first_splits.ready(name, unit, 0))
                    w_hi, w_lo = hi_unit(name, unit), lo_unit(name, unit)
                    out_c = dst[:, S * c:S * (c + 1)]
                    for k in range(KD):
                        if before_k and c == 0:
                            before_k(k)
                        pe.matmul(out_c, w_hi[:, k, cols], src_hi[:, S * k:S * (k + 1)], start=(k == 0), stop=False)
                        pe.matmul(out_c, w_hi[:, k, cols], src_lo[:, S * k:S * (k + 1)], start=False, stop=False)
                        mm = pe.matmul(out_c, w_lo[:, k, cols], src_hi[:, S * k:S * (k + 1)], start=False, stop=(k == KD - 1))
                mm.then_inc(tile_done[ring_plan.slot(name)], 1)

            h_hi_, h_lo_ = h_hi.rearrange("p c t -> p (c t)"), h_lo.rearrange("p c t -> p (c t)")

            def h_chunk(k):
                pe.wait_ge(first_h_lo, k + 1)

            def layer_columns():
                pe.wait_ge(scaled_ready, 1)
                pe.wait_ge(layer_rows_loaded, 16 * LAYERS * len(LAYER_ROWS))
                for l in range(LAYERS):
                    mm = pe.transpose(bank[5][:, S + P * l:S + P * l + n_layer], rows_in[0:n_layer, 1 + l, :],
                                      ident[0:n_layer, 0:n_layer])
                mm.then_inc(layer_colsT_done, 1)


            for i in range(6):
                name = ("win", i)
                if i == 1:
                    pe.wait_ge(x_ready, 4)
                if i >= 2:
                    pe.wait_ge(proj_ready, i - 1)
                dst = two_banks[i % 2]
                if i in (1, 5):
                    pe.wait_ge(first_lo_ready, first_splits.ready(name, 1, 0))
                    w_hi = ring_r[:, SPLIT_SLOTS + first_splits.hi_slot(name), :]
                    w_lo = ring_r[:, ring_plan.slot(name), :]
                    for t in range(TT):
                        out_t = dst[:, 512 * t:512 * (t + 1)]
                        for k in range(KD):
                            tokens, cols = slice(P * t, P * (t + 1)), slice(512 * k, 512 * (k + 1))
                            pe.matmul(out_t, h_hi[:, k, tokens], w_hi[:, cols], start=(k == 0), stop=False)
                            pe.matmul(out_t, h_hi[:, k, tokens], w_lo[:, cols], start=False, stop=False)
                            mm = pe.matmul(out_t, h_lo[:, k, tokens], w_hi[:, cols], start=False, stop=(k == KD - 1))
                    mm.then_inc(tile_done[ring_plan.slot(name)], 1)
                else:
                    split_products(name, dst, h_hi_, h_lo_, h_chunk if i == 0 else None)
                if i == 0:
                    layer_columns()
                if i >= 2:
                    modulation_columns(2 + i)
                if i >= 1:
                    modulation(3 + i)

            pe.wait_ge(proj_ready, 6)
            pe.wait_ge(consts_ready, 2)

            def ret_scores(hd):
                c = hd // 2
                if hd >= 2:
                    pe.wait_ge(pret_ready, hd - 1)
                for s in range(TT):
                    mm = pe.matmul(bank[4 + hd % 2][:, S * s:S * (s + 1)],
                                   rk[hd % 2][:, c, P * s:P * (s + 1)], rq[:, c, :], start=True, stop=True)
                mm.then_inc(ret_scored, 1)

            def ret_values(hd):
                pe.wait_ge(pret_ready, hd + 1)
                for s in range(TT):
                    mm = pe.matmul(two_banks[0][:, S * hd:S * (hd + 1)], rv[:, s, P * hd:P * (hd + 1)],
                                   pret[:, hd % 2, s, :], start=(s == 0), stop=(s == TT - 1))
                mm.then_inc(ret_done, 1)

            def att_scores(hd):
                c = hd // 2
                if hd >= 4:
                    pe.wait_ge(att_max_ready, hd - 1)
                for t in range(TT):
                    mm = pe.matmul(score_bank(hd)[:, S * t:S * (t + 1)], aq[hd % 2][:, c, P * t:P * (t + 1)],
                                   ak[:, c, :], start=True, stop=True)
                mm.then_inc(att_scored, 1)

            ret_scores(0)
            ret_scores(1)
            modulation_columns(8)
            pe.wait_ge(mod_ready, 9)
            att_scores(0)
            att_scores(1)
            for hd in range(RET_HEADS):
                ret_values(hd)
                if hd + 2 < RET_HEADS:
                    ret_scores(hd + 2)

            for b in range(2):
                pe.wait_ge(ret_copied, b + 1)
                mm = pe.matmul(two_banks[1][:, 512 * b:512 * (b + 1)], mean_v[:], gn_[:, 512 * b:512 * (b + 1)],
                               start=True, stop=True)
            mm.then_inc(gmean_done, 1)

            def group_variance():
                for c in range(RET_HEADS * TT):
                    if c % RET_HEADS == 0:
                        pe.wait_ge(gsq_ready, c // RET_HEADS + 1)
                    mm = pe.matmul(two_banks[0][:, c:c + 1], gsq_[:, P * c:P * (c + 1)], mean_v[:, 0:1],
                                   start=True, stop=True)
                mm.then_inc(gvar_done, 1)

            def att_transpose(hd):
                pe.wait_ge(att_p_ready, hd + 1)
                if hd >= 1:
                    pe.wait_ge(att_pT_ready, hd)
                for s in range(TT):
                    for t in range(TT):
                        mm = pe.transpose(bank[6][:, S * s + P * t:S * s + P * (t + 1)],
                                          p_att[:, hd % 2, t, P * s:P * (s + 1)], ident[:])
                mm.then_inc(att_pT_done, 1)

            def att_values(hd):
                at, c = ATT_DIM * (hd % 2), hd // 2
                pe.wait_ge(att_pT_ready, hd + 1)
                for s in range(TT):
                    mm = pe.matmul(two_banks[1][at:at + ATT_DIM, S * c:S * (c + 1)],
                                   av[:, s, ATT_DIM * hd:ATT_DIM * (hd + 1)], pT_att[:, s, :],
                                   start=(s == 0), stop=(s == TT - 1), skip_group_check=True)
                mm.then_inc(att_done, 1)

            for hd in range(ATT_HEADS):
                att_transpose(hd)
                if hd + 2 < ATT_HEADS:
                    att_scores(hd + 2)
                if hd in (0, 2, 4):
                    modulation(9 + hd // 2)
                if hd == 0:
                    group_variance()
                    pe.wait_ge(centred_ready, 2)
                if hd == 6:
                    spread_columns(grstd_ready, 1, two_banks[0], RET_HEADS * TT, grstd_spread)
                att_values(hd)
                if hd in (0, 2, 4):
                    modulation_columns(9 + hd // 2)

            def mixin_chunk(k):
                if k in (0, 6):
                    pe.wait_ge(mixin_lo_ready, 2 if k == 0 else 3)

            pe.wait_ge(yret_ready, 1)
            for i in range(2):
                split_products(("wout", i), two_banks[i], mixin_hi, mixin_lo, mixin_chunk if i == 0 else None)
            for s in range(SPLIT_SLOTS, SLOTS):
                pe.sem_inc(tile_done[s], 1)
            square_sums(sq_ready, 5, 5, ms_done)
            spread_columns(rstd_ready, 2, bank[5], TT, rstd_spread)
            square_sums(sq_ready, 9, 5, ms_done)
            spread_columns(rstd_ready, 3, bank[5], TT, rstd_spread)

            pe.wait_ge(misc_loaded, 48)
            for k in range(KD):
                pe.wait_ge(h_ready, KD + k + 1)
                for t in range(TT):
                    mm = pe.matmul(bank[4 + 2 * t][:, 0:E], h[:, k, P * t:P * (t + 1)], w_router[:, k, :],
                                   start=(k == 0), stop=(k == KD - 1))
            mm.then_inc(logits_done, 1)

            def tokens_out(t):
                for c in range(KD):
                    mm = pe.transpose(bank[2 * t + c // 4][:, P * (c % 4):P * (c % 4 + 1)], h[:, c, P * t:P * (t + 1)],
                                      ident[:])
                    if c % 4 == 3:
                        mm.then_inc(htokT_done, 1)

            tokens_out(0)
            pe.wait_ge(aff_ready, 1)
            for t in range(TT):
                mm = pe.transpose(bank[5][0:E, P * t:P * (t + 1)], aff[:, t, :], ident[:])
            mm.then_inc(affT_done, 1)
            tokens_out(1)
            pe.wait_ge(spread_ready, 1)
            pe.matmul(bank[6], ones_e, spread.rearrange("p e c -> p (e c)"), start=True, stop=True).then_inc(index_done, 1)
            pe.wait_ge(onehot_ready, 1)
            for b in range(4, 8):
                pe.matmul(bank[b], zeros[:, 0:P], zeros, start=True, stop=True)

            pe.wait_ge(htok_ready, 4)
            with pe.Fori(0, E) as e:
                def gather():
                    pe.wait_ge(y_ready, e + 1)
                    for k in range(KD):
                        for t in range(TT):
                            mm = pe.matmul(bank[2][:, CAP * k:CAP * (k + 1)], h_tok[:, t, k::KD],
                                           onehot[:, t, bass.ds(e * CAP, CAP)], start=(t == 0), stop=(t == TT - 1))
                    mm.then_inc(xe_done, 1)

                def gather_gates():
                    pe.wait_ge(weighted_ready, e + 1)
                    for t in range(TT):
                        mm = pe.transpose(bank[3][:, P * t:P * (t + 1)], weighted[:, t, :], ident[:])
                    mm.then_inc(gT_done, 1)

                def hidden_products(kind, dst):
                    for q in range(FB):
                        name = (kind, q)
                        pe.wait_ge(loaded[ring_plan.slot(name)], ring_plan.loaded(name, e))
                        w = slot_view(name, 2, FF)
                        for k in range(2):
                            for g in range(4):
                                mm = pe.matmul(dst[32 * g:32 * g + 32, :], xe[:, 2 * q + k, :],
                                               w[:, k, 512 * g:512 * (g + 1)], start=(q == 0 and k == 0),
                                               stop=(q == FB - 1 and k == 1), skip_group_check=True)
                        mm.then_inc(tile_done[ring_plan.slot(name)], 1)

                def hidden_transpose():
                    pe.wait_ge(gT_ready, e + 2)
                    pe.wait_ge(hidden_ready, e + 1)
                    for b in range(4):
                        mm = pe.transpose(bank[2][:, P * b:P * (b + 1)], hidden[:, b::4], ident[:])
                    mm.then_inc(hiddenT_done, 1)

                def down_products(q):
                    name = ("down", q)
                    if q == 0:
                        pe.wait_ge(hiddenT_ready, e + 1)
                    pe.wait_ge(loaded[ring_plan.slot(name)], ring_plan.loaded(name, e))
                    w = slot_view(name, 4, D)
                    for half in range(2):
                        for b in range(4):
                            mm = pe.matmul(two_banks[1][32 * b:32 * b + 32, 512 * half:512 * (half + 1)],
                                           hiddenT[:, b, 32 * q:32 * q + 32], w[:, b, 512 * half:512 * (half + 1)],
                                           start=(q == 0), stop=(q == FB - 1), skip_group_check=True)
                    mm.then_inc(tile_done[ring_plan.slot(name)], 1)

                gather()
                gather_gates()
                pe.wait_ge(xe_ready, e + 1)
                hidden_products("gate", bank[0])
                hidden_products("up", bank[1])
                hidden_transpose()
                for q in range(FB):
                    down_products(q)
                pe.wait_ge(y_ready, e + 2)
                for c in range(KD):
                    mm = pe.matmul(moe_acc[:, c, :], y_part[:, P * c:P * (c + 1)], gT_,
                                   start=False, stop=True, skip_group_check=True)
                mm.then_inc(moe_done, 1)

            square_sums(sq_ready, 13, 0, ms_done)
            spread_columns(rstd_ready, 4, bank[0], TT, rstd_spread)

            def keep_warm(dst, w, n):
                for _ in range(n):
                    pe.matmul(dst[:, 0:S], w[:, 0, 0:P], w[:, 0, 0:S], start=True, stop=True)

            def norm(n, alone, dst, w, b=6):
                if alone > 1:
                    pe.wait_ge(l_sum, n)
                for k in (0, *range(alone, KD)):
                    if k or alone == 1:
                        pe.wait_ge(l_sq, KD * n + (k + 1))
                    for t in range(TT):
                        mm = pe.matmul(bank[b + t][:, 0:1], h[:, k, P * t:P * (t + 1)], mean_d[:], start=(k == 0),
                                       stop=(k == KD - 1))
                mm.then_inc(l_ms, 1)
                keep_warm(dst, w, WARM)
                spread_columns(l_rstd, n + 1, bank[7], TT, l_spread)
                keep_warm(dst, w, WARM)

            pe.wait_ge(lo_ready, splits.ready(("upa", 0, 0), 0, 0))
            norm(0, 1, bank[2], hi_unit(("upa", 0, 0), 0), 0)

            with pe.Fori(0, LAYERS) as l:
                def tile(name, k, n):
                    pe.wait_ge(loaded[ring_plan.slot(name)], ring_plan.loaded(name, l))
                    return slot_view(name, k, n)

                def open_group(name):
                    e, n = groups.bank_free(name, l)
                    pe.wait_ge(emptied[e], n)
                    return bank[groups.bank(name)]

                def wait_emptied(name):
                    e, n = groups.emptied(name, l)
                    pe.wait_ge(emptied[e], n)

                def next_norm(n, alone, group, tile_name, layer):
                    e, value = groups.bank_free(group, layer)
                    pe.wait_ge(emptied[e], value)
                    pe.wait_ge(lo_ready, splits.ready(tile_name, 0, layer))
                    norm(n, alone, bank[groups.bank(group)], hi_unit(tile_name, 0))

                def three_passes(group, tile_name, unit, hi, lo, blocks, before_k=None, first=0):
                    dst = open_group(group)
                    pe.wait_ge(lo_ready, splits.ready(tile_name, unit, l))
                    n_k = parts_of(tile_name)[0]
                    w_hi, w_lo = hi_unit(tile_name, unit), lo_unit(tile_name, unit)
                    for b in range(blocks):
                        out_b, cols = dst[:, S * b:S * (b + 1)], slice(P * (first + b), P * (first + b + 1))
                        for k in range(n_k):
                            if before_k and b == 0:
                                before_k(k)
                            tokens = slice(S * k, S * (k + 1))
                            pe.matmul(out_b, w_hi[:, k, cols], hi[:, tokens], start=(k == 0), stop=False)
                            pe.matmul(out_b, w_hi[:, k, cols], lo[:, tokens], start=False, stop=False)
                            mm = pe.matmul(out_b, w_lo[:, k, cols], hi[:, tokens], start=False, stop=(k == n_k - 1))
                    mm.then_inc(group_done, 1)

                def project(group, tile_name, unit):
                    three_passes(group, tile_name, unit, h_hi_, h_lo_, 2)

                def first_projections(names, tile_name, i):
                    dst = [open_group(name) for name in names]
                    pe.wait_ge(lo_ready, splits.ready(tile_name, 1, l))
                    for b in range(2):
                        cols = slice(P * b, P * (b + 1))
                        order = [(k, q) for k in range(KD) for q in range(2)]
                        for k, q in order if b == 0 else sorted(order, key=lambda kq: kq[1]):
                            if b == 0 and q == 0:
                                pe.wait_ge(h_lo_ready, l * 24 + (8 * i + k + 1))
                            w_hi, w_lo = hi_unit(tile_name, q), lo_unit(tile_name, q)
                            out_b, tokens = dst[q][:, S * b:S * (b + 1)], slice(S * k, S * (k + 1))
                            pe.matmul(out_b, w_hi[:, k, cols], h_hi_[:, tokens], start=(k == 0), stop=False)
                            pe.matmul(out_b, w_hi[:, k, cols], h_lo_[:, tokens], start=False, stop=False)
                            mm = pe.matmul(out_b, w_lo[:, k, cols], h_hi_[:, tokens], start=False, stop=(k == KD - 1))
                            if b == 1 and k == KD - 1:
                                mm.then_inc(group_done, 1)

                def ffn(f, i):
                    first_projections((("a", f, 0), ("a", f, 1)), ("upa", f, 0), i)
                    for j in range(5):
                        for kind, part in (("upa", "a"), ("upb", "b")):
                            for q in range(2):
                                if j or kind == "upb":
                                    project((part, f, 2 * j + q), (kind, f, j), q)
                    project(("a", f, 10), ("upab", f), 0)
                    project(("b", f, 10), ("upab", f), 1)

                    def u_chunk(k):
                        if k % 2 == 0:
                            pe.wait_ge(u_lo_ready, l * 22 + (11 * f + k // 2 + 1))

                    for c in range(KD):
                        three_passes(("dn", f, c), ("dn", f, c), 0, u_hi, u_lo, 1, u_chunk if c == 0 else None)
                    if f == 0:
                        next_norm(3 * l + 1, 7, ("lru", 0), ("proj", 1), l)
                    else:
                        next_norm(3 * l + 3, 7, ("a", 0, 0), ("upa", 0, 0), l + 1)

                ffn(0, 0)

                for i in (1, 2):
                    for q in range(2):
                        if i == 1:
                            if q == 0:
                                first_projections((("lru", 0), ("lru", 1)), ("proj", 1), 1)
                        else:
                            project(("lru", 2 * (i - 1) + q), ("proj", i), q)
                project(("lru", 4), ("proj", 3), 0)
                project(("gelu", 0), ("proj", 3), 1)
                for q in range(2):
                    project(("pool", q), ("proj", 0), q)

                def per_head(name, w, first, src, heads):
                    dst = open_group(name)
                    for b, hd in enumerate(heads):
                        mm = pe.matmul(dst[:, S * b:S * (b + 1)], w[:, first + hd, :], src[:, hd, :],
                                       start=True, stop=True)
                    mm.then_inc(group_done, 1)

                w = tile("small", 2 * HEADS + POOLS, P)
                for q in range(5):
                    pe.wait_ge(v_ready, l * 5 + (q + 1))
                    per_head(("ra", q), w, 0, v, (2 * q, 2 * q + 1))
                for q in range(5):
                    per_head(("ix", q), w, HEADS, v, (2 * q, 2 * q + 1))
                pe.wait_ge(pooled_ready, l + 1)
                for q in range(2):
                    per_head(("pmix", q), w, 2 * HEADS, pooled, (2 * q, 2 * q + 1))
                for i in (4, 5):
                    for q in range(2):
                        project(("gelu", 1 + 2 * (i - 4) + q), ("proj", i), q)
                for i in range(4):
                    for q in range(2):
                        project(("g", 2 * i + q), ("proj", 6 + i), q)
                pe.wait_ge(pool_mix_lo_ready, l + 1)
                for q in range(4):
                    three_passes(("pup", q), ("pup", 0), q // 2, pool_mix_hi, pool_mix_lo, 2, first=2 * (q % 2))
                pe.wait_ge(lru_ready, 2 * l + 2)
                for c in range(KD):
                    three_passes(("lup", c), ("lup", c // 2), 0, gel_hi, gel_lo, 1, first=c % 2)

                def z_chunk(k):
                    pe.wait_ge(z_lo_ready, l * 8 + (k + 1))

                for i in range(2):
                    for q in range(2):
                        three_passes(("out", 2 * i + q), ("lout", i), q, z_hi, z_lo, 2,
                                     z_chunk if i == 0 and q == 0 else None)
                next_norm(3 * l + 2, 6, ("a", 1, 0), ("upa", 1, 0), l)

                ffn(1, 2)

            for t in range(TT):
                for c in range(KD):
                    if t == 0:
                        pe.wait_ge(f_h, c + 1)
                    mm = pe.transpose(bank[2 * t + c // 4][:, P * (c % 4):P * (c % 4 + 1)], h[:, c, P * t:P * (t + 1)],
                                      ident[:])
                    if c % 4 == 3:
                        mm.then_inc(outT_done, 1)

        @block.scalar
        def _(act):
            step = Steps(act, act_first)
            def root(b, n):
                act.wait_ge(ms_done, n)
                act.activation(std[:, 0:TT], both_tokens(b), ACT.Sqrt, bias=EPS).then_inc(std_ready, 1)

            act.wait_ge(cols_ready, 1)
            act.activation(silu_c, first_cols[:, fo["c"]:fo["c"] + KD].unsqueeze(2).broadcast_to([P, KD, 32]),
                           ACT.Silu).then_inc(silu_c_ready, 1)
            for b in range(4):
                act.wait_ge(x_ready, b + 1)
                act.activation(h[:, 2 * b:2 * b + 2, :], x[:, 2 * b:2 * b + 2, :], ACT.Square).then_inc(sq_ready, 1)
            root(5, 1)

            def split_first(name, units=(0, 1)):
                before, none_before = first_splits.before(name)
                if not none_before:
                    act.wait_ge(tile_done[ring_plan.slot(before)], ring_plan.done(before))
                act.wait_ge(loaded[ring_plan.slot(name)], ring_plan.loaded(name))
                for unit in units:
                    act.copy(hi_unit(name, unit), raw_unit(name, unit)).then_inc(first_hi_ready, 1)

            split_first(("win", 0), (0,))
            act.wait_ge(gains_ready, 1)
            act.wait_ge(scaled_ready, 1)
            for k in range(KD):
                act.activation(h_hi[:, k, :], mixin[:, k, :], ACT.Identity, scale=gains[:, 0, k:k + 1],
                               bias=mod[:, k:k + 1]).then_inc(h_ready, 1)
            split_first(("win", 0), (1,))
            split_first(("win", 1))
            act.wait_ge(softexp_ready, 1)
            act.activation(soft[:, 1, :], soft[:, 0, :], ACT.Exp, scale=-1.0).then_inc(softexp_ready, 1)

            def decay_exp(hd):
                act.wait_ge(dret_arg, hd + 1)
                act.activation(dret[:, hd, :], dret[:, hd, :], ACT.Exp).then_inc(dret_ready, 1)

            act.wait_ge(consts_ready, 2)
            half = P // 2
            for i, (dst, func) in enumerate(((None, None), (rv_, ACT.Copy), (rg_, ACT.Silu), (None, None),
                                             (ak_, ACT.Copy), (av_, ACT.Copy))):
                name = ("win", i)
                act.wait_ge(tile_done[ring_plan.slot(name)], ring_plan.done(name))
                src = two_banks[i % 2]
                if i == 0:
                    act.activation(rqk_[:, 0:512], src[:, 0:512], ACT.Copy)
                    k_src = src[:, 512:1024].rearrange("p (c t) -> p c t", c=2)
                    act.mul(rk[0][0:half], k_src[0:half], QK_SCALE)
                    act.mul(rk[1][half:P], k_src[half:P], QK_SCALE).then_inc(proj_ready, 1)
                elif i == 3:
                    q_src = src.rearrange("p (c t) -> p c t", c=4)
                    act.mul(aq[0][0:half], q_src[0:half], QK_SCALE)
                    act.mul(aq[1][half:P], q_src[half:P], QK_SCALE).then_inc(proj_ready, 1)
                else:
                    act.activation(dst, src, func).then_inc(proj_ready, 1)
                if i + 2 < 6:
                    split_first(("win", i + 2))
                elif i == 4:
                    split_first(("wout", 0))
                if i < 2:
                    decay_exp(2 * i)
                    decay_exp(2 * i + 1)

            def att_softmax(hd):
                act.wait_ge(att_max_ready, hd + 1)
                for t in range(TT):
                    ins = act.activation(s_att[:, hd % 2, t, :], s_att[:, hd % 2, t, :], ACT.Exp,
                                         bias=att_max[:, hd % 2, t:t + 1])
                ins.then_inc(att_exp, 1)

            att_softmax(0)
            att_softmax(1)
            for b in range(2):
                act.wait_ge(ret_done, 2 * b + 2)
                act.copy(gn_[:, 512 * b:512 * (b + 1)], two_banks[0][:, 512 * b:512 * (b + 1)]).then_inc(ret_copied, 1)
            for b in range(2):
                act.wait_ge(centred_ready, b + 1)
                act.activation(gsq_[:, 512 * b:512 * (b + 1)], gn_[:, 512 * b:512 * (b + 1)], ACT.Square).then_inc(gsq_ready, 1)

            def att_copy(hd):
                act.wait_ge(att_pT_done, hd + 1)
                if hd >= 1:
                    act.wait_ge(att_done, hd)
                act.copy(patt_, bank[6]).then_inc(att_pT_ready, 1)

            def att_out(half):
                act.wait_ge(att_done, 4 * half + 4)
                part = slice(1024 + 512 * half, 1024 + 512 * (half + 1))
                act.copy(x_tok_[:, part], bank[2 + half])
                act.copy(mixin_hi[:, part], bank[2 + half]).then_inc(mixin_hi_ready, 1)

            def att_weights(hd):
                act.wait_ge(att_inv_ready, hd + 1)
                for t in range(TT):
                    ins = act.mul(p_att[:, hd % 2, t, :], p_att[:, hd % 2, t, :], att_inv[:, hd % 2, t:t + 1])
                ins.then_inc(att_p_ready, 1)

            att_weights(0)
            for hd in range(ATT_HEADS):
                att_copy(hd)
                if hd + 1 < ATT_HEADS:
                    att_weights(hd + 1)
                if hd + 2 < ATT_HEADS:
                    att_softmax(hd + 2)
                if hd == 5:
                    act.wait_ge(gvar_done, 1)
                    act.activation(std[:], two_banks[0][:, 0:8], ACT.Sqrt, bias=GN_EPS).then_inc(gstd_ready, 1)
                if hd in (1, 2):
                    split_first(("wout", 1), (hd - 1,))
                if hd == 7:
                    act.wait_ge(yret_ready, 2)
                    act.copy(mixin_hi[:, 0:1024], x_tok_[:, 0:1024]).then_inc(mixin_hi_ready, 1)
                if hd == 4:
                    att_out(0)
            att_out(1)

            for b in range(4):
                name = ("wout", b // 2)
                act.wait_ge(tile_done[ring_plan.slot(name)], ring_plan.done(name))
                act.activation(h[:, 2 * b:2 * b + 2, :].rearrange("p c t -> p (c t)"),
                               two_banks[b // 2][:, 512 * (b % 2):512 * (b % 2 + 1)], ACT.Square).then_inc(sq_ready, 1)
            root(5, 2)
            for b in range(4):
                act.wait_ge(x_ready, 4 + 2 * b + 2)
                act.activation(h[:, 2 * b:2 * b + 2, :], x[:, 2 * b:2 * b + 2, :], ACT.Square).then_inc(sq_ready, 1)
            root(5, 3)
            act.wait_ge(gains_ready, 2)
            for k in range(KD):
                act.wait_ge(scaled_ready, k + 2)
                act.activation(h[:, k, :], h[:, k, :], ACT.Identity, scale=gains[:, 2, k:k + 1],
                               bias=mod[:, 24 + k:25 + k]).then_inc(h_ready, 1)

            act.activation(table[:], mean_d[:], ACT.Exp)

            act.wait_ge(lmax_ready, 1)
            for t in range(TT):
                ins = act.activation(aff[:, t, :], bank[4 + 2 * t][:, 0:E], ACT.Exp, bias=lmax[:, t:t + 1],
                                     accum_out=lsum[:, t:t + 1])
            ins.then_inc(lexp_ready, 1)
            for b in range(4):
                act.wait_ge(htokT_done, b + 1)
                act.copy(h_tok[:, b // 2, 512 * (b % 2):512 * (b % 2 + 1)], bank[b]).then_inc(htok_ready, 1)
            act.sem_inc(y_ready, 1)
            act.sem_inc(gT_ready, 1)

            with act.Fori(0, E) as e:
                act.wait_ge(gT_done, e + 1)
                act.copy(gT_, bank[3][:, 0:S]).then_inc(gT_ready, 1)
                name = ("gate", FB - 1)
                act.wait_ge(tile_done[ring_plan.slot(name)], ring_plan.done(name, e))
                act.activation(silu_gate, bank[0], ACT.Silu).then_inc(silu_ready, 1)
                act.wait_ge(hiddenT_done, e + 1)
                act.copy(hT_, bank[2]).then_inc(hiddenT_ready, 1)
                name = ("down", FB - 1)
                act.wait_ge(tile_done[ring_plan.slot(name)], ring_plan.done(name, e))
                act.copy(y_part, two_banks[1]).then_inc(y_ready, 1)

            def split(name, turn):
                before, in_last_layer = splits.before(name)
                if in_last_layer:
                    s = SPLIT_SLOTS + splits.hi_slot(name)
                    act.wait_ge(tile_done[s], ring_plan.end_of_experts[s])
                value = groups.done(last_group[before], turn)
                act.wait_ge(group_done, value - groups.total if in_last_layer else value)
                act.wait_ge(loaded[ring_plan.slot(name)], ring_plan.loaded(name, turn))
                for unit in range(dict(splits.tiles)[name]):
                    act.copy(hi_unit(name, unit), raw_unit(name, unit)).then_inc(hi_ready, 1)

            split(("upa", 0, 0), 0)
            act.activation(table[:], mean_d[:], ACT.Sqrt)
            act.wait_ge(moe_done, E)
            for b in range(4):
                act.activation(h[:, 2 * b:2 * b + 2, :], moe_acc[:, 2 * b:2 * b + 2, :], ACT.Square).then_inc(sq_ready, 1)
            root(0, 4)

            def square(k):
                act.activation(h[:, k, :], x[:, k, :], ACT.Square).then_inc(l_sq, 1)

            def layer_root(n, b=6):
                act.wait_ge(l_ms, n + 1)
                act.activation(std[:, 0:TT], both_tokens(b), ACT.Sqrt, bias=EPS).then_inc(l_std, 1)

            for k in range(KD):
                act.wait_ge(x_moe_ready, k + 1)
                square(k)
            layer_root(0, 0)
            act.sem_inc(emptied["act"], groups.per["act"])

            with act.Fori(0, LAYERS) as l:
                step = Steps(act, act_layer, 1, l)

                def done(name):
                    act.wait_ge(group_done, groups.done(name, l))
                    return bank[groups.bank(name)]

                def wait_emptied(name):
                    e, n = groups.emptied(name, l)
                    act.wait_ge(emptied[e], n)

                def h_high(i):
                    for k in range(KD):
                        act.wait_ge(h_scaled, l * 24 + (8 * i + k + 1))
                        act.copy(h_hi[:, k, :], h[:, k, :]).then_inc(h_hi_ready, 1)

                def ffn(f, i, after):
                    def silu(j):
                        src = done(("a", f, j))
                        if j >= 4:
                            wait_emptied(("b", f, j - 4))
                        act.activation(silu_a[:, j % 4, :], src, ACT.Silu).then_inc(emptied["act"], 1)

                    def u_high(j):
                        wait_emptied(("b", f, j))
                        act.copy(u_hi[:, 512 * j:512 * (j + 1)], u_[:, 512 * j:512 * (j + 1)]).then_inc(u_hi_ready, 1)

                    h_high(i)
                    for j in range(5):
                        split(("upb", f, j), l)
                        if j:
                            u_high(2 * j - 2)
                            u_high(2 * j - 1)
                        silu(2 * j)
                        silu(2 * j + 1)
                        split(("upa", f, j + 1) if j < 4 else ("upab", f), l)
                    split(("dn", f, 0), l)
                    u_high(8)
                    u_high(9)
                    silu(10)
                    act.activation(table[:], mean_d[:], ACT.Sqrt)
                    u_high(10)
                    for c in range(KD):
                        if c + 1 < KD:
                            split(("dn", f, c + 1), l)
                        elif after:
                            split(after, l + 1 if f else l)
                        if c:
                            wait_emptied(("dn", f, c - 1))
                            square(c - 1)
                    wait_emptied(("dn", f, KD - 1))
                    square(KD - 1)
                    layer_root(3 * l + (i + 1))

                ffn(0, 0, ("proj", 1))

                cw, cb = lo["conv_w"], lo["conv_b"]

                def lru_input(g):
                    src = done(("lru", g))
                    act.copy(upad[:, 2 * g:2 * g + 2, TAPS - 1:], src.rearrange("p (c t) -> p c t", c=2))
                    for b in range(2):
                        c = 2 * g + b
                        ins = act.activation(v[:, c, :], src[:, S * b:S * (b + 1)], ACT.Identity,
                                             scale=lc[:, cw + 3 * HEADS + c:cw + 3 * HEADS + c + 1],
                                             bias=lc[:, cb + c:cb + c + 1])
                    ins.then_inc(emptied["act"], 1)

                def gelu(g):
                    src = done(("gelu", g))
                    act.activation(gel_[:, 512 * g:512 * (g + 1)], src, ACT.Gelu_apprx_tanh).then_inc(emptied["act"], 1)

                def gate(g):
                    src = done(("g", g))
                    act.activation(gs_[:, 512 * g:512 * (g + 1)], src, ACT.Sigmoid).then_inc(emptied["act"], 1)

                h_high(1)
                split(("proj", 2), l)
                lru_input(0)
                lru_input(1)
                split(("proj", 3), l)
                lru_input(2)
                lru_input(3)
                split(("proj", 0), l)
                lru_input(4)
                gelu(0)
                for g in range(2):
                    src = done(("pool", g))
                    act.copy(pool_u[:, 2 * g:2 * g + 2, 16:], src.rearrange("p (c t) -> p c t", c=2)).then_inc(emptied["act"], 1)
                split(("proj", 4), l)
                for part, dst, b0 in (("ra", rgate, lo["lru_b_a"]), ("ix", igate, lo["lru_b_x"])):
                    for g in range(5):
                        src = done((part, g))
                        for b in range(2):
                            c = 2 * g + b
                            ins = act.activation(dst[:, c, :], src[:, S * b:S * (b + 1)], ACT.Sigmoid,
                                                 bias=lc[:, b0 + c:b0 + c + 1])
                        ins.then_inc(emptied["act"], 1)
                split(("proj", 5), l)
                wait_emptied(("ra", 4))
                for c in range(HEADS):
                    ins = act.activation(decay[:, c, :], rgate[:, c, :], ACT.Exp, scale=lc[:, n_layer + c:n_layer + c + 1])
                step(ins)
                gelu(1)
                gelu(2)
                split(("proj", 6), l)
                for c in range(HEADS):
                    ins = act.activation(rgate[:, c, :], rgate[:, c, :], ACT.Tanh,
                                         scale=lc[:, n_layer + HEADS + c:n_layer + HEADS + c + 1])
                ins.then_inc(decay_ready, 1)
                gelu(3)
                gelu(4)
                split(("proj", 7), l)
                gate(0)
                gate(1)
                split(("proj", 8), l)
                act.wait_ge(m2_ready, l + 1)
                act.activation(r_, r_, ACT.Sqrt).then_inc(mult_ready, 1)
                gate(2)
                gate(3)
                split(("proj", 9), l)
                gate(4)
                gate(5)
                split(("pup", 0), l)
                wait_emptied(("pmix", 1))
                act.wait_ge(scan_done, l + 1)
                act.copy(pool_mix_hi, pool_mix.rearrange("p c t -> p (c t)")).then_inc(pool_mix_hi_ready, 1)
                gate(6)
                gate(7)
                split(("lup", 0), l)
                act.wait_ge(lru_ready, 2 * l + 1)
                act.copy(gel_hi, gel_).then_inc(gel_hi_ready, 1)

                def z_high(c):
                    act.wait_ge(z_ready, l * 8 + (c + 1))
                    act.copy(z_hi[:, S * c:S * (c + 1)], gs[:, 8 + c, :]).then_inc(z_hi_ready, 1)

                for i in range(4):
                    split(("lup", i + 1) if i < 3 else ("lout", 0), l)
                    if i:
                        z_high(2 * i - 2)
                        z_high(2 * i - 1)
                z_high(6)
                z_high(7)
                split(("lout", 1), l)
                for i in range(2):
                    if i:
                        split(("upa", 1, 0), l)
                    for q in (2 * i, 2 * i + 1):
                        wait_emptied(("out", q))
                        square(2 * q)
                        square(2 * q + 1)
                layer_root(3 * l + 2)

                ffn(1, 2, ("upa", 0, 0))

            for t in range(TT):
                act.wait_ge(outT_done, 2 * t + 1)
                act.copy(out_tok[:, t, 0:512], bank[2 * t]).then_inc(out_ready_act, 1)

        @block.vector
        def _(dve):
            step = Steps(dve, dve_first)
            relf, relint = rel, reli.bitcast(I32)

            dve.wait_ge(rel_ready, 1)
            step(dve.scalar_tensor_tensor(out=dist, in0=relf, scalar=-1.0, in1=relf, op0=ALU.mult, op1=ALU.max))
            step(dve.tensor_scalar(mult_, dist, float(NEAR), None, ALU.is_le))
            for dilation in (4, 16):
                step(dve.tensor_scalar(keep.bitcast(I32), relint, dilation - 1, None, ALU.bitwise_and))
                step(dve.scalar_tensor_tensor(out=mult_, in0=keep.bitcast(I32), scalar=0.0, in1=mult_,
                                              op0=ALU.is_equal, op1=ALU.add))
            step(dve.tensor_scalar(negdist_, mult_, 0.0, NEG, ALU.is_equal, ALU.mult))
            step(dve.tensor_tensor(negdist_, negdist_, dist, ALU.subtract))

            step(dve.tensor_reduce(first_rows, ident[:, 0::32], AX.X, ALU.add))
            dve.wait_ge(colsT_done, 1)
            dve.tensor_copy(first_cols[:], bank[0][:, 0:n_first]).then_inc(cols_ready, 1)
            for b in range(4):
                dve.wait_ge(xT_done, b + 1)
                dve.tensor_copy(x[:, 2 * b:2 * b + 2, :].rearrange("p c t -> p (c t)"), bank[1 + b]).then_inc(x_ready, 1)

            def modulation(i):
                half = mod_bank(i)
                name = ("ada", i)
                dve.wait_ge(tile_done[ring_plan.slot(name)], ring_plan.done(name))
                if i >= 2:
                    dve.wait_ge(modT_done, i - 1)
                dve.tensor_copy(modrow[i % 2], half.rearrange("p (b n) -> p b n", b=2)).then_inc(modrow_ready, 1)

            def modulation_columns(i):
                half = mod_bank(i)
                dve.wait_ge(modT_done, i + 1)
                at = fo["b_ada"] + 4 * i
                dve.tensor_tensor(mod[:, 4 * i:4 * i + 4], half[:, 0:4], first_cols[:, at:at + 4],
                                  ALU.add).then_inc(mod_ready, 1)

            def inverse_root(n, at):
                dve.wait_ge(std_ready, n)
                dve.reciprocal(rstd_col[:, 0:TT], std[:, 0:TT]).then_inc(rstd_ready, 1)
                dve.wait_ge(rstd_spread, n)
                return at[:, 0:S]

            def split_first(name, units=(0, 1)):
                for unit in units:
                    dve.wait_ge(first_hi_ready, first_splits.ready(name, unit, 0))
                    dve.tensor_tensor(lo_unit(name, unit), raw_unit(name, unit), hi_unit(name, unit).bitcast(F32),
                                      ALU.subtract).then_inc(first_lo_ready, 1)

            rstd = inverse_root(1, bank[5])
            dve.wait_ge(x_ready, 4)
            dve.tensor_tensor(mixin, x[:], rstd.unsqueeze(1).broadcast_to([P, KD, S]), ALU.mult).then_inc(scaled_ready, 1)
            for i in range(4):
                modulation(i)
                modulation_columns(i)
            dve.wait_ge(mod_ready, 4)
            dve.scalar_tensor_tensor(out=gains[:, 0, :], in0=mod[:, 8:16], scalar=1.0,
                                     in1=first_cols[:, fo["g_pre_mix"]:fo["g_pre_mix"] + KD], op0=ALU.add,
                                     op1=ALU.mult).then_inc(gains_ready, 1)
            dve.wait_ge(gains_ready, 1)
            dve.wait_ge(scaled_ready, 1)
            for k in range(KD):
                step(dve.tensor_scalar(h[:, k, :], mixin[:, k, :], gains[:, 0, k:k + 1], mod[:, k:k + 1], ALU.mult, ALU.add))
                if k == 0:
                    split_first(("win", 0), (0,))
                dve.wait_ge(h_ready, k + 1)
                dve.tensor_tensor(h_lo[:, k, :], h[:, k, :], h_hi[:, k, :].bitcast(F32), ALU.subtract).then_inc(first_h_lo, 1)
            split_first(("win", 0), (1,))
            split_first(("win", 1))

            dve.wait_ge(layer_colsT_done, 1)
            for l in range(LAYERS):
                step(dve.tensor_copy(layer_cols[:, n_layer * l:n_layer * (l + 1)],
                                     bank[5][:, S + P * l:S + P * l + n_layer]))
            dve.wait_ge(misc_loaded, 48)
            for l in range(LAYERS):
                at = n_layer * l + lo["lru_lambda"]
                step(dve.tensor_copy(decay_in[:, 8 + HEADS * l:8 + HEADS * (l + 1)], layer_cols[:, at:at + HEADS]))
            dve.scalar_tensor_tensor(out=soft[:, 0, :], in0=decay_in[:], scalar=-1.0, in1=decay_in[:],
                                     op0=ALU.mult, op1=ALU.max).then_inc(softexp_ready, 1)
            dve.wait_ge(softexp_ready, 2)
            step(dve.tensor_scalar(soft[:, 2, :], soft[:, 1, :], 2.0, None, ALU.add))
            step(dve.reciprocal(soft[:, 3, :], soft[:, 2, :]))
            step(dve.tensor_tensor(soft[:, 2, :], soft[:, 1, :], soft[:, 3, :], ALU.mult))
            step(dve.tensor_tensor(soft[:, 3, :], soft[:, 2, :], soft[:, 2, :], ALU.mult))
            step(dve.tensor_scalar(soft[:, 4, :], soft[:, 3, :], 1.0 / 19.0, None, ALU.mult))
            for n in (17, 15, 13, 11, 9, 7, 5, 3):
                step(dve.scalar_tensor_tensor(out=soft[:, 4, :], in0=soft[:, 4, :], scalar=1.0 / n, in1=soft[:, 3, :],
                                              op0=ALU.add, op1=ALU.mult))
            step(dve.scalar_tensor_tensor(out=soft[:, 4, :], in0=soft[:, 4, :], scalar=1.0, in1=soft[:, 2, :],
                                          op0=ALU.add, op1=ALU.mult))
            step(dve.tensor_scalar(soft[:, 5, :], decay_in[:], -1.0, 0.0, ALU.mult, ALU.max))
            step(dve.scalar_tensor_tensor(out=soft[:, 5, :], in0=soft[:, 4, :], scalar=2.0, in1=soft[:, 5, :],
                                          op0=ALU.mult, op1=ALU.add))
            sp = soft[:, 5, :]
            step(dve.tensor_scalar(nsp8[:, 0, :], sp[:, 8:], -LRU_C, None, ALU.mult))
            step(dve.tensor_scalar(nsp8[:, 1, :], sp[:, 8:], LRU_C, None, ALU.mult))
            def decay_log(hd):
                if hd:
                    dve.wait_ge(dret_arg, hd)
                step(dve.tensor_scalar(dist, relf, 0.0, sp[:, hd:hd + 1], ALU.max, ALU.mult))
                step(dve.tensor_scalar(dret[:, hd, :], relf, 0.0, sp[:, 4 + hd:5 + hd], ALU.min, ALU.mult))
                dve.tensor_tensor(dret[:, hd, :], dret[:, hd, :], dist, ALU.subtract).then_inc(dret_arg, 1)

            for i in range(2, 6):
                if i < 4:
                    decay_log(2 * (i - 2))
                    decay_log(2 * (i - 2) + 1)
                split_first(("win", i))
                if i > 2:
                    modulation_columns(1 + i)
                modulation(2 + i)
            split_first(("wout", 0))
            modulation_columns(7)
            modulation(8)
            modulation_columns(8)
            dve.wait_ge(consts_ready, 2)
            for g, w in enumerate(POOL_WINDOWS):
                step(dve.tensor_scalar(pool_fix[:, g, :], pool_fix[:, g, :], float(w), None, ALU.min))
            step(dve.reciprocal(inv_count[:], pool_fix[:]))

            def ret_decay(hd):
                dve.wait_ge(ret_scored, hd + 1)
                if hd >= 2:
                    dve.wait_ge(ret_done, hd - 1)
                dve.tensor_tensor(pret[:, hd % 2].rearrange("p s t -> p (s t)"), bank[4 + hd % 2], dret[:, hd, :],
                                  ALU.mult).then_inc(pret_ready, 1)

            def att_scores(hd):
                dve.wait_ge(att_scored, hd + 1)
                sc = s_att[:, hd % 2].rearrange("p t s -> p (t s)")
                step(dve.scalar_tensor_tensor(out=sc, in0=negdist_, scalar=2.0 ** -(hd + 1), in1=score_bank(hd),
                                              op0=ALU.mult, op1=ALU.add))
                dve.tensor_reduce(att_max[:, hd % 2, :], s_att[:, hd % 2], AX.X, ALU.max,
                                  negate=True).then_inc(att_max_ready, 1)

            def att_sums(hd):
                dve.wait_ge(att_exp, hd + 1)
                if hd >= 2:
                    dve.wait_ge(att_pT_done, hd - 1)
                for t in range(TT):
                    ins = dve.tensor_tensor_reduce(p_att[:, hd % 2, t, :], s_att[:, hd % 2, t, :], mult_[:, S * t:S * (t + 1)],
                                                   1.0, 0.0, ALU.mult, ALU.add, att_sum[:, hd % 2, t:t + 1])
                step(ins)
                dve.reciprocal(att_inv[:, hd % 2, :], att_sum[:, hd % 2, :]).then_inc(att_inv_ready, 1)

            def mixin_low(first, end, n):
                dve.wait_ge(mixin_hi_ready, n)
                dve.tensor_tensor(mixin_lo[:, first:end], x_tok_[:, first:end], mixin_hi[:, first:end].bitcast(F32),
                                  ALU.subtract).then_inc(mixin_lo_ready, 1)

            dve.wait_ge(dret_ready, RET_HEADS)
            ret_decay(0)
            ret_decay(1)
            att_scores(0)
            ret_decay(2)
            att_scores(1)
            ret_decay(3)
            att_sums(0)
            dve.wait_ge(gmean_done, 1)
            for b in range(2):
                dve.wait_ge(ret_copied, b + 1)
                dve.tensor_tensor(gn_[:, 512 * b:512 * (b + 1)], gn_[:, 512 * b:512 * (b + 1)],
                                  two_banks[1][:, 512 * b:512 * (b + 1)], ALU.subtract).then_inc(centred_ready, 1)
            for hd in range(ATT_HEADS):
                if hd + 1 < ATT_HEADS:
                    att_sums(hd + 1)
                if hd + 2 < ATT_HEADS:
                    att_scores(hd + 2)
                if hd in (0, 2, 4):
                    modulation(9 + hd // 2)
                    modulation_columns(9 + hd // 2)
                if hd == 5:
                    dve.wait_ge(gstd_ready, 1)
                    dve.reciprocal(rstd_col[:], std[:]).then_inc(grstd_ready, 1)
                if hd == 6:
                    dve.wait_ge(grstd_spread, 1)
                    dve.tensor_tensor(gn_, gn_, two_banks[0], ALU.mult).then_inc(yret_ready, 1)
                    dve.wait_ge(yret_ready, 1)
                    dve.tensor_tensor(x_tok_[:, 0:1024], gn_, rg_, ALU.mult).then_inc(yret_ready, 1)
                if hd in (2, 3):
                    split_first(("wout", 1), (hd - 2,))
                if hd == 5:
                    mixin_low(1024, 1536, 1)
                if hd == 7:
                    mixin_low(0, 1024, 2)
            mixin_low(1536, 2048, 3)

            def gain(i, at, name, plus):
                return dve.scalar_tensor_tensor(out=gains[:, i, :], in0=mod[:, at:at + KD], scalar=plus,
                                                in1=first_cols[:, fo[name]:fo[name] + KD], op0=ALU.add, op1=ALU.mult)

            dve.wait_ge(mod_ready, 12)
            step(gain(1, 16, "g_post_mix", 0.0))
            gain(2, 32, "g_pre_ffn", 1.0).then_inc(gains_ready, 1)
            step(gain(3, 40, "g_post_ffn", 0.0))

            step(dve.tensor_copy(rstd_row[:], inverse_root(2, bank[5])))
            for b in range(2):
                step(dve.tensor_tensor(mix[:, 4 * b:4 * b + 4, :], two_banks[b].rearrange("p (c t) -> p c t", c=4),
                                       rstd_row[:].unsqueeze(1).broadcast_to([P, 4, S]), ALU.mult))
                for k in range(4 * b, 4 * b + 4):
                    dve.scalar_tensor_tensor(out=x[:, k, :], in0=mix[:, k, :], scalar=gains[:, 1, k:k + 1], in1=x[:, k, :],
                                             op0=ALU.mult, op1=ALU.add).then_inc(x_ready, 1)
            rstd = inverse_root(3, bank[5])
            dve.wait_ge(x_ready, 4 + KD)
            for k in range(KD):
                dve.tensor_tensor(h[:, k, :], x[:, k, :], rstd, ALU.mult).then_inc(scaled_ready, 1)

            step(dve.memset(ones_e, 1.0))
            step(dve.memset(zeros, 0.0))
            dve.wait_ge(logits_done, 1)
            dve.tensor_reduce(lmax, psum[:, 2048:4096].rearrange("p (t n) -> p t n", t=TT)[:, :, 0:E], AX.X, ALU.max,
                              negate=True).then_inc(lmax_ready, 1)
            dve.wait_ge(lexp_ready, 1)
            step(dve.reciprocal(linv, lsum))
            for t in range(TT):
                ins = dve.tensor_scalar(aff[:, t, :], aff[:, t, :], linv[:, t:t + 1], None, ALU.mult)
            ins.then_inc(aff_ready, 1)
            dve.wait_ge(affT_done, 1)
            step(dve.tensor_copy(affT, bank[5][0:E, 0:S]))
            now, then = affT, affW
            for r in range(CAP // 8):
                best = top[:, 8 * r:8 * r + 8]
                step(dve.max(best, now))
                step(dve.max_index(topi[:, 8 * r:8 * r + 8], best, now))
                if r + 1 < CAP // 8:
                    step(dve.match_replace(then, best, now, -1.0))
                    now, then = then, now
            step(dve.tensor_copy(topf, topi))
            dve.tensor_tensor(spread, ident[0:E, 0:E].unsqueeze(2).broadcast_to([E, E, CAP]),
                              topf.unsqueeze(1).broadcast_to([E, E, CAP]), ALU.mult).then_inc(spread_ready, 1)
            dve.wait_ge(index_done, 1)
            for t in range(TT):
                ins = dve.tensor_scalar(onehot[:, t, :], bank[6], t_col[:, t:t + 1], None, ALU.is_equal)
            ins.then_inc(onehot_ready, 1)
            dve.wait_ge(onehot_ready, 1)
            dve.wait_ge(aff_ready, 1)

            with dve.Fori(0, E) as e:
                dve.wait_ge(gT_ready, e + 1)
                dve.tensor_tensor(weighted_.rearrange("p (t g c) -> p t g c", t=TT, g=4),
                                  onehot[:, :, bass.ds(e * CAP, CAP)].unsqueeze(2).broadcast_to([P, TT, 4, CAP]),
                                  aff[:, :, bass.ds(e, 1)].unsqueeze(3).broadcast_to([P, TT, 4, CAP]),
                                  ALU.mult).then_inc(weighted_ready, 1)
                dve.wait_ge(xe_done, e + 1)
                dve.tensor_copy(xe_, bank[2][:, 0:KD * CAP]).then_inc(xe_ready, 1)
                name = ("up", FB - 1)
                dve.wait_ge(tile_done[ring_plan.slot(name)], ring_plan.done(name, e))
                dve.wait_ge(silu_ready, e + 1)
                dve.tensor_tensor(hidden, silu_gate, bank[1], ALU.mult).then_inc(hidden_ready, 1)

            def split(name, turn):
                for unit in range(dict(splits.tiles)[name]):
                    dve.wait_ge(hi_ready, splits.ready(name, unit, turn))
                    dve.tensor_tensor(lo_unit(name, unit), raw_unit(name, unit), hi_unit(name, unit).bitcast(F32),
                                      ALU.subtract).then_inc(lo_ready, 1)

            split(("upa", 0, 0), 0)
            step(dve.tensor_copy(rstd_row[:], inverse_root(4, bank[0])))
            for b in range(2):
                half = y_part.rearrange("p (c t) -> p c t", c=4)
                if b:
                    dve.wait_ge(x_moe_ready, 4)
                step(dve.tensor_tensor(half, moe_acc[:, 4 * b:4 * b + 4, :],
                                       rstd_row[:].unsqueeze(1).broadcast_to([P, 4, S]), ALU.mult))
                for k in range(4 * b, 4 * b + 4):
                    dve.scalar_tensor_tensor(out=x[:, k, :], in0=half[:, k % 4, :], scalar=gains[:, 3, k:k + 1],
                                             in1=x[:, k, :], op0=ALU.mult, op1=ALU.add).then_inc(x_moe_ready, 1)
            dve.wait_ge(x_moe_ready, KD)
            dve.sem_inc(emptied["dve"], groups.per["dve"])


            def add_square(n, k, last):
                dve.wait_ge(l_sq, KD * n + (k + 1))
                ins = dve.tensor_tensor(h[:, 0, :], h[:, 0, :], h[:, k, :], ALU.add)
                if k == last:
                    ins.then_inc(l_sum, 1)
                else:
                    step(ins)

            with dve.Fori(0, LAYERS) as l:
                step = Steps(dve, dve_layer, 31, l)

                def done(name):
                    dve.wait_ge(group_done, groups.done(name, l))
                    return bank[groups.bank(name)]

                def wait_emptied(name):
                    e, n = groups.emptied(name, l)
                    dve.wait_ge(emptied[e], n)

                def norm(i, at):
                    dve.wait_ge(l_std, 3 * l + (i + 1))
                    dve.reciprocal(rstd_col[:, 0:TT], std[:, 0:TT]).then_inc(l_rstd, 1)
                    dve.wait_ge(l_spread, 3 * l + (i + 1))
                    rstd = bank[7][:, 0:S]
                    for k in range(KD + 1):
                        if k < KD:
                            dve.scalar_tensor_tensor(out=h[:, k, :], in0=x[:, k, :], scalar=lc[:, at + k:at + k + 1],
                                                     in1=rstd, op0=ALU.mult, op1=ALU.mult).then_inc(h_scaled, 1)
                        if k:
                            dve.wait_ge(h_hi_ready, l * 24 + (8 * i + k))
                            dve.tensor_tensor(h_lo[:, k - 1, :], h[:, k - 1, :], h_hi[:, k - 1, :].bitcast(F32),
                                              ALU.subtract).then_inc(h_lo_ready, 1)

                def ffn(f, i, at, after):
                    def gated(j):
                        src = done(("b", f, j))
                        wait_emptied(("a", f, j))
                        dve.tensor_tensor(u_[:, 512 * j:512 * (j + 1)], src, silu_a[:, j % 4, :],
                                          ALU.mult).then_inc(emptied["dve"], 1)

                    def u_low(j):
                        dve.wait_ge(u_hi_ready, l * 22 + (11 * f + j + 1))
                        part = slice(512 * j, 512 * (j + 1))
                        dve.tensor_tensor(u_lo[:, part], u_[:, part], u_hi[:, part].bitcast(F32),
                                          ALU.subtract).then_inc(u_lo_ready, 1)

                    norm(i, at)
                    for j in range(5):
                        split(("upb", f, j), l)
                        if j:
                            u_low(2 * j - 2)
                            u_low(2 * j - 1)
                        split(("upa", f, j + 1) if j < 4 else ("upab", f), l)
                        gated(2 * j)
                        gated(2 * j + 1)
                    split(("dn", f, 0), l)
                    u_low(8)
                    u_low(9)
                    gated(10)
                    u_low(10)
                    for c in range(KD):
                        if c + 1 < KD:
                            split(("dn", f, c + 1), l)
                        elif after:
                            split(after, l + 1 if f else l)
                        if c >= 2:
                            add_square(3 * l + (i + 1), c - 1, 6)
                        src = done(("dn", f, c))
                        dve.scalar_tensor_tensor(out=x[:, c, :], in0=src[:, 0:S], scalar=0.5, in1=x[:, c, :], op0=ALU.mult,
                                                 op1=ALU.add).then_inc(emptied["dve"], 1)
                    wait_emptied(("dn", f, KD - 1))

                step(dve.tensor_copy(lc[:, 0:n_layer], layer_cols[:, bass.ds(l * n_layer, n_layer)]))
                step(dve.tensor_copy(lc[:, n_layer:n_layer + HEADS], nsp8[:, 0, bass.ds(l * HEADS, HEADS)]))
                dve.tensor_copy(lc[:, n_layer + HEADS:], nsp8[:, 1, bass.ds(l * HEADS, HEADS)]).then_inc(cols_layer, 1)
                dve.wait_ge(cols_layer, l + 1)
                ffn(0, 0, lo["norm_ffn1"], ("proj", 1))

                cw = lo["conv_w"]

                def conv(g):
                    wait_emptied(("lru", g))
                    for k in range(TAPS - 1):
                        for c in (2 * g, 2 * g + 1):
                            ins = dve.scalar_tensor_tensor(
                                out=v[:, c, :], in0=upad[:, c, k:k + S], scalar=lc[:, cw + HEADS * k + c:cw + HEADS * k + c + 1],
                                in1=v[:, c, :], op0=ALU.mult, op1=ALU.add)
                        if k < TAPS - 2:
                            step(ins)
                    ins.then_inc(v_ready, 1)

                norm(1, lo["norm_mix"])
                step(dve.memset(upad[:, :, 0:TAPS - 1], 0.0))
                split(("proj", 2), l)
                conv(0)
                split(("proj", 3), l)
                conv(1)
                conv(2)
                split(("proj", 0), l)
                conv(3)
                conv(4)
                split(("proj", 4), l)
                dve.wait_ge(pool_sums, l + 1)
                sums = (pool_a, pool_b, pool_a, pool_b)
                for g, w in enumerate(POOL_WINDOWS):
                    dve.tensor_tensor(pool_fix[:, g, :], sums[g][:, g, 16:32], inv_count[:, g, :], ALU.mult)
                    ins = dve.scalar_tensor_tensor(out=pooled[:, g, :], in0=sums[g][:, g, 16:], scalar=1.0 / w,
                                                   in1=pool_u[:, g, 16:], op0=ALU.mult, op1=ALU.subtract)
                step(ins)
                dve.tensor_tensor(pooled[:, :, 0:16], pool_fix[:], pool_u[:, :, 16:32], ALU.subtract).then_inc(pooled_ready, 1)
                for g in range(2):
                    src = done(("pmix", g))
                    for b in range(2):
                        c = 2 * g + b
                        ins = dve.tensor_scalar(pool_mix[:, c, :], src[:, S * b:S * (b + 1)],
                                                lc[:, lo["pool_b"] + c:lo["pool_b"] + c + 1],
                                                lc[:, lo["pool_scale"] + c:lo["pool_scale"] + c + 1], ALU.add, ALU.mult)
                    ins.then_inc(emptied["dve"], 1)
                split(("proj", 5), l)
                split(("proj", 6), l)
                dve.wait_ge(decay_ready, l + 1)
                step(dve.tensor_tensor(decay_sq, decay_, decay_, ALU.mult))
                split(("proj", 7), l)
                dve.scalar_tensor_tensor(out=r_, in0=decay_sq, scalar=1.0, in1=r_, op0=ALU.add,
                                         op1=ALU.mult).then_inc(m2_ready, 1)
                step(dve.memset(decay[:, :, 0:1], 0.0))
                split(("proj", 8), l)
                dve.wait_ge(mult_ready, l + 1)
                dve.wait_ge(iv_ready, l + 1)
                step(dve.tensor_tensor(i_, i_, r_, ALU.mult))
                split(("proj", 9), l)
                dve.tensor_tensor_scan(v_, decay_, i_, 0.0, ALU.mult, ALU.add).then_inc(scan_done, 1)
                split(("pup", 0), l)
                dve.wait_ge(pool_mix_hi_ready, l + 1)
                dve.tensor_tensor(pool_mix_lo, pool_mix.rearrange("p c t -> p (c t)"), pool_mix_hi.bitcast(F32),
                                  ALU.subtract).then_inc(pool_mix_lo_ready, 1)
                wait_emptied(("gelu", 4))
                dve.wait_ge(scan_done, l + 1)
                dve.tensor_tensor(gel_, gel_, v_, ALU.mult).then_inc(lru_ready, 1)
                split(("lup", 0), l)
                dve.wait_ge(gel_hi_ready, l + 1)
                dve.tensor_tensor(gel_lo, gel_, gel_hi.bitcast(F32), ALU.subtract).then_inc(lru_ready, 1)
                for q in range(4):
                    src = done(("pup", q))
                    wait_emptied(("g", q))
                    gq = gs_[:, 512 * q:512 * (q + 1)]
                    dve.tensor_tensor(gq, src, gq, ALU.mult).then_inc(emptied["dve"], 1)

                def gated_sum(c):
                    src = done(("lup", c))
                    wait_emptied(("g", 4 + c // 2))
                    dve.tensor_tensor(gs[:, 8 + c, :], src[:, 0:S], gs[:, 8 + c, :], ALU.mult).then_inc(emptied["dve"], 1)
                    wait_emptied(("lup", c))
                    dve.tensor_tensor(gs[:, 8 + c, :], gs[:, 8 + c, :], gs[:, c, :], ALU.add).then_inc(z_ready, 1)

                def z_low(c):
                    dve.wait_ge(z_hi_ready, l * 8 + (c + 1))
                    part = slice(S * c, S * (c + 1))
                    dve.tensor_tensor(z_lo[:, part], gs[:, 8 + c, :], z_hi[:, part].bitcast(F32),
                                      ALU.subtract).then_inc(z_lo_ready, 1)

                for i in range(4):
                    split(("lup", i + 1) if i < 3 else ("lout", 0), l)
                    if i:
                        z_low(2 * i - 2)
                        z_low(2 * i - 1)
                    gated_sum(2 * i)
                    gated_sum(2 * i + 1)
                z_low(6)
                z_low(7)
                split(("lout", 1), l)
                for i in range(2):
                    if i:
                        split(("upa", 1, 0), l)
                    for q in (2 * i, 2 * i + 1):
                        for k in range(max(1, 2 * q - 4), 2 * q - 2):
                            add_square(3 * l + 2, k, 5)
                        src = done(("out", q))
                        xs = x[:, 2 * q:2 * q + 2, :].rearrange("p c t -> p (c t)")
                        dve.tensor_tensor(xs, src, xs, ALU.add).then_inc(emptied["dve"], 1)
                for k in (4, 5):
                    add_square(3 * l + 2, k, 5)
                wait_emptied(("out", 3))

                ffn(1, 2, lo["norm_ffn2"], ("upa", 0, 0))
                assert step.n == step.per, step.n

            dve.wait_ge(l_std, 3 * LAYERS + 1)
            dve.reciprocal(rstd_col[:, 0:TT], std[:, 0:TT]).then_inc(l_rstd, 1)
            dve.wait_ge(l_spread, 3 * LAYERS + 1)
            at = fo["final_norm"]
            for k in range(KD):
                dve.scalar_tensor_tensor(out=h[:, k, :], in0=x[:, k, :], scalar=first_cols[:, at + k:at + k + 1],
                                         in1=bank[7][:, 0:S], op0=ALU.mult, op1=ALU.mult).then_inc(f_h, 1)
            for t in range(TT):
                dve.wait_ge(outT_done, 2 * t + 2)
                dve.tensor_copy(out_tok[:, t, 512:1024], bank[2 * t + 1]).then_inc(out_ready_dve, 1)


_INS = [(n, n) for n in ("x", "c", "w_ada", "b_ada", "g_pre_mix", "g_post_mix", "g_pre_ffn", "g_post_ffn", "w_in",
                         "ret_decay_fwd", "ret_decay_bwd", "w_out", "w_router", "w_gate_e", "w_up_e", "w_down_e")]
_INS += [(n, n if n in ("w_in_2", "w_out_2") else n[:-2]) for n in (
    "norm_ffn1_2", "ffn1_w_up_2", "ffn1_w_down_2", "norm_mix_2", "w_in_2", "pool_w_2", "pool_b_2", "pool_scale_2",
    "w_pool_up_2", "conv_w_2", "conv_b_2", "lru_w_a_2", "lru_b_a_2", "lru_w_x_2", "lru_b_x_2", "lru_lambda_2",
    "w_lru_up_2", "w_out_2", "norm_ffn2_2", "ffn2_w_up_2", "ffn2_w_down_2", "final_norm_2")]


def kernel(**inputs):
    import numpy as _np
    import concourse.bacc as _bacc
    from concourse import mybir as _mybir
    from concourse.bass_utils import run_bass_kernel_spmd as _run

    nc = _bacc.Bacc("TRN2", target_bir_lowering=False, num_devices=1)
    arrays, args = {}, {}
    for name, own in _INS:
        arr = _np.ascontiguousarray(inputs[name])
        arrays[f"in_{name}_dram"] = arr
        args[own] = nc.dram_tensor(f"in_{name}_dram", arr.shape, _mybir.dt.from_np(arr.dtype), kind="ExternalInput").ap()
    out = nc.dram_tensor("out_0_dram", (1, S, D), F32, kind="ExternalOutput").ap()
    block_kernel(nc, args, out)
    r = _run(nc, [arrays], core_ids=[0])
    return r.results[0]["out_0_dram"]
```
